# Optimizing a Trainium2 kernel written in Bass

```python
import math
import jax, jax.numpy as jnp
from jax import lax
import numpy as np

D_MODEL = 1024
BATCH = 1
SEQ = 256
DEPTH = 2

N_MIXERS = 2
N_A_LAYERS = (DEPTH + N_MIXERS - 1) // N_MIXERS
N_B_LAYERS = DEPTH // N_MIXERS

ATTN_HEAD_DIM = 128
ATTN_HEADS = D_MODEL // ATTN_HEAD_DIM
MOBA_BLOCK = 256
MOBA_TOPK = 3
Q_CHUNK = 128
ROPE_THETA = 10000.0

SSM_EXPAND = 2
SSM_D_INNER = SSM_EXPAND * D_MODEL
SSM_HEAD_DIM = 64
SSM_HEADS = SSM_D_INNER // SSM_HEAD_DIM
SSM_GROUPS = 8
SSM_HEADS_PER_GROUP = SSM_HEADS // SSM_GROUPS
SSM_STATE = 128
SSM_CONV = 4
SSM_CHUNK = 128
SSM_CONV_DIM = SSM_D_INNER + 2 * SSM_GROUPS * SSM_STATE
SSM_IN_DIM = SSM_D_INNER + SSM_CONV_DIM + SSM_HEADS

D_FF = 2816
EPS = 1e-6


def rms_norm(x, g):
    xf = x.astype(jnp.float32)
    y = xf * lax.rsqrt(jnp.mean(xf * xf, axis=-1, keepdims=True) + EPS)
    return (y * g.astype(jnp.float32)).astype(x.dtype)

def swiglu(x, w_gate, w_up, w_down):
    return (jax.nn.silu(x @ w_gate) * (x @ w_up)) @ w_down

def rope(x, positions):
    half = x.shape[-1] // 2
    inv_freq = ROPE_THETA ** (-jnp.arange(half, dtype=jnp.float32) / half)
    ang = positions.astype(jnp.float32)[..., None] * inv_freq
    cos = jnp.cos(ang)[:, :, None, :]
    sin = jnp.sin(ang)[:, :, None, :]
    xf = x.astype(jnp.float32)
    x1, x2 = xf[..., :half], xf[..., half:]
    out = jnp.concatenate([x1 * cos - x2 * sin, x2 * cos + x1 * sin], axis=-1)
    return out.astype(x.dtype)

def moba_mixer(h, positions, w_qkv, q_gain, k_gain, w_o):
    bsz, seq, _ = h.shape
    H, Dh, BS = ATTN_HEADS, ATTN_HEAD_DIM, MOBA_BLOCK
    qkv = (h @ w_qkv).reshape(bsz, seq, 3, H, Dh)
    q = rope(rms_norm(qkv[:, :, 0], q_gain), positions)
    k = rope(rms_norm(qkv[:, :, 1], k_gain), positions)
    v = qkv[:, :, 2]
    q = jnp.swapaxes(q, 1, 2)
    k = jnp.swapaxes(k, 1, 2)
    v = jnp.swapaxes(v, 1, 2)
    n_blk = -(-seq // BS)
    pad = n_blk * BS - seq
    k = jnp.pad(k, ((0, 0), (0, 0), (0, pad), (0, 0)))
    v = jnp.pad(v, ((0, 0), (0, 0), (0, pad), (0, 0)))
    kb = k.reshape(bsz, H, n_blk, BS, Dh)
    vb = v.reshape(bsz, H, n_blk, BS, Dh)
    n_sel = min(MOBA_TOPK, n_blk - 1)
    q_blk = jnp.arange(seq) // BS
    scale = Dh ** -0.5

    if n_sel > 0:
        k_mean = jnp.mean(kb.astype(jnp.float32), axis=3)
        gate = jnp.einsum('bhtd,bhnd->bhtn', q.astype(jnp.float32), k_mean)
        past = jnp.arange(n_blk)[None, :] < q_blk[:, None]
        gate = jnp.where(past, gate, -jnp.inf)
        _, sel_idx = lax.top_k(gate, n_sel)
        sel_valid = sel_idx < q_blk[:, None]

    n_qc = seq // Q_CHUNK
    head_ix = jnp.arange(H)[:, None, None]

    def one_chunk(s):
        b = s // n_qc
        t0 = (s % n_qc) * Q_CHUNK
        qc = lax.dynamic_slice_in_dim(lax.dynamic_index_in_dim(q, b, 0, False), t0, Q_CHUNK, 1)
        kb_b = lax.dynamic_index_in_dim(kb, b, 0, False)
        vb_b = lax.dynamic_index_in_dim(vb, b, 0, False)
        own = t0 // BS
        k_own = lax.dynamic_index_in_dim(kb_b, own, 1, False)
        v_own = lax.dynamic_index_in_dim(vb_b, own, 1, False)
        q_pos = t0 + jnp.arange(Q_CHUNK)
        k_pos = own * BS + jnp.arange(BS)
        s_own = jnp.einsum('hqd,hkd->hqk', qc, k_own).astype(jnp.float32) * scale
        s_own = jnp.where(k_pos[None, :] <= q_pos[:, None], s_own, -jnp.inf)
        if n_sel == 0:
            p = jax.nn.softmax(s_own, axis=-1).astype(v_own.dtype)
            return jnp.einsum('hqk,hkd->hqd', p, v_own)
        idx = lax.dynamic_slice_in_dim(lax.dynamic_index_in_dim(sel_idx, b, 0, False), t0, Q_CHUNK, 1)
        valid = lax.dynamic_slice_in_dim(lax.dynamic_index_in_dim(sel_valid, b, 0, False), t0, Q_CHUNK, 1)
        k_sel = kb_b[head_ix, idx]
        v_sel = vb_b[head_ix, idx]
        s_sel = jnp.einsum('hqd,hqjkd->hqjk', qc, k_sel).astype(jnp.float32) * scale
        s_sel = jnp.where(valid[..., None], s_sel, -jnp.inf).reshape(H, Q_CHUNK, n_sel * BS)
        p = jax.nn.softmax(jnp.concatenate([s_sel, s_own], axis=-1), axis=-1).astype(v_own.dtype)
        p_sel = p[..., :n_sel * BS].reshape(H, Q_CHUNK, n_sel, BS)
        p_own = p[..., n_sel * BS:]
        return (jnp.einsum('hqjk,hqjkd->hqd', p_sel, v_sel)
                + jnp.einsum('hqk,hkd->hqd', p_own, v_own))

    o = lax.map(one_chunk, jnp.arange(bsz * n_qc))
    o = o.reshape(bsz, n_qc, H, Q_CHUNK, Dh).transpose(0, 1, 3, 2, 4).reshape(bsz, seq, H * Dh)
    return o @ w_o

def ssd_chunked(xdt, a_dt, bm, cm):
    bsz, seq = xdt.shape[:2]
    G, R, P, N, CH = SSM_GROUPS, SSM_HEADS_PER_GROUP, SSM_HEAD_DIM, SSM_STATE, SSM_CHUNK
    nc = seq // CH
    x = xdt.reshape(bsz, nc, CH, G, R, P)
    a = a_dt.reshape(bsz, nc, CH, G, R).transpose(0, 3, 4, 1, 2)
    bc = bm.reshape(bsz, nc, CH, G, N)
    cc = cm.reshape(bsz, nc, CH, G, N)
    a_cs = jnp.cumsum(a, axis=-1)
    tril = jnp.tril(jnp.ones((CH, CH), dtype=bool))
    seg = a_cs[..., :, None] - a_cs[..., None, :]
    L = jnp.exp(jnp.where(tril, seg, -jnp.inf))
    cb = jnp.einsum('bclgn,bcsgn->bgcls', cc, bc)
    y_diag = jnp.einsum('bgrcls,bcsgrp->bclgrp', cb[:, :, None] * L, x)
    decay = jnp.exp(a_cs[..., -1:] - a_cs)
    states = jnp.einsum('bclgn,bgrcl,bclgrp->bcgrpn', bc, decay, x)
    chunk_decay = jnp.exp(a_cs[..., -1])

    def step(hs, inp):
        st, dec = inp
        return hs * dec[..., None, None] + st, hs

    h0 = jnp.zeros((bsz, G, R, P, N), dtype=jnp.float32)
    _, prev = lax.scan(step, h0, (jnp.moveaxis(states, 1, 0), jnp.moveaxis(chunk_decay, -1, 0)))
    prev = jnp.moveaxis(prev, 0, 1)
    y_off = jnp.einsum('bclgn,bcgrpn,bgrcl->bclgrp', cc, prev, jnp.exp(a_cs))
    return (y_diag + y_off).reshape(bsz, seq, G * R, P)

def mamba2_mixer(h, w_in, conv_w, conv_b, dt_bias, a_log, d_skip, norm_g, w_out):
    bsz, seq, _ = h.shape
    DI, G, N, H, P = SSM_D_INNER, SSM_GROUPS, SSM_STATE, SSM_HEADS, SSM_HEAD_DIM
    proj = h @ w_in
    z = proj[..., :DI]
    xbc = proj[..., DI:DI + SSM_CONV_DIM]
    dt = proj[..., DI + SSM_CONV_DIM:]
    xbc = lax.conv_general_dilated(xbc, conv_w[:, None, :], window_strides=(1,),
                                   padding=[(SSM_CONV - 1, 0)],
                                   dimension_numbers=('NWC', 'WIO', 'NWC'),
                                   feature_group_count=SSM_CONV_DIM)
    xbc = jax.nn.silu(xbc + conv_b)
    xs = xbc[..., :DI].reshape(bsz, seq, H, P).astype(jnp.float32)
    bm = xbc[..., DI:DI + G * N].reshape(bsz, seq, G, N).astype(jnp.float32)
    cm = xbc[..., DI + G * N:].reshape(bsz, seq, G, N).astype(jnp.float32)
    dt = jax.nn.softplus(dt.astype(jnp.float32) + dt_bias.astype(jnp.float32))
    a = -jnp.exp(a_log.astype(jnp.float32))
    y = ssd_chunked(xs * dt[..., None], dt * a, bm, cm)
    y = y + d_skip.astype(jnp.float32)[:, None] * xs
    y = y.reshape(bsz, seq, DI) * jax.nn.silu(z.astype(jnp.float32))
    yg = y.reshape(bsz, seq, G, DI // G)
    yg = yg * lax.rsqrt(jnp.mean(yg * yg, axis=-1, keepdims=True) + EPS)
    y = yg.reshape(bsz, seq, DI) * norm_g.astype(jnp.float32)
    return y.astype(h.dtype) @ w_out

def first_inputs(seed: int = 0) -> dict:
    key = jax.random.key(seed)
    ks = jax.random.split(key, 26)
    f32 = jnp.float32

    def nrm(k, shape, fan_in):
        return jax.random.normal(k, shape, f32) * (fan_in ** -0.5)

    def gain(k, shape):
        return 1.0 + 0.05 * jax.random.normal(k, shape, f32)

    dt_init = jnp.exp(jax.random.uniform(ks[20], (N_B_LAYERS, SSM_HEADS), f32)
                      * (math.log(0.1) - math.log(0.001)) + math.log(0.001))
    dt_init = jnp.maximum(dt_init, 1e-4)
    return {
        "x": jax.random.normal(ks[0], (BATCH, SEQ, D_MODEL), f32),
        "positions": jnp.broadcast_to(jnp.arange(SEQ, dtype=jnp.int32), (BATCH, SEQ)),
        "ffn1_norm": gain(ks[1], (DEPTH, D_MODEL)),
        "ffn1_w_gate": nrm(ks[2], (DEPTH, D_MODEL, D_FF), D_MODEL),
        "ffn1_w_up": nrm(ks[3], (DEPTH, D_MODEL, D_FF), D_MODEL),
        "ffn1_w_down": nrm(ks[4], (DEPTH, D_FF, D_MODEL), D_FF),
        "mix_norm": gain(ks[5], (DEPTH, D_MODEL)),
        "ffn2_norm": gain(ks[6], (DEPTH, D_MODEL)),
        "ffn2_w_gate": nrm(ks[7], (DEPTH, D_MODEL, D_FF), D_MODEL),
        "ffn2_w_up": nrm(ks[8], (DEPTH, D_MODEL, D_FF), D_MODEL),
        "ffn2_w_down": nrm(ks[9], (DEPTH, D_FF, D_MODEL), D_FF),
        "attn_w_qkv": nrm(ks[10], (N_A_LAYERS, D_MODEL, 3 * D_MODEL), D_MODEL),
        "attn_q_norm": gain(ks[11], (N_A_LAYERS, ATTN_HEAD_DIM)),
        "attn_k_norm": gain(ks[12], (N_A_LAYERS, ATTN_HEAD_DIM)),
        "attn_w_o": nrm(ks[13], (N_A_LAYERS, D_MODEL, D_MODEL), D_MODEL),
        "ssm_w_in": nrm(ks[14], (N_B_LAYERS, D_MODEL, SSM_IN_DIM), D_MODEL),
        "ssm_conv_w": nrm(ks[15], (N_B_LAYERS, SSM_CONV, SSM_CONV_DIM), SSM_CONV),
        "ssm_conv_b": 0.02 * jax.random.normal(ks[16], (N_B_LAYERS, SSM_CONV_DIM), f32),
        "ssm_dt_bias": dt_init + jnp.log(-jnp.expm1(-dt_init)),
        "ssm_a_log": jnp.log(jax.random.uniform(ks[17], (N_B_LAYERS, SSM_HEADS), f32, 1.0, 16.0)),
        "ssm_d": 1.0 + 0.1 * jax.random.normal(ks[18], (N_B_LAYERS, SSM_HEADS), f32),
        "ssm_norm": gain(ks[19], (N_B_LAYERS, SSM_D_INNER)),
        "ssm_w_out": nrm(ks[21], (N_B_LAYERS, SSM_D_INNER, D_MODEL), SSM_D_INNER),
    }

def first_block(x, positions, ffn1_norm, ffn1_w_gate, ffn1_w_up, ffn1_w_down, mix_norm,
              ffn2_norm, ffn2_w_gate, ffn2_w_up, ffn2_w_down,
              attn_w_qkv, attn_q_norm, attn_k_norm, attn_w_o,
              ssm_w_in, ssm_conv_w, ssm_conv_b, ssm_dt_bias, ssm_a_log, ssm_d, ssm_norm, ssm_w_out):
    for i in range(DEPTH):
        x = x + 0.5 * swiglu(rms_norm(x, ffn1_norm[i]), ffn1_w_gate[i], ffn1_w_up[i], ffn1_w_down[i])
        h = rms_norm(x, mix_norm[i])
        j = i // N_MIXERS
        if i % N_MIXERS == 0:
            x = x + moba_mixer(h, positions, attn_w_qkv[j], attn_q_norm[j], attn_k_norm[j], attn_w_o[j])
        else:
            x = x + mamba2_mixer(h, ssm_w_in[j], ssm_conv_w[j], ssm_conv_b[j], ssm_dt_bias[j],
                                 ssm_a_log[j], ssm_d[j], ssm_norm[j], ssm_w_out[j])
        x = x + 0.5 * swiglu(rms_norm(x, ffn2_norm[i]), ffn2_w_gate[i], ffn2_w_up[i], ffn2_w_down[i])
    return x


DEPTH_2 = 1

HG_HEADS = 8
HG_DK = 128
HG_DV = D_MODEL // HG_HEADS
HG_CHUNK = 64
RET_HEADS = 8
RET_DV = D_MODEL // RET_HEADS
RET_DK = RET_DV // 2
RET_CHUNK = 128
ROPE_BASE = 10000.0

HG_Q = HG_HEADS * HG_DK
HG_V = HG_HEADS * HG_DV
RET_Q = RET_HEADS * RET_DK
RET_V = RET_HEADS * RET_DV
SPLITS = [HG_Q, HG_Q, HG_V, HG_V, RET_Q, RET_Q, RET_V, RET_V, D_MODEL, D_MODEL]
D_IN = sum(SPLITS)


def rms_norm_2(x, g):
    xf = x.astype(jnp.float32)
    y = xf * lax.rsqrt(jnp.mean(xf * xf, axis=-1, keepdims=True) + EPS)
    return (y * g.astype(jnp.float32)).astype(x.dtype)

def head_rms_norm(o, g):
    H, d = o.shape[-2], o.shape[-1]
    y = o * lax.rsqrt(jnp.mean(o * o, axis=-1, keepdims=True) + EPS)
    y = y * g.astype(jnp.float32).reshape(H, d)
    return y.reshape(o.shape[0], o.shape[1], H * d)

def rotary(t, pos):
    dk = t.shape[-1]
    inv_freq = 1.0 / (ROPE_BASE ** jnp.linspace(0.0, 1.0, dk // 2, dtype=jnp.float32))
    ang = pos.astype(jnp.float32)[:, None] * inv_freq[None, :]
    cos = jnp.cos(ang)[None, :, None, :]
    sin = jnp.sin(ang)[None, :, None, :]
    t1, t2 = t[..., : dk // 2], t[..., dk // 2:]
    return jnp.concatenate([t1 * cos - t2 * sin, t1 * sin + t2 * cos], axis=-1)

def hgrn2_chunkwise(q, fpre, v, lb):
    B, L, H, dk = q.shape
    dv = v.shape[-1]
    C = HG_CHUNK
    N = L // C
    q = jax.nn.silu(q)
    lbh = lb.astype(jnp.float32).reshape(H, dk)
    f = lbh + (1.0 - lbh) * jax.nn.sigmoid(fpre)
    k = 1.0 - f
    logf = jnp.log(f)

    def to_chunks(t):
        return t.reshape(B, N, C, H, t.shape[-1]).transpose(1, 0, 3, 2, 4)

    mask = jnp.tril(jnp.ones((C, C), dtype=bool))[:, :, None]

    def step(S, inp):
        qc, kc, lfc, vc = inp
        b = jnp.cumsum(lfc, axis=2)
        inter = jnp.einsum('bhtd,bhde->bhte', qc * jnp.exp(b), S)
        diff = b[:, :, :, None, :] - b[:, :, None, :, :]
        decay = jnp.exp(jnp.where(mask, diff, -jnp.inf))
        A = jnp.einsum('bhtsd,bhsd->bhts', qc[:, :, :, None, :] * decay, kc)
        intra = jnp.einsum('bhts,bhse->bhte', A, vc)
        b_last = b[:, :, -1:, :]
        S_new = jnp.exp(b_last[:, :, 0, :])[..., None] * S + jnp.einsum(
            'bhsd,bhse->bhde', kc * jnp.exp(b_last - b), vc)
        return S_new, inter + intra

    S0 = jnp.zeros((B, H, dk, dv), jnp.float32)
    _, o = lax.scan(step, S0, (to_chunks(q), to_chunks(k), to_chunks(logf), to_chunks(v)))
    return o.transpose(1, 0, 3, 2, 4).reshape(B, L, H, dv)

def retention_chunkwise(q, k, v):
    B, L, H, dk = q.shape
    dv = v.shape[-1]
    C = RET_CHUNK
    N = L // C
    log_gamma = jnp.log(1.0 - jnp.exp2(-5.0 - jnp.arange(H, dtype=jnp.float32)))
    k = k * (dk ** -0.5)
    qc = q.reshape(B, N, C, H, dk).transpose(0, 3, 1, 2, 4)
    kc = k.reshape(B, N, C, H, dk).transpose(0, 3, 1, 2, 4)
    vc = v.reshape(B, N, C, H, dv).transpose(0, 3, 1, 2, 4)
    idx = jnp.arange(C, dtype=jnp.float32)
    rel = idx[:, None] - idx[None, :]
    Dm = jnp.where(rel >= 0, jnp.exp(log_gamma[:, None, None] * jnp.maximum(rel, 0.0)), 0.0)
    scores = jnp.einsum('bhnid,bhnjd->bhnij', qc, kc) * Dm[:, None]
    intra = jnp.einsum('bhnij,bhnje->bhnie', scores, vc)
    zeta = jnp.exp(log_gamma[:, None] * (C - 1.0 - idx))
    chunk_state = jnp.einsum('bhnjd,bhnje->bhnde', kc * zeta[:, None, :, None], vc)
    chunk_decay = jnp.exp(log_gamma * C)[None, :, None, None]

    def step(R, s):
        return chunk_decay * R + s, R

    R0 = jnp.zeros((B, H, dk, dv), jnp.float32)
    _, R_prev = lax.scan(step, R0, chunk_state.transpose(2, 0, 1, 3, 4))
    R_prev = R_prev.transpose(1, 2, 0, 3, 4)
    xi = jnp.exp(log_gamma[:, None] * (idx + 1.0))
    cross = jnp.einsum('bhnid,bhnde->bhnie', qc * xi[:, None, :, None], R_prev)
    return (intra + cross).transpose(0, 2, 3, 1, 4).reshape(B, L, H, dv)

def second_inputs(seed: int = 0) -> dict:
    key = jax.random.key(seed)
    ks = jax.random.split(key, 12)
    f32 = jnp.float32
    x = jax.random.normal(ks[0], (BATCH, SEQ, D_MODEL), f32)
    c = jax.random.normal(ks[1], (BATCH, D_MODEL), f32)
    norm_g = 1.0 + 0.05 * jax.random.normal(ks[2], (DEPTH_2, D_MODEL), f32)
    w_ada = 0.5 * D_MODEL ** -0.5 * jax.random.normal(ks[3], (DEPTH_2, D_MODEL, 3 * D_MODEL), f32)
    b_ada = 0.02 * jax.random.normal(ks[4], (DEPTH_2, 3 * D_MODEL), f32)
    w_in = D_MODEL ** -0.5 * jax.random.normal(ks[5], (DEPTH_2, D_MODEL, D_IN), f32)
    hg_lb_logits = 0.5 * jax.random.normal(ks[6], (DEPTH_2 + 1, HG_Q), f32)
    hg_norm_g = 1.0 + 0.05 * jax.random.normal(ks[7], (DEPTH_2, HG_V), f32)
    ret_norm_g = 1.0 + 0.05 * jax.random.normal(ks[8], (DEPTH_2, RET_V), f32)
    w_out = D_MODEL ** -0.5 * jax.random.normal(ks[9], (DEPTH_2, D_MODEL, D_MODEL), f32)
    final_g = 1.0 + 0.05 * jax.random.normal(ks[10], (D_MODEL,), f32)
    return {"x": x, "c": c, "norm_g": norm_g, "w_ada": w_ada, "b_ada": b_ada,
            "w_in": w_in, "hg_lb_logits": hg_lb_logits, "hg_norm_g": hg_norm_g,
            "ret_norm_g": ret_norm_g, "w_out": w_out, "final_g": final_g}

def second_block(x, c, norm_g, w_ada, b_ada, w_in, hg_lb_logits, hg_norm_g, ret_norm_g, w_out, final_g):
    B, L, D = x.shape
    pos = jnp.arange(L, dtype=jnp.int32)
    lower_bounds = jnp.cumsum(jax.nn.softmax(hg_lb_logits.astype(jnp.float32), axis=0), axis=0)
    offsets = np.cumsum([0] + SPLITS)[1:-1].tolist()
    for layer in range(DEPTH_2):
        mod = jax.nn.silu(c) @ w_ada[layer] + b_ada[layer]
        shift, scale, gate = jnp.split(mod[:, None, :], 3, axis=-1)
        h = rms_norm_2(x, norm_g[layer]) * (1.0 + scale) + shift
        proj = h @ w_in[layer]
        (hq, hf, hi, hz, rq, rk, rv, rz, ga, gb) = jnp.split(proj, offsets, axis=-1)
        f32 = jnp.float32
        oA = hgrn2_chunkwise(hq.astype(f32).reshape(B, L, HG_HEADS, HG_DK),
                             hf.astype(f32).reshape(B, L, HG_HEADS, HG_DK),
                             hi.astype(f32).reshape(B, L, HG_HEADS, HG_DV),
                             lower_bounds[layer])
        uA = head_rms_norm(oA, hg_norm_g[layer]) * jax.nn.silu(hz.astype(f32))
        qB = rotary(rq.astype(f32).reshape(B, L, RET_HEADS, RET_DK), pos)
        kB = rotary(rk.astype(f32).reshape(B, L, RET_HEADS, RET_DK), pos)
        oB = retention_chunkwise(qB, kB, rv.astype(f32).reshape(B, L, RET_HEADS, RET_DV))
        uB = head_rms_norm(oB, ret_norm_g[layer]) * jax.nn.silu(rz.astype(f32))
        m = (jax.nn.sigmoid(ga.astype(f32)) * uA + jax.nn.sigmoid(gb.astype(f32)) * uB).astype(x.dtype)
        x = x + gate * (m @ w_out[layer])
    return rms_norm_2(x, final_g)


def setup_inputs(seed=0):
    out = dict(first_inputs(seed))
    for name, value in second_inputs(seed + 1).items():
        if name != "x":
            out[name + "_2"] = value
    return out


def reference(
    x, positions, ffn1_norm, ffn1_w_gate, ffn1_w_up, ffn1_w_down, mix_norm, ffn2_norm,
    ffn2_w_gate, ffn2_w_up, ffn2_w_down, attn_w_qkv, attn_q_norm, attn_k_norm, attn_w_o,
    ssm_w_in, ssm_conv_w, ssm_conv_b, ssm_dt_bias, ssm_a_log, ssm_d, ssm_norm, ssm_w_out, c_2,
    norm_g_2, w_ada_2, b_ada_2, w_in_2, hg_lb_logits_2, hg_norm_g_2, ret_norm_g_2, w_out_2,
    final_g_2,
):
    x = first_block(
        x, positions, ffn1_norm, ffn1_w_gate, ffn1_w_up, ffn1_w_down, mix_norm, ffn2_norm,
        ffn2_w_gate, ffn2_w_up, ffn2_w_down, attn_w_qkv, attn_q_norm, attn_k_norm, attn_w_o,
        ssm_w_in, ssm_conv_w, ssm_conv_b, ssm_dt_bias, ssm_a_log, ssm_d, ssm_norm, ssm_w_out,
    )
    return second_block(
        x, c_2, norm_g_2, w_ada_2, b_ada_2, w_in_2, hg_lb_logits_2, hg_norm_g_2, ret_norm_g_2,
        w_out_2, final_g_2,
    )


_drawn_inputs = setup_inputs


def setup_inputs(seed=0):
    import zlib

    import numpy as np

    out = dict(_drawn_inputs(seed))
    spreads = {}
    factors = {'attn_q_norm': 4.641,
     'attn_k_norm': 5.414,
     'ssm_conv_b': 3.041,
     'norm_g_2': 6.492,
     'b_ada_2': 6.115,
     'hg_lb_logits_2': 8.0,
     'hg_norm_g_2': 8.0,
     'ret_norm_g_2': 8.0}
    for name, (base, spread) in spreads.items():
        noise = np.random.default_rng([zlib.crc32(name.encode()), seed]).standard_normal(out[name].shape)
        drawn = base * np.exp(spread * noise) if base else spread * noise
        out[name] = __import__('jax').numpy.asarray(drawn.astype(out[name].dtype))
    for name, factor in factors.items():
        out[name] = (out[name] * factor).astype(out[name].dtype)
    return out
```

```python
from contextlib import ExitStack

import numpy as np

import concourse.bass as bass
from concourse import mybir

F32 = mybir.dt.float32
R32 = mybir.dt.float32r
I32 = mybir.dt.int32
U32 = mybir.dt.uint32
ALU = mybir.AluOpType
ACT = mybir.ActivationFunctionType
X_AXIS = mybir.AxisListType.X

P = 128
SEQ = 256
TT = SEQ // P
D = 1024
KD = D // P
FF = 2816
FC = 256
NFC = FF // FC
EPS = 1e-6

HEADS = 8
HD = 128
SCALE = HD ** -0.5
HALF = HD // 2
MASKED = -1e30

DI = 2048
GROUPS = 8
SH = 32
HPG = SH // GROUPS
SP = DI // SH
NB = GROUPS * 128
CONVD = DI + 2 * NB
TAPS = 4
GW = DI // GROUPS
KI = DI // P

HG_C = 64
LEVELS = 6
RH = 8
RDK = 64
RHALF = RDK // 2

SLOTS = 3
UNIT = 4 * 512
PARTS = 2

TWO_PI_HI = 6.28125
TWO_PI_MID = float(np.round((2 * np.pi - TWO_PI_HI) * 2 ** 20) / 2 ** 20)
TWO_PI_LO = float(2 * np.pi - TWO_PI_HI - TWO_PI_MID)
ROUND = 1.5 * 2.0 ** 23


def first_constants():
    i = np.arange(P)
    ident = np.eye(P)
    causal = np.where(i[None, :] <= i[:, None], 0.0, MASKED)
    runsum = (i[:, None] <= i[None, :]) * 1.0
    freq = np.broadcast_to(10000.0 ** (-np.arange(HALF) / HALF), (P, HALF))
    blocked = np.full((P, P), MASKED)
    return np.concatenate([ident, causal, blocked, 0.0 * ident, causal, causal.T, runsum, np.ones((P, P)), freq],
                          1).astype(np.float32)


FIRST = {"ident": (0, P), "causal": (P, 4 * P), "causal_t": (5 * P, P), "runsum": (6 * P, P), "ones": (7 * P, P),
         "freq": (8 * P, HALF)}
FIRST_W = 8 * P + HALF


def second_constants():
    i = np.arange(P)
    s, t = i[:, None], i[None, :]
    masks = [s == t]
    for level in range(1, LEVELS + 1):
        b, h = 2 ** level, 2 ** (level - 1)
        masks.append((s // b == t // b) & (s % b < h) & (t % b >= h))
    masks = np.concatenate([m * 1.0 for m in masks], 1)
    gamma = np.log(1.0 - 2.0 ** (-5.0 - np.arange(RH)))
    rel = t - s
    decay = np.concatenate([np.where(rel >= 0, np.exp(g * np.maximum(rel, 0)), 0.0) * RDK ** -0.5 for g in gamma], 1)
    xi = np.concatenate([np.exp(gamma[2 * j + (i[:, None] >= RDK)] * (t + 1.0)) for j in range(RH // 2)], 1)
    zeta = np.exp(gamma[None, :] * (P - 1.0 - i[:, None])) * RDK ** -0.5
    inv = 1.0 / (10000.0 ** np.linspace(0.0, 1.0, RHALF))
    ang = np.arange(SEQ)[:, None] * inv.astype(np.float32).astype(np.float64)[None, :]
    cos = np.cos(ang).reshape(TT, P, RHALF).transpose(1, 0, 2).reshape(P, TT * RHALF)
    sin = np.sin(ang).reshape(TT, P, RHALF).transpose(1, 0, 2).reshape(P, TT * RHALF)
    keep = np.broadcast_to((np.arange(SEQ) % HG_C != 0) * 1.0, (P, SEQ))
    return np.concatenate([masks, decay, xi, zeta, cos, sin, keep], 1).astype(np.float32)


SECOND, _at = {}, 0
for _name, _w in (("levels", (LEVELS + 1) * P), ("decay", RH * P), ("xi", RH // 2 * P), ("zeta", RH),
                  ("cos", TT * RHALF), ("sin", TT * RHALF), ("keep", SEQ)):
    SECOND[_name] = (_at, _w)
    _at += _w
SECOND_W = _at

ROWS, _at = {}, 0
for _name, _n in (("ffn1_norm", 16), ("mix_norm", 16), ("ffn2_norm", 16), ("norm_g_2", 8), ("ssm_norm", 16),
                  ("ssm_conv_b", 32), ("c_2", 8), ("hg_lb_logits_2", 16)):
    ROWS[_name] = (_at, _n)
    _at += _n
assert _at == P


STAGES = [("ffn1_0", 3 * NFC), ("qkv", 12), ("wo", 4), ("ffn2_0", 3 * NFC), ("ffn1_1", 3 * NFC), ("ssm_xbc", 16),
          ("ssm_dt", 1), ("ssm_z", 8), ("ssm_out", 8), ("ffn2_1", 3 * NFC), ("in2", 36), ("out2", 4)]
FFNS = ("ffn1_0", "ffn2_0", "ffn1_1", "ffn2_1")
FIRST_UNIT, UNITS = {}, 0
for _name, _n in STAGES:
    FIRST_UNIT[_name] = UNITS
    UNITS += _n


def place(unit, step=0, per=0):
    return unit + per * step, unit % SLOTS, unit // SLOTS + per // SLOTS * step


def build(nc, w, out):
    with ExitStack() as ctx:
        sems = {}

        def sem(name):
            if name not in sems:
                sems[name] = ctx.enter_context(nc.semaphore(name))
            return sems[name]

        counts = {}

        def in_order(engine, name):
            def order(*instructions):
                for i in instructions:
                    i.then_inc(sem(name), 1)
                counts[name] = counts.get(name, 0) + len(instructions)
                engine.wait_ge(sem(name), counts[name])
            return order

        top = [-(-nc.sbuf_base // 64) * 64]

        def at(offset, name, shape, dt=F32):
            t = nc.alloc_sbuf_tensor_at(name, shape, dt, offset=offset)
            size = int(np.prod(shape[1:])) * 4
            assert offset + size <= nc.sbuf_usable_end, (name, offset + size - nc.sbuf_usable_end)
            return t, offset + -(-size // 64) * 64

        def keep(name, shape, dt=F32):
            t, top[0] = at(top[0], name, shape, dt)
            return t

        def region(start):
            end = [start]

            def take(name, shape, dt=F32):
                t, end[0] = at(end[0], name, shape, dt)
                return t

            return take, end

        x = keep("x", [P, TT, D])
        hT_hi = keep("hT_hi", [P, KD, SEQ], R32)
        hT_lo = keep("hT_lo", [P, KD, SEQ], R32)
        raw = keep("raw", [P, SLOTS, UNIT])
        w_hi = keep("w_hi", [P, SLOTS, UNIT], R32)
        w_lo = keep("w_lo", [P, SLOTS, UNIT], R32)
        ffn_tiles = top[0]
        silu_g = keep("silu_g", [P, TT, FC])
        hid = keep("hid", [P, TT, FC])
        last_hidT_hi, _ = at(ffn_tiles, "last_hidT_hi", [P, 2, SEQ], R32)
        last_hidT_lo, _ = at(ffn_tiles + 4 * TT * FC, "last_hidT_lo", [P, 2, SEQ], R32)
        hidT_hi = keep("hidT_hi", [P, 2, SEQ], R32)
        hidT_lo = keep("hidT_lo", [P, 2, SEQ], R32)
        const1 = keep("const1", [P, FIRST_W])
        cols = keep("cols", [P, P])
        taps = keep("taps", [P, P])
        sumsq = keep("sumsq", [P, 2, TT])
        meansq = keep("meansq", [P, TT])
        rstd = keep("rstd", [P, TT])
        neg_half = keep("neg_half", [P, 2 * SH])
        gate2 = keep("gate2", [P, D])
        mod_cols = keep("mod_cols", [P, 16])
        gain2 = keep("gain2", [P, KD])
        silu_c = keep("silu_c", [P, KD])
        WORK = top[0]

        psum = ctx.enter_context(nc.psum_tensor("psum", [P, 8, 512], F32))

        def c1(name):
            a, n = FIRST[name]
            return const1[:, a:a + n]

        ident, ones = c1("ident"), c1("ones")

        def col(name, n, count=1):
            a = ROWS[name][0] + n
            return cols[:, a:a + count]

        start, start_end = region(WORK + 8192)
        rows_in = start("rows_in", [P, P])
        taps_in = start("taps_in", [P, P])
        pos_i = start("pos_i", [P, TT], I32)
        pos_f = start("pos_f", [P, TT])
        angle = start("angle", [P, 2, TT, HALF])
        turns = start("turns", [P, 2, TT, HALF])
        trig = start("trig", [P, 2, TT, HALF])
        ada_in = start("ada_in", [P, 2, 3 * D])
        ada_term = start("ada_term", [P, 3 * D])
        ada = start("ada", [P, 3 * D])
        b_ada = start("b_ada", [1, 3 * D])

        norm, norm_end = region(WORK)
        xn = norm("xn", [P, TT, D])

        r, r_end = region(WORK + 8192)
        late_start = (nc.sbuf_usable_end - 6 * 1024) // 64 * 64
        rope_c = {}
        late, late_end = region(late_start)
        for name in ("q", "k"):
            for part in ("cos1", "sin2", "cos2", "sin1"):
                rope_c[name, part] = late(f"{name}_{part}", [P, TT, HALF])
        gains = late("qk_gains", [P, 2, HD])
        qk = r("qk", [P, TT, 2 * D])
        v_sb = r("v_sb", [P, TT, D])
        qk_sq = r("qk_sq", [P, TT, 512])
        qk_ss = r("qk_ss", [P, TT, 2 * HEADS])
        qk_ms = r("qk_ms", [P, TT, 2 * HEADS])
        qk_rstd = r("qk_rstd", [P, TT, 2 * HEADS])
        rope_a = r("rope_a", [P, TT, 4, HALF])
        rope_b = r("rope_b", [P, TT, 4, HALF])
        rope_d = r("rope_d", [P, TT, 4, HALF])
        rope_e = r("rope_e", [P, TT, 4, HALF])
        qkT = r("qkT", [P, 2, 2, SEQ])
        prob = r("prob", [P, 2, TT, SEQ])
        probT = r("probT", [P, 2, 3 * P])
        top_s = r("top_s", [P, HEADS, TT])
        bias_s = r("bias_s", [P, HEADS, TT])
        sum_s = r("sum_s", [P, HEADS, TT])
        inv_s = r("inv_s", [P, HEADS, TT])
        assert max(r_end[0], start_end[0]) <= late_start

        r, r_end = region(WORK)
        conv = r("conv", [P, 2, 4, SEQ])
        r, r_end = region(WORK)
        decay = r("decay", [P, 2, HPG, P])
        within = r("within", [P, 2, HPG, P])
        z = r("z", [P, TT, DI])
        y = r("y", [P, TT, DI])
        r2, r2_end = region(r_end[0])
        xs = r("xs", [P, TT, DI])
        bcT = r("bcT", [P, 2 * GROUPS, SEQ])
        b_rows = r("b_rows", [P, GROUPS, P])
        yT_hi = r2("yT_hi", [P, KI, SEQ], R32)
        yT_lo = r2("yT_lo", [P, KI, SEQ], R32)
        r2, r2_end = region(r_end[0])
        xT = r("xT", [P, 2, 4, SEQ])
        xdt = r2("xdt", [P, 2, HPG, SP])
        x_decayed = r2("x_decayed", [P, HPG, SP])
        x_skip = r2("x_skip", [P, 2, HPG, SP])
        states = r2("states", [P, 2, GW])
        per_head = {n: r(n, [P, SH]) for n in ("dt_bias", "a_rate", "d_skip", "end_decay", "start_decay")}
        per_token = {n: r(n, [P, TT, SH]) for n in ("dt_raw", "dt_exp", "dt_a", "dt_b", "dt_s", "dt_p", "dt", "a_dt",
                                                    "a_sum")}
        y_ss = r("y_ss", [P, TT, GROUPS])
        y_ms = r("y_ms", [P, TT, GROUPS])
        y_rstd = r("y_rstd", [P, TT, GROUPS])
        assert r2_end[0] <= r_end[0]

        second = {}
        r, r_end = region(WORK)
        for zone in ("exp", "pair", "query", "key", "sum", "value", "ret_qk", "ret_v", "out_gate"):
            second[zone] = r_end[0]
            r_end[0] += 8192
        second["att"] = ffn_tiles

        def zoned(zone, name, shape, dt=F32, offset=0):
            return at(second[zone] + offset, name, shape, dt)[0]

        h_tmp = zoned("pair", "h_tmp", [P, KD, SEQ])
        hg_exp = zoned("exp", "hg_exp", [P, HEADS, SEQ])
        hg_pair = zoned("pair", "hg_pair", [P, HEADS, SEQ])
        hg_q = zoned("query", "hg_q", [P, HEADS, SEQ])
        hg_k = zoned("key", "hg_k", [P, HEADS, SEQ])
        hg_b = zoned("sum", "hg_b", [P, HEADS, SEQ])
        hg_v = zoned("value", "hg_v", [P, TT, D])
        hg_att = zoned("att", "hg_att", [P, HEADS * TT, P])
        hg_k_rows = zoned("pair", "hg_k_rows", [P, HEADS * TT, P])
        hg_s = [zoned("sum", "hg_s1", [P, HEADS, P]), zoned("sum", "hg_s2", [P, HEADS, P], offset=4096),
                zoned("exp", "hg_s3", [P, HEADS, P])]
        out_a = zoned("key", "out_a", [P, TT, D])
        square_a = zoned("exp", "square_a", [P, TT, D])
        ret_qk = zoned("ret_qk", "ret_qk", [P, TT, 2, D // 2])
        ret_v = zoned("ret_v", "ret_v", [P, TT, D])
        ret_T = zoned("pair", "ret_T", [P, RH // 2, 2, SEQ])
        ret_q_cross = zoned("att", "ret_q_cross", [P, RH // 2, P])
        ret_k_end = zoned("att", "ret_k_end", [P, RH, RDK], offset=2048)
        ret_state = zoned("att", "ret_state", [P, RH // 2, P], offset=4096)
        ret_att = zoned("sum", "ret_att", [P, RH * TT, P])
        out_b = zoned("exp", "out_b", [P, TT, D])
        square_b = zoned("sum", "square_b", [P, TT, D])
        gate_a = zoned("out_gate", "gate_a", [P, TT, D])
        gate_b = zoned("query", "gate_b", [P, TT, D])
        mT_hi = zoned("pair", "mT_hi", [P, KD, SEQ], R32)
        mT_lo = zoned("value", "mT_lo", [P, KD, SEQ], R32)
        scaled = zoned("key", "scaled", [P, TT, D])
        const2_at = r_end[0]
        const2 = r("const2", [P, SECOND_W])
        rot = at(const2_at, "rot", [P, 3, RH, RHALF])[0]
        gain_row = r("gain_row", [P, D])
        sig = r("sig", [P, TT, 512])
        lb = r("lb", [P, HEADS])
        lb_rest = r("lb_rest", [P, HEADS])
        lb_top = r("lb_top", [P, HEADS])
        lb_e = r("lb_e", [P, 2, HEADS])
        hg_last = r("hg_last", [P, HEADS, SEQ // HG_C])
        head_ss = r("head_ss", [P, 2, TT * HEADS])
        head_ms = r("head_ms", [P, 2, TT * HEADS])
        head_rstd = r("head_rstd", [P, 2, TT * HEADS])

        def c2(name):
            a, n = SECOND[name]
            return const2[:, a:a + n]

        def halves_of(name, k0, n0, width=512):
            src = w[name][0].rearrange("(k p) n -> p k n", p=P)
            return [(k, src[:, k0 + k:k0 + k + 2, n0:n0 + width]) for k in (0, 2)]

        def load_unit(sp, unit, halves, step=0, per=0):
            n, slot, turn = place(unit, step, per)
            if unit >= SLOTS:
                sp.wait_ge(sem("lo_ready"), n - (SLOTS - 1))
            for dst, src in halves:
                sp.dma_start(dst, src).then_inc(sem(f"landed_{slot}"), 16)

        def split_hi(act, unit, step=0, per=0):
            if unit >= UNITS:
                return
            n, slot, turn = place(unit, step, per)
            act.wait_ge(sem(f"landed_{slot}"), 16 * PARTS * (turn + 1))
            if unit >= SLOTS:
                act.wait_ge(sem("unit_used"), n - (SLOTS - 1))
            act.activation(w_hi[:, slot, :], raw[:, slot, :], ACT.Copy).then_inc(sem("hi_ready"), 1)

        def split_lo(dve, unit, step=0, per=0):
            if unit >= UNITS:
                return
            n, slot, _ = place(unit, step, per)
            dve.wait_ge(sem("hi_ready"), n + 1)
            dve.tensor_tensor(w_lo[:, slot, :], raw[:, slot, :], w_hi[:, slot, :].bitcast(F32), ALU.subtract)\
               .then_inc(sem("lo_ready"), 1)

        def raw_unit(slot):
            return raw[:, slot, :].rearrange("p (k n) -> p k n", k=4)

        def load_linear(sp, stage, name, n0, k0s, chunks):
            u = FIRST_UNIT[stage]
            for c in range(chunks):
                for k0 in k0s:
                    slot = u % SLOTS
                    load_unit(sp, u, [(raw_unit(slot)[:, k:k + 2, :], src)
                                      for k, src in halves_of(name, k0, n0 + 512 * c)])
                    u += 1

        def use_unit(pe, unit, step=0, per=0):
            n, slot, _ = place(unit, step, per)
            pe.wait_ge(sem("lo_ready"), n + 1)
            return (w_hi[:, slot, :].rearrange("p (k n) -> p k n", k=4),
                    w_lo[:, slot, :].rearrange("p (k n) -> p k n", k=4))

        def linear_chunk(pe, unit, k0s, a_hi, a_lo, banks, ready=None):
            last_k = k0s[-1] + 3
            for j, k0 in enumerate(k0s):
                hi, lo = use_unit(pe, unit + j)
                for kk in range(4):
                    k = k0 + kk
                    if ready:
                        pe.wait_ge(sem(ready[0]), ready[1] + k + 1)
                    for t in range(TT):
                        to = psum[:, banks[t], :]
                        a, b = a_hi[:, k, t * P:(t + 1) * P], a_lo[:, k, t * P:(t + 1) * P]
                        pe.matmul(to, a, hi[:, kk, :], start=k == 0, stop=False)
                        pe.matmul(to, a, lo[:, kk, :], start=False, stop=False)
                        m = pe.matmul(to, b, hi[:, kk, :], start=False, stop=k == last_k)
                m.then_inc(sem("unit_used"), 1)

        def turned_chunk(pe, unit, banks, ready=None):
            for j in range(2):
                hi, lo = use_unit(pe, unit + j)
                for kk in range(4):
                    k = 4 * j + kk
                    if ready:
                        pe.wait_ge(sem(ready[0]), ready[1] + k + 1)
                    for c in range(4):
                        to = psum[:, banks[c // 2], (c % 2) * SEQ:(c % 2 + 1) * SEQ]
                        a, b = hi[:, kk, c * P:(c + 1) * P], lo[:, kk, c * P:(c + 1) * P]
                        pe.matmul(to, a, hT_hi[:, k, :], start=k == 0 and c % 2 == 0, stop=False, skip_group_check=True)
                        pe.matmul(to, a, hT_lo[:, k, :], start=False, stop=False, skip_group_check=True)
                        m = pe.matmul(to, b, hT_hi[:, k, :], start=False, stop=k == KD - 1, skip_group_check=True)
                m.then_inc(sem("unit_used"), 1)

        XT_BANKS = (2, 3, 4, 6)

        def turned_x(k):
            return psum[:, XT_BANKS[k // 2], (k % 2) * SEQ:(k % 2 + 1) * SEQ]

        def squares(act, n):
            for h in range(2):
                for t in range(TT):
                    if n:
                        act.wait_ge(sem("x_added"), 4 * (n - 1) + 2 * h + t + 1)
                    else:
                        act.wait_ge(sem("x_in"), 16 * TT)
                    cs = slice(512 * h, 512 * (h + 1))
                    act.activation(xn[:, t, cs], x[:, t, cs], ACT.Square, accum_out=sumsq[:, h, t:t + 1])\
                       .then_inc(sem("sumsq"), 1)

        def norm_act(act, n, gain, deferred, late_unit=UNITS):
            if not deferred:
                squares(act, n)
            if gain:
                for k in range(KD):
                    act.wait_ge(sem("xT"), KD * n + (k | 1) + 1)
                    act.activation(hT_hi[:, k, :], turned_x(k), ACT.Copy, scale=col(gain[0], gain[1] + k))\
                       .then_inc(sem("hT_hi"), 1)
            if deferred:
                squares(act, n)
            split_hi(act, late_unit)

        def norm_pool(pool, n):
            order = in_order(pool, "gpsimd_order")
            pool.wait_ge(sem("sumsq"), 4 * (n + 1))
            order(pool.tensor_tensor(meansq[:, :], sumsq[:, 0, :], sumsq[:, 1, :], ALU.add))
            order(pool.tensor_scalar(meansq[:, :], meansq[:, :], 1.0 / D, EPS, ALU.mult, ALU.add))
            pool.tensor_tensor(rstd[:, :], meansq[:, :], neg_half[:, 0:TT], ALU.pow).then_inc(sem("rstd"), 1)

        def norm_dve(dve, n, gain, deferred, late_unit=UNITS):
            if not deferred:
                dve.wait_ge(sem("rstd"), n + 1)
                for t in range(TT):
                    dve.tensor_scalar(xn[:, t, :], x[:, t, :], rstd[:, t:t + 1], None, ALU.mult).then_inc(sem("xn"), 1)
            if gain:
                for k in range(KD):
                    dve.wait_ge(sem("hT_hi"), KD * n + (k | 1) + 1)
                    dve.scalar_tensor_tensor(hT_lo[:, k, :], turned_x(k), col(gain[0], gain[1] + k),
                                             hT_hi[:, k, :].bitcast(F32), ALU.mult, ALU.subtract)\
                       .then_inc(sem("hT"), 1)
            split_lo(dve, late_unit)

        def norm_pe(pe, n, deferred, xn_before=0):
            for k in range(KD):
                for t in range(TT):
                    if k % 4 == 0:
                        if not deferred:
                            pe.wait_ge(sem("xn"), xn_before + TT)
                        elif n:
                            pe.wait_ge(sem("x_added"), 4 * (n - 1) + 2 * (k // 4) + t + 1)
                        else:
                            pe.wait_ge(sem("x_in"), 16 * TT)
                    m = pe.transpose(psum[:, XT_BANKS[k // 2], (k % 2) * SEQ + t * P:(k % 2) * SEQ + (t + 1) * P],
                                     (x if deferred else xn)[:, t, k * P:(k + 1) * P], ident)
                m.then_inc(sem("xT"), 1)

        def ffn_sp(sp, f, names, layer):
            u0 = FIRST_UNIT[f]
            gate, up, down = (w[n][layer] for n in names)
            gate = gate.rearrange("(k p) n -> p k n", p=P)
            up = up.rearrange("(k p) n -> p k n", p=P)
            down = down.rearrange("(c k p) n -> p c k n", k=2, p=P)

            def gate_up(u, c, step=0, per=0):
                for h in range(2):
                    dst = raw[:, (u + h) % SLOTS, :].rearrange("p (k g n) -> p k g n", k=4, g=2)
                    cs = bass.ds(c * FC, FC)
                    load_unit(sp, u + h, [(dst[:, :, 0, :], gate[:, 4 * h:4 * h + 4, cs]),
                                          (dst[:, :, 1, :], up[:, 4 * h:4 * h + 4, cs])], step, per)

            def down_rows(u, c, step=0, per=0):
                dst = raw[:, u % SLOTS, :].rearrange("p (k n) -> p k n", k=2)
                rows = down[:, bass.ds(c, 1), :, :].rearrange("p c k n -> p (c k) n")
                load_unit(sp, u, [(dst[:, k:k + 1, :], rows[:, k:k + 1, :]) for k in range(2)], step, per)

            gate_up(u0, 0)
            gate_up(u0 + 2, 1)
            down_rows(u0 + 4, 0)
            with sp.Fori(2, NFC) as c:
                gate_up(u0 + 5, c, c - 2, 3)
                down_rows(u0 + 7, c - 1, c - 2, 3)
            down_rows(u0 + 3 * NFC - 1, NFC - 1)

        def ffn_pe(pe, f, n, before_last=None):
            u0 = FIRST_UNIT[f]

            def gate_up(u, c, step=0, per=0, first=False):
                for h in range(2):
                    hi, lo = use_unit(pe, u + h, step, per)
                    if h == 0 and not first:
                        pe.wait_ge(sem("ffn_hid"), TT * (NFC * FFNS.index(f) + c))
                    for kk in range(4):
                        k = 4 * h + kk
                        if first:
                            pe.wait_ge(sem("hT"), KD * n + k + 1)
                        for t in range(TT):
                            to = psum[:, t, :]
                            a, b = hT_hi[:, k, t * P:(t + 1) * P], hT_lo[:, k, t * P:(t + 1) * P]
                            pe.matmul(to, a, hi[:, kk, :], start=k == 0, stop=False)
                            pe.matmul(to, a, lo[:, kk, :], start=False, stop=False)
                            m = pe.matmul(to, b, hi[:, kk, :], start=False, stop=k == KD - 1)
                    m.then_inc(sem("unit_used"), 1)

            def down(u, c, step=0, per=0, first=False, last=False, ks=(0, 1)):
                n_, slot, _ = place(u, step, per)
                pe.wait_ge(sem("lo_ready"), n_ + 1)
                pe.wait_ge(sem("ffn_hidT"), NFC * FFNS.index(f) + c + 1)
                hi = w_hi[:, slot, :].rearrange("p (k n) -> p k n", k=2)
                lo = w_lo[:, slot, :].rearrange("p (k n) -> p k n", k=2)
                if last:
                    for h in range(2):
                        cs = slice(512 * h, 512 * h + 512)
                        for t in range(TT):
                            for k in range(2):
                                to = psum[:, 4 + 2 * t + h, :]
                                a, b = last_hidT_hi[:, k, t * P:(t + 1) * P], last_hidT_lo[:, k, t * P:(t + 1) * P]
                                pe.matmul(to, a, hi[:, k, cs], start=False, stop=False)
                                pe.matmul(to, a, lo[:, k, cs], start=False, stop=False)
                                m = pe.matmul(to, b, hi[:, k, cs], start=False, stop=k == 1)
                        m.then_inc(sem("unit_used" if h else "down_half"), 1)
                    return
                for k in ks:
                    for t in range(TT):
                        a, b = hidT_hi[:, k, t * P:(t + 1) * P], hidT_lo[:, k, t * P:(t + 1) * P]
                        begin = first and k == 0
                        for h in range(2):
                            to, cs = psum[:, 4 + 2 * t + h, :], slice(512 * h, 512 * h + 512)
                            pe.matmul(to, a, hi[:, k, cs], start=begin, stop=False)
                            pe.matmul(to, a, lo[:, k, cs], start=False, stop=False)
                            m = pe.matmul(to, b, hi[:, k, cs], start=False, stop=False)
                if k == 1:
                    m.then_inc(sem("unit_used"), 1)

            def turn(c):
                for t in range(TT):
                    pe.wait_ge(sem("ffn_hid"), TT * (NFC * FFNS.index(f) + c) + t + 1)
                    for k in range(2):
                        m = pe.transpose(psum[:, 2, k * SEQ + t * P:k * SEQ + (t + 1) * P],
                                         hid[:, t, k * P:(k + 1) * P], ident)
                m.then_inc(sem("ffn_turned"), 1)

            gate_up(u0, 0, first=True)
            turn(0)
            gate_up(u0 + 2, 1)
            down(u0 + 4, 0, first=True)
            turn(1)
            with pe.Fori(2, NFC - 1) as c:
                gate_up(u0 + 5, c, c - 2, 3)
                down(u0 + 7, c - 1, c - 2, 3)
                turn(c)
            gate_up(u0 + 3 * NFC - 4, NFC - 1)
            down(u0 + 3 * NFC - 2, NFC - 2, ks=(0,))
            turn(NFC - 1)
            down(u0 + 3 * NFC - 2, NFC - 2, ks=(1,))
            if before_last:
                before_last(pe)
            down(u0 + 3 * NFC - 1, NFC - 1, last=True)

        def ffn_act(act, f, n):
            u0 = FIRST_UNIT[f]

            def gate(u, c, step=0, per=0, first=False):
                act.wait_ge(sem("unit_used"), place(u, step, per)[0] + 1)
                if first:
                    act.wait_ge(sem("rstd"), n + 1)
                else:
                    act.wait_ge(sem("ffn_hid"), TT * (NFC * FFNS.index(f) + c))
                for t in range(TT):
                    act.activation(silu_g[:, t, :], psum[:, t, 0:FC], ACT.Silu, scale=rstd[:, t:t + 1])\
                       .then_inc(sem("ffn_silu"), 1)

            def turned(c, to=hidT_hi):
                act.wait_ge(sem("ffn_turned"), NFC * FFNS.index(f) + c + 1)
                act.activation(to[:, :, :], psum[:, 2, :].rearrange("p (k n) -> p k n", k=2), ACT.Copy)\
                   .then_inc(sem("ffn_hidT_hi"), 1)

            split_hi(act, u0 + SLOTS)
            gate(u0 + 1, 0, first=True)
            split_hi(act, u0 + 1 + SLOTS)
            turned(0)
            split_hi(act, u0 + 2 + SLOTS)
            gate(u0 + 3, 1)
            split_hi(act, u0 + 3 + SLOTS)
            split_hi(act, u0 + 4 + SLOTS)
            turned(1)
            with act.Fori(2, NFC - 1) as c:
                split_hi(act, u0 + 5 + SLOTS, c - 2, 3)
                gate(u0 + 6, c, c - 2, 3)
                split_hi(act, u0 + 6 + SLOTS, c - 2, 3)
                split_hi(act, u0 + 7 + SLOTS, c - 2, 3)
                turned(c)
            split_hi(act, u0 + 3 * NFC - 4 + SLOTS)
            gate(u0 + 3 * NFC - 3, NFC - 1)
            split_hi(act, u0 + 3 * NFC - 3 + SLOTS)
            turned(NFC - 1, last_hidT_hi)
            split_hi(act, u0 + 3 * NFC - 2 + SLOTS)

        def ffn_dve(dve, f, before_last=None):
            u0 = FIRST_UNIT[f]

            def times_up(c, first=False):
                if not first:
                    dve.wait_ge(sem("ffn_turned"), NFC * FFNS.index(f) + c)
                for t in range(TT):
                    dve.wait_ge(sem("ffn_silu"), TT * (NFC * FFNS.index(f) + c) + t + 1)
                    dve.scalar_tensor_tensor(hid[:, t, :], psum[:, t, FC:2 * FC], rstd[:, t:t + 1], silu_g[:, t, :],
                                             ALU.mult, ALU.mult).then_inc(sem("ffn_hid"), 1)

            def turned(c, hi=hidT_hi, lo=hidT_lo):
                dve.wait_ge(sem("ffn_hidT_hi"), NFC * FFNS.index(f) + c + 1)
                dve.tensor_tensor(lo[:, :, :], psum[:, 2, :].rearrange("p (k n) -> p k n", k=2),
                                  hi[:, :, :].bitcast(F32), ALU.subtract).then_inc(sem("ffn_hidT"), 1)

            split_lo(dve, u0 + SLOTS)
            times_up(0, first=True)
            split_lo(dve, u0 + 1 + SLOTS)
            turned(0)
            split_lo(dve, u0 + 2 + SLOTS)
            times_up(1)
            split_lo(dve, u0 + 3 + SLOTS)
            split_lo(dve, u0 + 4 + SLOTS)
            turned(1)
            with dve.Fori(2, NFC - 1) as c:
                split_lo(dve, u0 + 5 + SLOTS, c - 2, 3)
                times_up(c)
                split_lo(dve, u0 + 6 + SLOTS, c - 2, 3)
                split_lo(dve, u0 + 7 + SLOTS, c - 2, 3)
                turned(c)
            split_lo(dve, u0 + 3 * NFC - 4 + SLOTS)
            times_up(NFC - 1)
            split_lo(dve, u0 + 3 * NFC - 3 + SLOTS)
            turned(NFC - 1, last_hidT_hi, last_hidT_lo)
            split_lo(dve, u0 + 3 * NFC - 2 + SLOTS)
            if before_last:
                before_last(dve)
            for h in range(2):
                if h:
                    dve.wait_ge(sem("unit_used"), u0 + 3 * NFC)
                else:
                    dve.wait_ge(sem("down_half"), FFNS.index(f) + 1)
                cs = slice(512 * h, 512 * h + 512)
                for t in range(TT):
                    dve.scalar_tensor_tensor(x[:, t, cs], psum[:, 4 + 2 * t + h, :], 0.5, x[:, t, cs],
                                             ALU.mult, ALU.add).then_inc(sem("x_added"), 1)

        def start_sp(sp):
            for t in range(TT):
                sp.dma_start(x[:, t, :], w["x"][0, t * P:(t + 1) * P, :]).then_inc(sem("x_in"), 16)

        def start_act_loads(act):
            act.dma_start(const1[:, :], w["first_constants"]).then_inc(sem("const1_in"), 16)
            for name, (a, n) in ROWS.items():
                src = w[name]
                src = src.rearrange("l (r c) -> (l r) c", c=P)
                act.dma_start(rows_in[a:a + n, :], src).then_inc(sem("rows_in"), 16)
            act.dma_start(taps_in[:, :], w["ssm_conv_w"][0].rearrange("t (r c) -> (t r) c", c=P))\
               .then_inc(sem("rows_in"), 16)

        ROWS_IN = 16 * (len(ROWS) + 1)

        def start_pool(pool):
            pool.memset(neg_half[:, :], -0.5).then_inc(sem("neg_half"), 1)
            pool.dma_start(pos_i[:, :], w["positions"][0].rearrange("(t p) -> p t", p=P),
                           allow_slow_non_contiguous=True).then_inc(sem("pos_in"), 16)
            pool.dma_start(gains[:, 0, :], w["attn_q_norm"][0].partition_broadcast(P)).then_inc(sem("pos_in"), 16)
            pool.dma_start(gains[:, 1, :], w["attn_k_norm"][0].partition_broadcast(P)).then_inc(sem("pos_in"), 16)
            pool.dma_start(b_ada[:, :], w["b_ada_2"]).then_inc(sem("b_ada_in"), 16)
            pool.wait_ge(sem("neg_half"), 1)

        def ada_pool(pool):
            src = w["w_ada_2"][0].rearrange("(k p) n -> p k n", p=P)
            order = in_order(pool, "gpsimd_order")

            def load(k):
                pool.dma_start(ada_in[:, k % 2, :], src[:, k, :]).then_inc(sem(f"ada_in_{k % 2}"), 16)

            load(0)
            load(1)
            pool.wait_ge(sem("silu_c"), 1)
            for k in range(KD):
                pool.wait_ge(sem(f"ada_in_{k % 2}"), 16 * (k // 2 + 1))
                to = ada if k == 0 else ada_term
                order(pool.tensor_scalar(to[:, :], ada_in[:, k % 2, :], silu_c[:, k:k + 1], None, ALU.mult))
                if k + 2 < KD:
                    load(k + 2)
                if k:
                    order(pool.tensor_tensor(ada[:, :], ada[:, :], ada_term[:, :], ALU.add))
            pool.wait_ge(sem("b_ada_in"), 16)
            pool.tensor_tensor(ada[0:1, :], ada[0:1, :], b_ada[:, :], ALU.add).then_inc(sem("ada"), 1)

        def start_pe(pe):
            pe.wait_ge(sem("const1_in"), 16)
            pe.wait_ge(sem("rows_in"), ROWS_IN)
            pe.transpose(psum[:, 0, 0:P], rows_in[:, :], ident)
            pe.transpose(psum[:, 0, P:2 * P], taps_in[:, :], ident).then_inc(sem("rows_turned"), 1)

        def start_act(act):
            start_act_loads(act)
            split_hi(act, 0)
            act.wait_ge(sem("cols"), 2)
            act.activation(silu_c[:, :], col("c_2", 0, KD), ACT.Silu).then_inc(sem("silu_c"), 1)

        def trig_act(act):
            act.wait_ge(sem("angles"), 1)
            act.activation(trig[:, :, :, :], angle[:, :, :, :], ACT.Sin).then_inc(sem("trig"), 1)

        def start_dve(dve):
            split_lo(dve, 0)
            dve.wait_ge(sem("rows_turned"), 1)
            dve.tensor_copy(cols[:, :], psum[:, 0, 0:P]).then_inc(sem("cols"), 1)
            dve.tensor_copy(taps[:, :], psum[:, 0, P:2 * P]).then_inc(sem("cols"), 1)
            dve.wait_ge(sem("cols"), 2)

        def trig_dve(dve):
            order = in_order(dve, "vector_order")
            dve.wait_ge(sem("pos_in"), 48)
            order(dve.tensor_copy(pos_f[:, :], pos_i[:, :]))
            for t in range(TT):
                order(dve.tensor_scalar(angle[:, 0, t, :], c1("freq"), pos_f[:, t:t + 1], None, ALU.mult))
            order(dve.tensor_copy(angle[:, 1, :, :], angle[:, 0, :, :]))
            order(dve.tensor_scalar(turns[:, 0, :, :], angle[:, 0, :, :], 1 / (2 * np.pi), None, ALU.mult),
                  dve.tensor_scalar(turns[:, 1, :, :], angle[:, 1, :, :], 1 / (2 * np.pi), 0.25, ALU.mult, ALU.add))
            order(dve.tensor_scalar(turns[:, :, :, :], turns[:, :, :, :], ROUND, None, ALU.add))
            order(dve.tensor_scalar(turns[:, :, :, :], turns[:, :, :, :], ROUND, None, ALU.subtract))
            for part in (TWO_PI_HI, TWO_PI_MID, TWO_PI_LO):
                order(dve.scalar_tensor_tensor(angle[:, :, :, :], turns[:, :, :, :], -part, angle[:, :, :, :],
                                               ALU.mult, ALU.add))
            order(dve.tensor_scalar(angle[:, 1, :, :], angle[:, 1, :, :], np.pi / 2, None, ALU.add))
            limit = 3.1415925
            dve.tensor_scalar(angle[:, :, :, :], angle[:, :, :, :], -limit, limit, ALU.max, ALU.min)\
               .then_inc(sem("angles"), 1)
            dve.wait_ge(sem("trig"), 1)
            sin, cos = trig[:, 0, :, :], trig[:, 1, :, :]
            for g, name in enumerate(("q", "k")):
                for part, table, h in (("cos1", cos, 0), ("sin2", sin, 1), ("cos2", cos, 1), ("sin1", sin, 0)):
                    gain = gains[:, g:g + 1, h * HALF:(h + 1) * HALF].broadcast_to([P, TT, HALF])
                    dve.tensor_tensor(rope_c[name, part][:, :, :], table, gain, ALU.mult).then_inc(sem("rope_tables"), 1)

        def ada_pe(pe):
            pe.wait_ge(sem("ada"), 1)
            for h in range(2):
                pe.matmul(psum[:, h, :], ones, ada[:, 2 * D + 512 * h:2 * D + 512 * (h + 1)], start=True, stop=True)
            for j in range(2 * KD):
                m = pe.matmul(psum[:, 3, j:j + 1], ada[:, j * P:(j + 1) * P], ones[:, 0:1], start=True, stop=True)
            m.then_inc(sem("mod_ready"), 1)

        def ada_dve(dve):
            dve.wait_ge(sem("mod_ready"), 1)
            dve.tensor_copy(gate2[:, :].rearrange("p (a n) -> p a n", a=2), psum[:, 0:2, :]).then_inc(sem("mod_read"), 1)
            dve.tensor_copy(mod_cols[:, :], psum[:, 3, 0:2 * KD]).then_inc(sem("mod_read"), 1)
            dve.wait_ge(sem("mod_read"), 2)
            dve.scalar_tensor_tensor(gain2[:, :], mod_cols[:, KD:2 * KD], 1.0, col("norm_g_2", 0, KD),
                                     ALU.add, ALU.mult).then_inc(sem("gain2"), 1)

        def heads(ap):
            return ap.rearrange("p t (h d) -> p t h d", d=HD)

        def attn_pe(pe):
            pe.wait_ge(sem("mod_read"), 2)
            norm_pe(pe, 1, True)
            u = FIRST_UNIT["qkv"]
            for n in range(6):
                if n >= 3:
                    pe.wait_ge(sem("qkv_copied"), TT * (n - 2))
                b = 2 * (n % 3)
                linear_chunk(pe, u + 2 * n, (0, 4), hT_hi, hT_lo, (b, b + 1), ("hT", KD * 1) if n == 0 else None)
            pe.wait_ge(sem("qkv_copied"), TT * 6)
            pe.wait_ge(sem("roped_1"), 4)
            pe.wait_ge(sem("roped_2"), 4)
            for i in range(HEADS + 3):
                if i < HEADS:
                    h = i
                    if h >= 2:
                        pe.wait_ge(sem("qkT"), h - 1)
                    for j in range(2):
                        for t in range(TT):
                            c = j * D + h * HD
                            m = pe.transpose(psum[:, h % 2, j * SEQ + t * P:j * SEQ + (t + 1) * P],
                                             qk[:, t, c:c + HD], ident)
                    m.then_inc(sem("qk_turned"), 1)
                h = i - 1
                if 0 <= h < HEADS:
                    pe.wait_ge(sem("qkT"), h + 1)
                    if h >= 2:
                        pe.wait_ge(sem("exps"), 2 * (h - 1))
                    for t in range(TT):
                        m = pe.matmul(psum[:, 2 + h % 2, t * SEQ:(t + 1) * SEQ], qkT[:, h % 2, 0, t * P:(t + 1) * P],
                                      qkT[:, h % 2, 1, :], start=True, stop=True)
                    m.then_inc(sem("scores"), 1)
                h = i - 2
                if 0 <= h < HEADS:
                    pe.wait_ge(sem("prob"), h + 1)
                    if h >= 2:
                        pe.wait_ge(sem("probT"), h - 1)
                    to = psum[:, 4 + h % 2, :]
                    pe.transpose(to[:, 0:P], prob[:, h % 2, 0, 0:P], ident)
                    pe.transpose(to[:, P:2 * P], prob[:, h % 2, 1, 0:P], ident)
                    pe.transpose(to[:, 2 * P:3 * P], prob[:, h % 2, 1, P:2 * P], ident).then_inc(sem("prob_turned"), 1)
                h = i - 3
                if 0 <= h < HEADS:
                    pe.wait_ge(sem("probT"), h + 1)
                    if h >= 2:
                        pe.wait_ge(sem("oT"), h - 1)
                    to = psum[:, 6 + h % 2, 0:SEQ]
                    pe.matmul(to, v_sb[:, 0, h * HD:(h + 1) * HD], probT[:, h % 2, 0:SEQ], start=True, stop=False)
                    pe.matmul(to[:, P:2 * P], v_sb[:, 1, h * HD:(h + 1) * HD], probT[:, h % 2, SEQ:SEQ + P],
                              start=False, stop=True).then_inc(sem("o_ready"), 1)
            for n in range(2):
                linear_chunk(pe, FIRST_UNIT["wo"] + 2 * n, (0, 4), hT_hi, hT_lo, ((0, 1), (5, 7))[n],
                             ("oT", 0) if n == 0 else None)

        def attn_act(act):
            u = FIRST_UNIT["qkv"]
            norm_act(act, 1, ("mix_norm", 0), True, u - 1 + SLOTS)
            act.wait_ge(sem("rstd"), 2)
            for n in range(6):
                split_hi(act, u + 2 * n + SLOTS)
                act.wait_ge(sem("unit_used"), u + 2 * n + 2)
                b, cs = 2 * (n % 3), slice(512 * n, 512 * n + 512)
                to = qk[:, :, cs] if n < 4 else v_sb[:, :, 512 * (n - 4):512 * (n - 3)]
                for t in range(TT):
                    act.activation(to[:, t, :], psum[:, b + t, :], ACT.Copy, scale=rstd[:, t:t + 1])\
                       .then_inc(sem("qkv_copied"), 1)
                if n < 4:
                    if n:
                        act.wait_ge(sem("qk_ss"), n)
                    act.wait_ge(sem("qkv_copied"), TT * (n + 1))
                    act.activation(qk_sq[:, :, :], qk[:, :, cs], ACT.Square).then_inc(sem("qk_sq"), 1)
                split_hi(act, u + 2 * n + 1 + SLOTS)
            for i in range(HEADS + 3):
                if i < HEADS:
                    h = i
                    act.wait_ge(sem("qk_turned"), h + 1)
                    if h >= 2:
                        act.wait_ge(sem("scores"), h - 1)
                    act.activation(qkT[:, h % 2, :, :], psum[:, h % 2, :].rearrange("p (j n) -> p j n", j=2), ACT.Copy)\
                       .then_inc(sem("qkT"), 1)
                h = i - 1
                if 0 <= h < HEADS:
                    act.wait_ge(sem("bias"), h + 1)
                    if h >= 2:
                        act.wait_ge(sem("prob_turned"), h - 1)
                    for t in range(TT):
                        act.activation(prob[:, h % 2, t, :], psum[:, 2 + h % 2, t * SEQ:(t + 1) * SEQ], ACT.Exp,
                                       bias=bias_s[:, h, t:t + 1], scale=SCALE, accum_out=sum_s[:, h, t:t + 1])\
                           .then_inc(sem("exps"), 1)
                h = i - 2
                if 0 <= h < HEADS:
                    act.wait_ge(sem("prob_turned"), h + 1)
                    if h >= 2:
                        act.wait_ge(sem("o_ready"), h - 1)
                    act.activation(probT[:, h % 2, :], psum[:, 4 + h % 2, 0:3 * P], ACT.Copy).then_inc(sem("probT"), 1)
                h = i - 3
                if 0 <= h < HEADS:
                    act.wait_ge(sem("o_ready"), h + 1)
                    act.activation(hT_hi[:, h, :], psum[:, 6 + h % 2, 0:SEQ], ACT.Copy).then_inc(sem("oT_hi"), 1)
            for j in range(3):
                split_hi(act, FIRST_UNIT["wo"] + j + SLOTS)

        def attn_pool(pool):
            norm_pool(pool, 1)
            pool.wait_ge(sem("rope_tables"), 8)
            for n in range(4):
                cs = slice(4 * n, 4 * n + 4)
                pool.wait_ge(sem("qk_ss"), n + 1)
                pool.tensor_scalar(qk_ms[:, :, cs], qk_ss[:, :, cs], 1.0 / HD, EPS, ALU.mult, ALU.add)\
                    .then_inc(sem("qk_ms"), 1)
                pool.wait_ge(sem("qk_ms"), n + 1)
                pool.tensor_tensor(qk_rstd[:, :, cs], qk_ms[:, :, cs],
                                   neg_half[:, 0:8].rearrange("p (t h) -> p t h", t=TT), ALU.pow)\
                    .then_inc(sem("qk_rstd"), 1)
                pool.wait_ge(sem("qk_scaled"), n + 1)
                if n:
                    pool.wait_ge(sem("roped_2"), n)
                name = "q" if n < 2 else "k"
                both = heads(qk[:, :, 512 * n:512 * n + 512])
                one, two = both[:, :, :, 0:HALF], both[:, :, :, HALF:HD]
                pool.tensor_tensor(rope_d[:, :, :, :], two, by_head(rope_c[name, "cos2"]), ALU.mult)\
                    .then_inc(sem("rope_de"), 1)
                pool.tensor_tensor(rope_e[:, :, :, :], one, by_head(rope_c[name, "sin1"]), ALU.mult)\
                    .then_inc(sem("rope_de"), 1)
                pool.wait_ge(sem("rope_de"), 2 * n + 2)
                pool.wait_ge(sem("rope_ab"), 2 * n + 2)
                pool.tensor_tensor(two, rope_d[:, :, :, :], rope_e[:, :, :, :], ALU.add).then_inc(sem("roped_2"), 1)

        def by_head(table):
            return table[:, :, :].unsqueeze(2).broadcast_to([P, TT, 4, HALF])

        def attn_dve(dve):
            u = FIRST_UNIT["qkv"]
            norm_dve(dve, 1, ("mix_norm", 0), True, u - 1 + SLOTS)
            for n in range(6):
                split_lo(dve, u + 2 * n + SLOTS)
                if n < 4:
                    both = heads(qk[:, :, 512 * n:512 * n + 512])
                    one, two = both[:, :, :, 0:HALF], both[:, :, :, HALF:HD]
                    name = "q" if n < 2 else "k"
                    dve.wait_ge(sem("qk_sq"), n + 1)
                    dve.tensor_reduce(qk_ss[:, :, 4 * n:4 * n + 4], heads(qk_sq[:, :, :]), X_AXIS, ALU.add)\
                       .then_inc(sem("qk_ss"), 1)
                split_lo(dve, u + 2 * n + 1 + SLOTS)
                if n < 4:
                    dve.wait_ge(sem("qk_rstd"), n + 1)
                    r_ = qk_rstd[:, :, 4 * n:4 * n + 4].unsqueeze(3).broadcast_to([P, TT, 4, HD])
                    dve.tensor_tensor(both, both, r_, ALU.mult).then_inc(sem("qk_scaled"), 1)
                    dve.wait_ge(sem("qk_scaled"), n + 1)
                    if n:
                        dve.wait_ge(sem("roped_1"), n)
                    dve.wait_ge(sem("rope_tables"), 8)
                    dve.tensor_tensor(rope_a[:, :, :, :], one, by_head(rope_c[name, "cos1"]), ALU.mult)\
                       .then_inc(sem("rope_ab"), 1)
                    dve.tensor_tensor(rope_b[:, :, :, :], two, by_head(rope_c[name, "sin2"]), ALU.mult)\
                       .then_inc(sem("rope_ab"), 1)
                    dve.wait_ge(sem("rope_ab"), 2 * n + 2)
                    dve.wait_ge(sem("rope_de"), 2 * n + 2)
                    dve.tensor_tensor(one, rope_a[:, :, :, :], rope_b[:, :, :, :], ALU.subtract)\
                       .then_inc(sem("roped_1"), 1)
            order = in_order(dve, "vector_order")
            mask = c1("causal")
            for i in range(1, HEADS + 3):
                h = i - 1
                if h < HEADS:
                    dve.wait_ge(sem("scores"), h + 1)
                    s = psum[:, 2 + h % 2, :]
                    order(dve.tensor_tensor(s, s, mask, ALU.add))
                    order(dve.tensor_reduce(top_s[:, h, :], s.rearrange("p (t k) -> p t k", t=TT), X_AXIS, ALU.max))
                    dve.tensor_scalar(bias_s[:, h, :], top_s[:, h, :], -SCALE, None, ALU.mult).then_inc(sem("bias"), 1)
                    dve.wait_ge(sem("exps"), 2 * h + 2)
                    order(dve.reciprocal(inv_s[:, h, :], sum_s[:, h, :]))
                    dve.tensor_tensor(prob[:, h % 2, :, :], prob[:, h % 2, :, :],
                                      inv_s[:, h, :].unsqueeze(2).broadcast_to([P, TT, SEQ]), ALU.mult)\
                       .then_inc(sem("prob"), 1)
                h = i - 3
                if h >= 0:
                    dve.wait_ge(sem("oT_hi"), h + 1)
                    dve.tensor_tensor(hT_lo[:, h, :], psum[:, 6 + h % 2, 0:SEQ], hT_hi[:, h, :].bitcast(F32),
                                      ALU.subtract).then_inc(sem("oT"), 1)
            add_to_x(dve, "wo", 2, ((0, 1), (5, 7)))

        def add_to_x(dve, stage, units, banks):
            u = FIRST_UNIT[stage]
            for h in range(2):
                for j in range(units - 1):
                    split_lo(dve, u + units * h + j + SLOTS)
                dve.wait_ge(sem("unit_used"), u + units * (h + 1))
                for t in range(TT):
                    cs = slice(512 * h, 512 * h + 512)
                    dve.tensor_tensor(x[:, t, cs], psum[:, banks[h][t], :], x[:, t, cs], ALU.add)\
                       .then_inc(sem("x_added"), 1)
                if h == 0:
                    split_lo(dve, u + units - 1 + SLOTS)

        CHUNKS = CONVD // 512
        X_CHUNKS = DI // 512
        B_CHUNKS = NB // 512
        ITEMS = GROUPS * TT

        def ssm_sp(sp):
            load_linear(sp, "ssm_xbc", "ssm_w_in", DI, (0, 4), CHUNKS)
            u = FIRST_UNIT["ssm_dt"]
            src = w["ssm_w_in"][0].rearrange("(k p) n -> p k n", p=P)[:, :, DI + CONVD:DI + CONVD + SH]
            dst = raw[:, u % SLOTS, 0:KD * SH].rearrange("p (k n) -> p k n", k=KD)
            load_unit(sp, u, [(dst[:, k:k + 4, :], src[:, k:k + 4, :]) for k in (0, 4)])
            load_linear(sp, "ssm_z", "ssm_w_in", 0, (0, 4), DI // 512)
            load_linear(sp, "ssm_out", "ssm_w_out", 0, (0, 4, 8, 12), 2)

        def ssm_pe(pe):
            norm_pe(pe, 4, False)
            u = FIRST_UNIT["ssm_xbc"]
            for c in range(CHUNKS):
                if c >= 2:
                    pe.wait_ge(sem("conv_out"), 4 * (c - 1))
                b = 2 * (c % 2)
                turned_chunk(pe, u + 2 * c, (b, b + 1), ("hT", KD * 4) if c == 0 else None)
                if 1 <= c <= X_CHUNKS + B_CHUNKS:
                    ssm_turn(pe, c - 1)
            hi, lo = use_unit(pe, FIRST_UNIT["ssm_dt"])
            slot = FIRST_UNIT["ssm_dt"] % SLOTS
            hi = w_hi[:, slot, 0:KD * SH].rearrange("p (k n) -> p k n", k=KD)
            lo = w_lo[:, slot, 0:KD * SH].rearrange("p (k n) -> p k n", k=KD)
            for t in range(TT):
                to = psum[:, 6, t * SH:(t + 1) * SH]
                for k in range(KD):
                    a, b = hT_hi[:, k, t * P:(t + 1) * P], hT_lo[:, k, t * P:(t + 1) * P]
                    pe.matmul(to, a, hi[:, k, :], start=k == 0, stop=False)
                    pe.matmul(to, a, lo[:, k, :], start=False, stop=False)
                    m = pe.matmul(to, b, hi[:, k, :], start=False, stop=k == KD - 1)
            m.then_inc(sem("unit_used"), 1)

            def z_unit(j):
                q, k0 = j // 2, 4 * (j % 2)
                if j % 2 == 0:
                    pe.wait_ge(sem("conv_out"), 4 * CHUNKS)
                    if q:
                        pe.wait_ge(sem("z"), q)
                hi, lo = use_unit(pe, FIRST_UNIT["ssm_z"] + j)
                for kk in range(4):
                    k = k0 + kk
                    for t in range(TT):
                        a, b = hT_hi[:, k, t * P:(t + 1) * P], hT_lo[:, k, t * P:(t + 1) * P]
                        pe.matmul(psum[:, t, :], a, hi[:, kk, :], start=k == 0, stop=False)
                        pe.matmul(psum[:, t, :], a, lo[:, kk, :], start=False, stop=False)
                        m = pe.matmul(psum[:, t, :], b, hi[:, kk, :], start=False, stop=k == KD - 1)
                m.then_inc(sem("unit_used"), 1)

            def scores(i):
                g, t = divmod(i, TT)
                if i >= 2:
                    pe.wait_ge(sem("ssm_diff"), HPG * (i - 1))
                for hh in range(HPG):
                    pe.matmul(psum[:, 2 + i % 2, hh * P:(hh + 1) * P],
                              per_token["a_dt"][:, t, HPG * g + hh:HPG * g + hh + 1].broadcast_to([P, P]),
                              c1("runsum"), start=True, stop=True)
                if i >= 2:
                    pe.wait_ge(sem("within"), i - 1)
                ts = slice(t * P, (t + 1) * P)
                pe.matmul(psum[:, 4 + i % 2, 0:P], bcT[:, g, ts], bcT[:, GROUPS + g, ts], start=True, stop=True)\
                  .then_inc(sem("ssm_scores"), 1)

            def outputs(i):
                g, t = divmod(i, TT)
                pe.wait_ge(sem("within"), i + 1)
                pe.wait_ge(sem("xdt"), i + 1)
                if i >= 2:
                    pe.wait_ge(sem("y"), i - 1)
                bank = psum[:, 6 + i % 2, :]
                for hh in range(HPG):
                    pe.matmul(bank[:, hh * SP:(hh + 1) * SP], within[:, i % 2, hh, :], xdt[:, i % 2, hh, :],
                              start=True, stop=True)
                if t == 0:
                    pe.wait_ge(sem("x_decayed"), g + 1)
                    m = pe.matmul(bank[:, GW:2 * GW], b_rows[:, g, :], x_decayed[:, :, :], start=True, stop=True)
                else:
                    pe.wait_ge(sem("states"), g + 1)
                    m = pe.matmul(bank[:, GW:2 * GW], bcT[:, GROUPS + g, P:SEQ], states[:, g % 2, :],
                                  start=True, stop=True)
                m.then_inc(sem("ssm_out"), 1)

            for j in range(ITEMS // 2 + 1):
                if j < ITEMS // 2:
                    z_unit(j)
                    if j == 0:
                        pe.wait_ge(sem("a_dt"), 1)
                        for t in range(TT):
                            pe.matmul(psum[:, 7, t * SH:(t + 1) * SH], c1("runsum"), per_token["a_dt"][:, t, :],
                                      start=True, stop=True)
                        pe.matmul(psum[:, 7, 2 * SH:3 * SH], ones, per_token["a_dt"][:, 0, :], start=True, stop=True)\
                          .then_inc(sem("a_sums"), 1)
                        pe.wait_ge(sem("a_sum"), 2)
                    scores(2 * j)
                    scores(2 * j + 1)
                if j:
                    outputs(2 * j - 2)
                    outputs(2 * j - 1)
            for q in range(4):
                pe.wait_ge(sem("y_scaled"), q + 1)
                if q >= 2:
                    pe.wait_ge(sem("yT"), 4 * (q - 1))
                for kk in range(4):
                    k, b = 4 * q + kk, 2 + 2 * (q % 2) + kk // 2
                    for t in range(TT):
                        at_ = (kk % 2) * SEQ + t * P
                        m = pe.transpose(psum[:, b, at_:at_ + P], y[:, t, k * P:(k + 1) * P], ident)
                    m.then_inc(sem("y_turned"), 1)
            u = FIRST_UNIT["ssm_out"]
            linear_chunk(pe, u, (0, 4, 8, 12), yT_hi, yT_lo, (0, 1), ("yT", 0))
            linear_chunk(pe, u + 4, (0, 4, 8, 12), yT_hi, yT_lo, (5, 7))

        def ssm_turn(pe, c):
            pe.wait_ge(sem("xbc"), 4 * (c + 1))
            if c:
                pe.wait_ge(sem("rows"), c)
            for i in range(4):
                if c < X_CHUNKS:
                    for t in range(TT):
                        m = pe.transpose(psum[:, 4 + t, i * P:(i + 1) * P], xT[:, c % 2, i, t * P:(t + 1) * P], ident)
                else:
                    m = pe.transpose(psum[:, 4, i * P:(i + 1) * P], bcT[:, 4 * (c - X_CHUNKS) + i, 0:P], ident)
            m.then_inc(sem("rows_ready"), 1)

        def ssm_act(act):
            u = FIRST_UNIT["ssm_xbc"]
            norm_act(act, 4, ("mix_norm", KD), False, u - 1 + SLOTS)

            def copy_rows(c):
                act.wait_ge(sem("rows_ready"), c + 1)
                if c < X_CHUNKS:
                    act.activation(xs[:, :, 512 * c:512 * (c + 1)], psum[:, 4:6, :], ACT.Copy).then_inc(sem("rows"), 1)
                else:
                    g = 4 * (c - X_CHUNKS)
                    act.activation(b_rows[:, g:g + 4, :], psum[:, 4, :].rearrange("p (g n) -> p g n", g=4), ACT.Copy)\
                       .then_inc(sem("rows"), 1)

            for c in range(CHUNKS):
                split_hi(act, u + 2 * c + SLOTS)
                act.wait_ge(sem("unit_used"), u + 2 * c + 2)
                if c >= 2:
                    act.wait_ge(sem("xbc"), 4 * (c - 1))
                for i in range(4):
                    tile = 4 * c + i
                    act.activation(conv[:, c % 2, i, :], psum[:, 2 * (c % 2) + i // 2, (i % 2) * SEQ:(i % 2 + 1) * SEQ],
                                   ACT.Copy, scale=taps[:, (TAPS - 1) * 32 + tile:(TAPS - 1) * 32 + tile + 1])\
                       .then_inc(sem("conv_first"), 1)
                split_hi(act, u + 2 * c + 1 + SLOTS)
                if 1 <= c <= X_CHUNKS + B_CHUNKS:
                    copy_rows(c - 1)
                for i in range(4):
                    tile = 4 * c + i
                    act.wait_ge(sem("conv_out"), tile + 1)
                    if i == 0 and 2 <= c < X_CHUNKS:
                        act.wait_ge(sem("rows_ready"), c - 1)
                    to = xT[:, c % 2, i, :] if c < X_CHUNKS else bcT[:, tile - 4 * X_CHUNKS, :]
                    act.activation(to, conv[:, c % 2, i, :], ACT.Silu, bias=col("ssm_conv_b", tile))\
                       .then_inc(sem("xbc"), 1)
            act.wait_ge(sem("per_head_in"), 48)
            act.activation(per_head["a_rate"][:, :], per_head["a_rate"][:, :], ACT.Exp).then_inc(sem("a_rate"), 1)
            split_hi(act, FIRST_UNIT["ssm_dt"] + SLOTS)
            act.wait_ge(sem("dt_abs"), 1)
            act.activation(per_token["dt_exp"][:, :, :], per_token["dt_a"][:, :, :], ACT.Exp, scale=-1.0)\
               .then_inc(sem("dt_exp"), 1)
            act.wait_ge(sem("a_sum"), 2)
            act.activation(per_head["end_decay"][:, :], per_head["end_decay"][:, :], ACT.Exp).then_inc(sem("decays"), 1)
            act.activation(per_head["start_decay"][:, :], per_token["a_sum"][:, 1, :], ACT.Exp)\
               .then_inc(sem("decays"), 1)

            def exps(i):
                act.wait_ge(sem("ssm_diff"), HPG * (i + 1))
                act.activation(decay[:, i % 2, :, :], decay[:, i % 2, :, :], ACT.Exp).then_inc(sem("decay"), 1)

            def copy_states(g):
                act.wait_ge(sem("ssm_out"), TT * g + 1)
                act.activation(states[:, g % 2, :], psum[:, 6, GW:2 * GW], ACT.Copy).then_inc(sem("states"), 1)

            for j in range(ITEMS // 2 + 1):
                if j < ITEMS // 2:
                    exps(2 * j)
                    exps(2 * j + 1)
                    split_hi(act, FIRST_UNIT["ssm_z"] + j + SLOTS)
                    if j % 2:
                        q = j // 2
                        act.wait_ge(sem("unit_used"), FIRST_UNIT["ssm_z"] + j + 1)
                        act.activation(z[:, :, 512 * q:512 * (q + 1)], psum[:, 0:TT, :], ACT.Copy).then_inc(sem("z"), 1)
                if j:
                    copy_states(j - 1)
            for q in range(4):
                act.wait_ge(sem("z"), q + 1)
                zq = z[:, :, 512 * q:512 * (q + 1)]
                act.activation(zq, zq, ACT.Silu).then_inc(sem("z_silu"), 1)
            for q in range(4):
                act.wait_ge(sem("y_gated"), q + 1)
                cs = slice(512 * q, 512 * (q + 1))
                act.activation(z[:, :, cs], y[:, :, cs], ACT.Square).then_inc(sem("y_sq"), 1)
            for k in range(KI):
                act.wait_ge(sem("y_turned"), (k | 1) + 1)
                act.activation(yT_hi[:, k, :], y_bank(k), ACT.Copy, scale=col("ssm_norm", k)).then_inc(sem("yT_hi"), 1)
            for j in range(7):
                split_hi(act, FIRST_UNIT["ssm_out"] + j + SLOTS)

        def y_bank(k):
            b = 2 + 2 * (k // 4 % 2) + k % 4 // 2
            return psum[:, b, (k % 2) * SEQ:(k % 2 + 1) * SEQ]

        def ssm_pool(pool):
            for name, src in (("dt_bias", "ssm_dt_bias"), ("a_rate", "ssm_a_log"), ("d_skip", "ssm_d")):
                pool.dma_start(per_head[name][:, :], w[src][0].partition_broadcast(P)).then_inc(sem("per_head_in"), 16)
            norm_pool(pool, 4)
            pool.wait_ge(sem("rows"), X_CHUNKS)
            pool.wait_ge(sem("dt"), 1)
            pool.wait_ge(sem("decays"), 2)
            for i in range(ITEMS):
                g, t = divmod(i, TT)
                src = xs[:, t, g * GW:(g + 1) * GW].rearrange("p (h d) -> p h d", d=SP)
                hs = slice(HPG * g, HPG * (g + 1))
                if i >= 2:
                    pool.wait_ge(sem("ssm_out"), i - 1)
                pool.tensor_tensor(xdt[:, i % 2, :, :], src, by_channel(per_token["dt"][:, t, hs]), ALU.mult)\
                    .then_inc(sem("xdt"), 1)
                if t == 0:
                    pool.wait_ge(sem("xdt"), i + 1)
                    pool.tensor_tensor(x_decayed[:, :, :], xdt[:, i % 2, :, :],
                                       by_channel(per_head["end_decay"][:, hs]), ALU.mult).then_inc(sem("x_decayed"), 1)
                if i >= 2:
                    pool.wait_ge(sem("y"), i - 1)
                pool.tensor_tensor(x_skip[:, i % 2, :, :], src, by_channel(per_head["d_skip"][:, hs]), ALU.mult)\
                    .then_inc(sem("x_skip"), 1)
            for q in range(4):
                gs = slice(2 * q, 2 * q + 2)
                pool.wait_ge(sem("y_ss"), q + 1)
                pool.tensor_scalar(y_ms[:, :, gs], y_ss[:, :, gs], 1.0 / GW, EPS, ALU.mult, ALU.add)\
                    .then_inc(sem("y_ms"), 1)
                pool.wait_ge(sem("y_ms"), q + 1)
                pool.tensor_tensor(y_rstd[:, :, gs], y_ms[:, :, gs],
                                   neg_half[:, 0:4].rearrange("p (t g) -> p t g", t=TT), ALU.pow)\
                    .then_inc(sem("y_rstd"), 1)

        def by_channel(ap):
            return ap.unsqueeze(2).broadcast_to([P, HPG, SP])

        def ssm_dve(dve):
            u = FIRST_UNIT["ssm_xbc"]
            norm_dve(dve, 4, ("mix_norm", KD), False, u - 1 + SLOTS)
            conv_order = in_order(dve, "vector_order")
            for c in range(CHUNKS):
                split_lo(dve, u + 2 * c + SLOTS)
                for j in range(2):
                    dve.wait_ge(sem("conv_first"), 4 * c + 2 * j + 2)
                    for back in range(1, TAPS):
                        steps = []
                        for i in (2 * j, 2 * j + 1):
                            tap = (TAPS - 1 - back) * 32 + 4 * c + i
                            to = conv[:, c % 2, i, back:SEQ]
                            src = psum[:, 2 * (c % 2) + j, (i % 2) * SEQ:(i % 2 + 1) * SEQ - back]
                            steps.append(dve.scalar_tensor_tensor(to, src, taps[:, tap:tap + 1], to, ALU.mult, ALU.add))
                        if back < TAPS - 1:
                            conv_order(*steps)
                        else:
                            for s in steps:
                                s.then_inc(sem("conv_out"), 1)
                split_lo(dve, u + 2 * c + 1 + SLOTS)
            split_lo(dve, FIRST_UNIT["ssm_dt"] + SLOTS)

            order = in_order(dve, "vector_order")
            raw_, a, b, s, p, e = (per_token[n][:, :, :] for n in ("dt_raw", "dt_a", "dt_b", "dt_s", "dt_p", "dt_exp"))
            across = lambda ap: ap.unsqueeze(1).broadcast_to([P, TT, SH])
            dve.wait_ge(sem("per_head_in"), 48)
            dve.wait_ge(sem("unit_used"), FIRST_UNIT["ssm_dt"] + 1)
            order(dve.tensor_tensor(raw_, psum[:, 6, 0:TT * SH].rearrange("p (t h) -> p t h", t=TT),
                                    across(per_head["dt_bias"][:, :]), ALU.add))
            dve.scalar_tensor_tensor(a, raw_, -1.0, raw_, ALU.mult, ALU.max).then_inc(sem("dt_abs"), 1)
            dve.wait_ge(sem("dt_exp"), 1)
            order(dve.tensor_scalar(b, e, 2.0, None, ALU.add))
            order(dve.reciprocal(p, b))
            order(dve.tensor_tensor(s, e, p, ALU.mult))
            order(dve.tensor_tensor(b, s, s, ALU.mult))
            n_terms = 9
            order(dve.tensor_scalar(p, b, 1.0 / (2 * n_terms + 1), None, ALU.mult))
            for n in range(n_terms - 1, 0, -1):
                order(dve.scalar_tensor_tensor(p, p, 1.0 / (2 * n + 1), b, ALU.add, ALU.mult))
            order(dve.scalar_tensor_tensor(p, p, 1.0, s, ALU.add, ALU.mult))
            order(dve.tensor_scalar(p, p, 2.0, None, ALU.mult))
            dve.scalar_tensor_tensor(per_token["dt"][:, :, :], raw_, 0.0, p, ALU.max, ALU.add).then_inc(sem("dt"), 1)
            dve.wait_ge(sem("dt"), 1)
            dve.wait_ge(sem("a_rate"), 1)
            dve.scalar_tensor_tensor(per_token["a_dt"][:, :, :], per_token["dt"][:, :, :], -1.0,
                                     across(per_head["a_rate"][:, :]), ALU.mult, ALU.mult)\
               .then_inc(sem("a_dt"), 1)
            dve.wait_ge(sem("a_sums"), 1)
            dve.tensor_copy(per_token["a_sum"][:, :, :], psum[:, 7, 0:TT * SH].rearrange("p (t h) -> p t h", t=TT))\
               .then_inc(sem("a_sum"), 1)
            dve.wait_ge(sem("a_sum"), 1)
            dve.tensor_tensor(per_head["end_decay"][:, :], psum[:, 7, 2 * SH:3 * SH], per_token["a_sum"][:, 0, :],
                              ALU.subtract).then_inc(sem("a_sum"), 1)

            def differences(i):
                g, t = divmod(i, TT)
                dve.wait_ge(sem("ssm_scores"), i + 1)
                for hh in range(HPG):
                    h = HPG * g + hh
                    dve.scalar_tensor_tensor(decay[:, i % 2, hh, :], psum[:, 2 + i % 2, hh * P:(hh + 1) * P],
                                             per_token["a_sum"][:, t, h:h + 1], c1("causal_t"),
                                             ALU.subtract, ALU.add).then_inc(sem("ssm_diff"), 1)

            def weigh(i):
                dve.wait_ge(sem("decay"), i + 1)
                if i >= 2:
                    dve.wait_ge(sem("ssm_out"), i - 1)
                dve.tensor_tensor(within[:, i % 2, :, :], decay[:, i % 2, :, :],
                                  psum[:, 4 + i % 2, 0:P].unsqueeze(1).broadcast_to([P, HPG, P]), ALU.mult)\
                   .then_inc(sem("within"), 1)

            y_order = in_order(dve, "vector_order")

            def finish(i):
                g, t = divmod(i, TT)
                dve.wait_ge(sem("ssm_out"), i + 1)
                dve.wait_ge(sem("x_skip"), i + 1)
                dve.wait_ge(sem("states"), g + 1)
                to = y[:, t, g * GW:(g + 1) * GW].rearrange("p (h d) -> p h d", d=SP)
                bank = psum[:, 6 + i % 2, :]
                inside = bank[:, 0:GW].rearrange("p (h d) -> p h d", d=SP)
                skip = x_skip[:, i % 2, :, :]
                if t == 0:
                    dve.tensor_tensor(to, inside, skip, ALU.add).then_inc(sem("y"), 1)
                else:
                    y_order(dve.tensor_tensor(to, bank[:, GW:2 * GW].rearrange("p (h d) -> p h d", d=SP),
                                              by_channel(per_head["start_decay"][:, HPG * g:HPG * (g + 1)]), ALU.mult))
                    y_order(dve.tensor_tensor(to, inside, to, ALU.add))
                    dve.tensor_tensor(to, to, skip, ALU.add).then_inc(sem("y"), 1)

            for j in range(ITEMS // 2 + 1):
                if j < ITEMS // 2:
                    differences(2 * j)
                    differences(2 * j + 1)
                    split_lo(dve, FIRST_UNIT["ssm_z"] + j + SLOTS)
                    weigh(2 * j)
                    weigh(2 * j + 1)
                if j:
                    finish(2 * j - 2)
                    finish(2 * j - 1)
            dve.wait_ge(sem("y"), ITEMS)
            for q in range(4):
                cs = slice(512 * q, 512 * (q + 1))
                dve.wait_ge(sem("z_silu"), q + 1)
                dve.tensor_tensor(y[:, :, cs], y[:, :, cs], z[:, :, cs], ALU.mult).then_inc(sem("y_gated"), 1)
            for q in range(4):
                cs, gs = slice(512 * q, 512 * (q + 1)), slice(2 * q, 2 * q + 2)
                dve.wait_ge(sem("y_sq"), q + 1)
                dve.tensor_reduce(y_ss[:, :, gs], z[:, :, cs].rearrange("p t (g c) -> p t g c", c=GW), X_AXIS, ALU.add)\
                   .then_inc(sem("y_ss"), 1)
            for q in range(4):
                cs, gs = slice(512 * q, 512 * (q + 1)), slice(2 * q, 2 * q + 2)
                dve.wait_ge(sem("y_rstd"), q + 1)
                yq = y[:, :, cs].rearrange("p t (g c) -> p t g c", c=GW)
                dve.tensor_tensor(yq, yq, y_rstd[:, :, gs].unsqueeze(3).broadcast_to([P, TT, 2, GW]), ALU.mult)\
                   .then_inc(sem("y_scaled"), 1)
            for k in range(KI):
                dve.wait_ge(sem("yT_hi"), (k | 1) + 1)
                dve.scalar_tensor_tensor(yT_lo[:, k, :], y_bank(k), col("ssm_norm", k), yT_hi[:, k, :].bitcast(F32),
                                         ALU.mult, ALU.subtract).then_inc(sem("yT"), 1)
            add_to_x(dve, "ssm_out", 4, ((0, 1), (5, 7)))

        TURNED = [0, 512, 1024, 1536]
        HG_I, HG_Z, RQ, RV, RZ, GA, GB = 2048, 3072, 4096, 5120, 6144, 7168, 8192
        CHUNKS2 = TURNED + [HG_I, HG_I + 512, RQ, RQ + 512, RV, RV + 512, HG_Z, HG_Z + 512, GA, GA + 512,
                            RZ, RZ + 512, GB, GB + 512]
        NT = len(TURNED)
        TICKS = 2 * (len(CHUNKS2) - NT)
        STEPS = 2 * (LEVELS + 1)
        K_ROWS, STATES_12, STATE_3, OUT_A, RET_TURN, RET_SCORES, RET_STATE, OUT_B = range(STEPS + 3, STEPS + 11)

        def second_sp(sp):
            u = FIRST_UNIT["in2"]
            for c, n0 in enumerate(CHUNKS2):
                for j in range(2):
                    n = u + 2 * c + j
                    load_unit(sp, n, [(raw_unit(n % SLOTS)[:, k:k + 2, :], src)
                                      for k, src in halves_of("w_in_2", 4 * j, n0)])
            load_linear(sp, "out2", "w_out_2", 0, (0, 4), 2)
            for t in range(TT):
                sp.wait_ge(sem("final"), t + 1)
                sp.dma_start(out[0, t * P:(t + 1) * P, :], xn[:, t, :]).then_inc(sem("stored"), 16)
            sp.wait_ge(sem("stored"), 16 * TT)

        def pair_banks(c):
            b = 2 * (c % 2)
            return (b, b + 1)

        def second_pe(pe):
            norm_pe(pe, 6, False, TT)
            u = FIRST_UNIT["in2"]
            for c in range(NT):
                if c >= 2:
                    pe.wait_ge(sem("in2_out"), c - 1)
                turned_chunk(pe, u + 2 * c, pair_banks(c), ("hT", KD * 6) if c == 0 else None)
            for i in range(TICKS):
                c, j = NT + i // 2, i % 2
                if j == 0:
                    pe.wait_ge(sem("in2_out"), c - 1)
                hi, lo = use_unit(pe, u + 2 * NT + i)
                for kk in range(4):
                    k = 4 * j + kk
                    for t in range(TT):
                        to = psum[:, pair_banks(c)[t], :]
                        a, b = hT_hi[:, k, t * P:(t + 1) * P], hT_lo[:, k, t * P:(t + 1) * P]
                        pe.matmul(to, a, hi[:, kk, :], start=k == 0, stop=False)
                        pe.matmul(to, a, lo[:, kk, :], start=False, stop=False)
                        m = pe.matmul(to, b, hi[:, kk, :], start=False, stop=k == KD - 1)
                m.then_inc(sem("unit_used"), 1)
                second_pe_tick(pe, i)
            for half in range(2):
                pe.wait_ge(sem("m"), half + 1)
                for k in range(4 * half, 4 * half + 4):
                    for t in range(TT):
                        a = (k % 2) * SEQ + t * P
                        m = pe.transpose(psum[:, 4 + k // 2, a:a + P], out_a[:, t, k * P:(k + 1) * P], ident)
                    m.then_inc(sem("m_turned"), 1)
            pe.wait_ge(sem("in2_out"), len(CHUNKS2))
            for n in range(2):
                linear_chunk(pe, FIRST_UNIT["out2"] + 2 * n, (0, 4), mT_hi, mT_lo, (2 * n, 2 * n + 1),
                             ("mT", 0) if n == 0 else None)

        def second_pe_tick(pe, i):
            s = i - 1
            if 0 <= s < STEPS:
                level, half = divmod(s, 2)
                if level:
                    pe.wait_ge(sem("hg_pair"), 2 * (s - 1))
                else:
                    pe.wait_ge(sem("hg_k"), half + 1)
                if s >= 2:
                    pe.wait_ge(sem("hg_att"), s - 1)
                for hh in range(4):
                    h = 4 * half + hh
                    for t in range(TT):
                        ts = slice(t * P, (t + 1) * P)
                        a, b = (hg_pair, hg_pair) if level else (hg_k, hg_q)
                        at_ = (hh % 2) * SEQ + t * P
                        m = pe.matmul(psum[:, 4 + 2 * half + hh // 2, at_:at_ + P], a[:, h, ts], b[:, h, ts],
                                      start=True, stop=True)
                m.then_inc(sem("hg_products"), 1)
            if i == K_ROWS:
                pe.wait_ge(sem("hg_ke"), 1)
                pe.wait_ge(sem("hg_att"), STEPS)
                for n in range(HEADS * TT):
                    h, t = divmod(n, TT)
                    m = pe.transpose(psum[:, 4 + n // 4, n % 4 * P:(n % 4 + 1) * P], hg_k[:, h, t * P:(t + 1) * P], ident)
                    if n % 8 == 7:
                        m.then_inc(sem("hg_k_turned"), 1)
            if i in (STATES_12, STATE_3):
                for c in ((0, 1) if i == STATES_12 else (2,)):
                    t, rows = c // 2, slice(c % 2 * HG_C, (c % 2 + 1) * HG_C)
                    pe.wait_ge(sem("hg_k_rows"), 2)
                    if c == 2:
                        pe.wait_ge(sem("hg_s1"), 1)
                    for h in range(HEADS):
                        m = pe.matmul(psum[:, 4 + 2 * (c % 2) + h // 4, h % 4 * P:(h % 4 + 1) * P],
                                      hg_k_rows[rows, h * TT + t, :], hg_v[rows, t, h * P:(h + 1) * P],
                                      start=True, stop=True)
                    m.then_inc(sem("hg_updates"), 1)
            if i == OUT_A:
                pe.wait_ge(sem("hg_qe"), 1)
                pe.wait_ge(sem("hg_s"), 2 * HEADS)
                for t in range(TT):
                    for h in range(HEADS):
                        bank = psum[:, 4 + 2 * t + h // 4, h % 4 * P:(h % 4 + 1) * P]
                        pe.matmul(bank, hg_att[:, h * TT + t, :], hg_v[:, t, h * P:(h + 1) * P], start=True, stop=False,
                                  skip_group_check=True)
                        for c in ((1,) if t == 0 else (2, 3)):
                            rows = slice(c % 2 * HG_C, (c % 2 + 1) * HG_C)
                            m = pe.matmul(bank[rows, :], hg_q[:, h, c * HG_C:(c + 1) * HG_C], hg_s[c - 1][:, h, :],
                                          start=False, stop=True, skip_group_check=True)
                    m.then_inc(sem("out_a_ready"), 1)
            if i == RET_TURN:
                pe.wait_ge(sem("out_a"), TT)
                pe.wait_ge(sem("ret_rotated"), 4)
                for j in range(RH // 2):
                    for a in range(2):
                        for t in range(TT):
                            at_ = a * SEQ + t * P
                            m = pe.transpose(psum[:, 4 + j, at_:at_ + P], ret_qk[:, t, a, j * P:(j + 1) * P], ident)
                    m.then_inc(sem("ret_turned"), 1)
            if i == RET_SCORES:
                pe.wait_ge(sem("ret_T"), 4)
                for n in range(RH * TT):
                    j, odd, t = n // 4, n // 2 % 2, n % 2
                    rows, ts = slice(odd * RDK, (odd + 1) * RDK), slice(t * P, (t + 1) * P)
                    at_ = j % 2 * SEQ + t * P
                    m = pe.matmul(psum[:, 4 + 2 * odd + j // 2, at_:at_ + P], ret_T[rows, j, 1, ts],
                                  ret_T[rows, j, 0, ts], start=True, stop=True)
                m.then_inc(sem("ret_scores"), 1)
            if i == RET_STATE:
                pe.wait_ge(sem("ret_att"), 4)
                pe.wait_ge(sem("ret_k_end"), 1)
                for h in range(RH):
                    rows = slice(h % 2 * RDK, (h % 2 + 1) * RDK)
                    m = pe.matmul(psum[rows, 4, h // 2 * P:(h // 2 + 1) * P], ret_k_end[:, h, :],
                                  ret_v[:, 0, h * P:(h + 1) * P], start=True, stop=True)
                m.then_inc(sem("ret_state_ready"), 1)
            if i == OUT_B:
                pe.wait_ge(sem("ret_state"), 1)
                pe.wait_ge(sem("ret_q_cross"), 1)
                for t in range(TT):
                    for h in range(RH):
                        rows = slice(h % 2 * RDK, (h % 2 + 1) * RDK)
                        bank = psum[:, 4 + 2 * t + h % 2, h // 2 * P:(h // 2 + 1) * P]
                        m = pe.matmul(bank, ret_att[:, h * TT + t, :], ret_v[:, t, h * P:(h + 1) * P],
                                      start=True, stop=t == 0)
                        if t:
                            m = pe.matmul(bank, ret_q_cross[rows, h // 2, :], ret_state[rows, h // 2, :],
                                          start=False, stop=True)
                    m.then_inc(sem("out_b_ready"), 1)

        def second_loads(act):
            act.dma_start(const2[:, :], w["second_constants"]).then_inc(sem("const2_in"), 16)
            act.dma_start(gain_row[:, :], w["hg_norm_g_2"][0].partition_broadcast(P)).then_inc(sem("gain_a_in"), 16)

        def blocks_of(ap, size):
            return ap.rearrange("p h (n b) -> p (h n) b", b=size)

        def second_act(act):
            norm_act(act, 6, None, False, FIRST_UNIT["in2"] - 1 + SLOTS)
            for k in range(KD):
                act.wait_ge(sem("h_tmp"), k + 1)
                act.activation(hT_hi[:, k, :], h_tmp[:, k, :], ACT.Copy).then_inc(sem("hT_hi"), 1)
            act.wait_ge(sem("lb_diff"), 2)
            act.activation(lb_e[:, :, :], lb_e[:, :, :], ACT.Exp).then_inc(sem("lb_e"), 1)
            u = FIRST_UNIT["in2"]

            def leave(c):
                act.wait_ge(sem("unit_used"), u + 2 * c + 2)
                n0, b = CHUNKS2[c], pair_banks(c)[0]
                src = psum[:, b:b + 2, :]
                cs = slice(n0 % D, n0 % D + 512)
                if c < NT:
                    hs = slice(4 * (c % 2), 4 * (c % 2) + 4)
                    to = hg_q if c < 2 else hg_k
                    act.activation(to[:, hs, :], src.rearrange("p b (h n) -> p (b h) n", h=2),
                                   ACT.Silu if c < 2 else ACT.Sigmoid).then_inc(sem("in2_out"), 1)
                elif n0 < HG_Z:
                    act.activation(hg_v[:, :, cs], src, ACT.Copy).then_inc(sem("in2_out"), 1)
                elif n0 < RQ:
                    act.activation(gate_a[:, :, cs], src, ACT.Silu).then_inc(sem("in2_out"), 1)
                elif n0 < RV:
                    act.activation(ret_qk[:, :, (n0 - RQ) // 512, :], src, ACT.Copy).then_inc(sem("in2_out"), 1)
                elif n0 < RZ:
                    act.activation(ret_v[:, :, cs], src, ACT.Copy).then_inc(sem("in2_out"), 1)
                elif n0 < GA:
                    act.wait_ge(sem("out_a_ready"), TT)
                    act.activation(gate_b[:, :, cs], src, ACT.Silu).then_inc(sem("in2_out"), 1)
                else:
                    n = 2 * (n0 >= GB) + (n0 % D) // 512
                    if n:
                        act.wait_ge(sem("gated"), n)
                    act.activation(sig[:, :, :], src, ACT.Sigmoid).then_inc(sem("in2_out"), 1)

            for c in range(NT):
                split_hi(act, u + 2 * c + SLOTS)
                leave(c)
                split_hi(act, u + 2 * c + 1 + SLOTS)
            for half in range(2):
                act.wait_ge(sem("hg_f"), 4 * half + 4)
                act.wait_ge(sem("hg_k"), half + 1)
                hs = slice(4 * half, 4 * half + 4)
                act.activation(hg_b[:, hs, :], hg_b[:, hs, :], ACT.Ln).then_inc(sem("hg_log"), 1)
            for i in range(TICKS):
                second_act_tick(act, i)
                split_hi(act, u + 2 * NT + i + SLOTS)
                if i % 2:
                    leave(NT + i // 2)
            for k in range(KD):
                act.wait_ge(sem("m_turned"), (k | 1) + 1)
                act.activation(mT_hi[:, k, :], psum[:, 4 + k // 2, (k % 2) * SEQ:(k % 2 + 1) * SEQ], ACT.Copy)\
                   .then_inc(sem("mT_hi"), 1)
            split_hi(act, FIRST_UNIT["out2"] + SLOTS)
            squares(act, 7)

        def second_act_tick(act, i):
            s = i - 1
            if 2 <= s < STEPS:
                hs = slice(4 * (s % 2), 4 * (s % 2) + 4)
                act.wait_ge(sem("hg_diff"), 2 * (s - 1))
                act.activation(hg_exp[:, hs, :], hg_exp[:, hs, :], ACT.Exp).then_inc(sem("hg_exp"), 1)
            if i == STEPS + 1:
                act.wait_ge(sem("hg_pair"), 2 * (STEPS - 2))
                act.activation(hg_exp[:, :, :], hg_b[:, :, :], ACT.Exp).then_inc(sem("hg_exp_b"), 1)
                act.activation(hg_last[:, :, :], blocks_of(hg_b[:, :, :], HG_C)[:, :, HG_C - 1].rearrange(
                    "p (h c) -> p h c", h=HEADS), ACT.Exp).then_inc(sem("hg_last"), 1)
            if i == STEPS + 2:
                act.wait_ge(sem("hg_end_diff"), 1)
                act.activation(hg_exp[:, :, :], hg_exp[:, :, :], ACT.Exp).then_inc(sem("hg_exp_end"), 1)
            if i == K_ROWS + 1:
                for b in range(2):
                    act.wait_ge(sem("hg_k_turned"), b + 1)
                    act.activation(hg_k_rows[:, 8 * b:8 * b + 8, :],
                                   psum[:, 4 + 2 * b:6 + 2 * b, :].rearrange("p b (n c) -> p (b n) c", c=P), ACT.Copy)\
                       .then_inc(sem("hg_k_rows"), 1)
            if i == STATES_12 + 1:
                act.wait_ge(sem("hg_updates"), 1)
                act.activation(hg_s[0][:, :, :], psum[:, 4:6, :].rearrange("p b (h e) -> p (b h) e", e=P), ACT.Copy)\
                   .then_inc(sem("hg_s1"), 1)
            if i == OUT_A + 1:
                for t in range(TT):
                    act.wait_ge(sem("out_a_ready"), t + 1)
                    act.activation(out_a[:, t, :].rearrange("p (b n) -> p b n", b=2), psum[:, 4 + 2 * t:6 + 2 * t, :],
                                   ACT.Copy).then_inc(sem("out_a"), 1)
                for t in range(TT):
                    act.wait_ge(sem("out_a"), TT)
                    act.activation(square_a[:, t, :], out_a[:, t, :], ACT.Square).then_inc(sem("square_a"), 1)
            if i == RET_TURN + 1:
                for j in range(4):
                    act.wait_ge(sem("ret_turned"), j + 1)
                    act.activation(ret_T[:, j, :, :], psum[:, 4 + j, :].rearrange("p (a n) -> p a n", a=2), ACT.Copy)\
                       .then_inc(sem("ret_T"), 1)
            if i == RET_STATE + 1:
                act.wait_ge(sem("ret_state_ready"), 1)
                act.activation(ret_state[:, :, :], psum[:, 4, :].rearrange("p (j e) -> p j e", e=P), ACT.Copy)\
                   .then_inc(sem("ret_state"), 1)
            if i == OUT_B + 1:
                act.wait_ge(sem("head_ss"), TT)
                for t in range(TT):
                    act.wait_ge(sem("out_b_ready"), t + 1)
                    act.activation(out_b[:, t, :].rearrange("p (j a e) -> p a j e", a=2, e=P),
                                   psum[:, 4 + 2 * t:6 + 2 * t, :].rearrange("p a (j e) -> p a j e", e=P), ACT.Copy).then_inc(sem("out_b"), 1)
                for t in range(TT):
                    act.wait_ge(sem("out_b"), TT)
                    act.activation(square_b[:, t, :], out_b[:, t, :], ACT.Square).then_inc(sem("square_b"), 1)

        def second_pool(pool):
            norm_pool(pool, 6)
            pool.memset(hg_att[:, :, :], 0.0).then_inc(sem("att_clear"), 1)
            for s in range(2, STEPS):
                level, half = divmod(s, 2)
                size, hs = 2 ** level, slice(4 * half, 4 * half + 4)
                mid = size // 2
                b, e = blocks_of(hg_b[:, hs, :], size), blocks_of(hg_exp[:, hs, :], size)
                ref = b[:, :, mid - 1:mid].broadcast_to([P, 4 * SEQ // size, mid])
                pool.wait_ge(sem("hg_b"), 4 * half + 4)
                if s >= 4:
                    pool.wait_ge(sem("hg_pair"), 2 * (s - 3))
                pool.tensor_tensor(e[:, :, 0:mid], ref, b[:, :, 0:mid], ALU.subtract).then_inc(sem("hg_diff"), 1)
                pool.tensor_tensor(e[:, :, mid:size], b[:, :, mid:size], ref, ALU.subtract).then_inc(sem("hg_diff"), 1)
            pool.wait_ge(sem("hg_qe"), 1)
            b, e = blocks_of(hg_b[:, :, :], HG_C), blocks_of(hg_exp[:, :, :], HG_C)
            pool.tensor_tensor(e, b[:, :, HG_C - 1:HG_C].broadcast_to([P, HEADS * SEQ // HG_C, HG_C]), b, ALU.subtract)\
                .then_inc(sem("hg_end_diff"), 1)
            pool.wait_ge(sem("hg_att"), STEPS)
            pool.wait_ge(sem("in2_out"), NT + 4)
            order = in_order(pool, "gpsimd_order")
            for a in range(2):
                for t in range(TT):
                    v = ret_qk[:, t, a, :].rearrange("p (h d) -> p h d", d=RDK)
                    one, two = v[:, :, 0:RHALF], v[:, :, RHALF:RDK]
                    cos, sin = (c2(n)[:, t * RHALF:(t + 1) * RHALF].unsqueeze(1).broadcast_to([P, RH, RHALF])
                                for n in ("cos", "sin"))
                    order(pool.tensor_tensor(rot[:, 0, :, :], one, cos, ALU.mult),
                          pool.tensor_tensor(rot[:, 1, :, :], two, sin, ALU.mult),
                          pool.tensor_tensor(rot[:, 2, :, :], one, sin, ALU.mult))
                    order(pool.tensor_tensor(one, rot[:, 0, :, :], rot[:, 1, :, :], ALU.subtract))
                    order(pool.tensor_tensor(rot[:, 0, :, :], two, cos, ALU.mult))
                    pool.tensor_tensor(two, rot[:, 0, :, :], rot[:, 2, :, :], ALU.add).then_inc(sem("ret_rotated"), 1)
                    pool.wait_ge(sem("ret_rotated"), 2 * a + t + 1)
            pool.wait_ge(sem("gain_a_in"), 16)
            for h in range(2):
                cs = slice(512 * h, 512 * (h + 1))
                pool.wait_ge(sem("gated"), h + 1)
                pool.tensor_tensor(gate_a[:, :, cs], gate_a[:, :, cs], across_tokens(gain_row[:, cs]), ALU.mult)\
                    .then_inc(sem("gained"), 1)
            pool.wait_ge(sem("out_a_ready"), TT)
            pool.tensor_tensor(ret_k_end[:, :, :], ret_qk[:, 0, 1, :].rearrange("p (h d) -> p h d", d=RDK),
                               c2("zeta").unsqueeze(2).broadcast_to([P, RH, RDK]), ALU.mult)\
                .then_inc(sem("ret_k_end"), 1)
            pool.wait_ge(sem("ret_T"), 4)
            pool.tensor_tensor(ret_q_cross[:, :, :], ret_T[:, :, 0, P:SEQ], c2("xi").rearrange("p (j t) -> p j t", t=P),
                               ALU.mult).then_inc(sem("ret_q_cross"), 1)
            head_rstd_pool(pool, 0)
            pool.wait_ge(sem("gained"), 2)
            pool.dma_start(gain_row[:, :], w["ret_norm_g_2"][0].partition_broadcast(P)).then_inc(sem("gain_b_in"), 16)
            pool.wait_ge(sem("gain_b_in"), 16)
            pool.wait_ge(sem("in2_out"), NT + 12)
            for h in range(2):
                cs = slice(512 * h, 512 * (h + 1))
                pool.tensor_tensor(gate_b[:, :, cs], gate_b[:, :, cs], across_tokens(gain_row[:, cs]), ALU.mult)\
                    .then_inc(sem("gained"), 1)
            head_rstd_pool(pool, 1)
            pool.wait_ge(sem("gained"), 4)
            pool.dma_start(gain_row[:, :], w["final_g_2"][0].partition_broadcast(P)).then_inc(sem("final_gain_in"), 16)
            norm_pool(pool, 7)

        def across_tokens(row):
            return row.unsqueeze(1).broadcast_to([P, TT, row.shape[1]])

        def head_rstd_pool(pool, a):
            pool.wait_ge(sem("head_ss"), TT * (a + 1))
            pool.tensor_scalar(head_ms[:, a, :], head_ss[:, a, :], 1.0 / HD, EPS, ALU.mult, ALU.add)\
                .then_inc(sem("head_ms"), 1)
            pool.wait_ge(sem("head_ms"), a + 1)
            pool.tensor_tensor(head_rstd[:, a, :], head_ms[:, a, :], neg_half[:, 0:TT * HEADS], ALU.pow)\
                .then_inc(sem("head_rstd"), 1)

        def second_dve(dve):
            l0, l1 = col("hg_lb_logits_2", 0, HEADS), col("hg_lb_logits_2", HEADS, HEADS)
            order = in_order(dve, "vector_order")
            order(dve.tensor_tensor(lb_top[:, :], l0, l1, ALU.max))
            for n, l in enumerate((l0, l1)):
                dve.tensor_tensor(lb_e[:, n, :], l, lb_top[:, :], ALU.subtract).then_inc(sem("lb_diff"), 1)
            norm_dve(dve, 6, None, False, FIRST_UNIT["in2"] - 1 + SLOTS)
            for k in range(KD):
                dve.wait_ge(sem("xT"), 6 * KD + (k | 1) + 1)
                if k == 0:
                    dve.wait_ge(sem("gain2"), 1)
                dve.tensor_scalar(h_tmp[:, k, :], turned_x(k),
                                  gain2[:, k:k + 1], mod_cols[:, k:k + 1], ALU.mult, ALU.add).then_inc(sem("h_tmp"), 1)
                if k:
                    second_dve_lo(dve, k - 1)
            second_dve_lo(dve, KD - 1)
            dve.wait_ge(sem("lb_e"), 1)
            order(dve.tensor_tensor(lb_top[:, :], lb_e[:, 0, :], lb_e[:, 1, :], ALU.add))
            order(dve.reciprocal(lb_rest[:, :], lb_top[:, :]))
            order(dve.tensor_tensor(lb[:, :], lb_e[:, 0, :], lb_rest[:, :], ALU.mult))
            order(dve.tensor_scalar(lb_rest[:, :], lb[:, :], -1.0, 1.0, ALU.mult, ALU.add))
            u = FIRST_UNIT["in2"]
            for c in range(NT):
                split_lo(dve, u + 2 * c + SLOTS)
                split_lo(dve, u + 2 * c + 1 + SLOTS)
                if c >= 2:
                    half = c - 2
                    dve.wait_ge(sem("in2_out"), c + 1)
                    for h in range(4 * half, 4 * half + 4):
                        dve.tensor_scalar(hg_b[:, h, :], hg_k[:, h, :], lb_rest[:, h:h + 1], lb[:, h:h + 1],
                                          ALU.mult, ALU.add).then_inc(sem("hg_f"), 1)
                    dve.wait_ge(sem("hg_f"), 4 * half + 4)
                    hs = slice(4 * half, 4 * half + 4)
                    dve.tensor_scalar(hg_k[:, hs, :], hg_b[:, hs, :], -1.0, 1.0, ALU.mult, ALU.add)\
                       .then_inc(sem("hg_k"), 1)
            dve.wait_ge(sem("const2_in"), 16)
            dve.wait_ge(sem("att_clear"), 1)
            for half in range(2):
                dve.wait_ge(sem("hg_log"), half + 1)
                for h in range(4 * half, 4 * half + 4):
                    dve.tensor_tensor_scan(hg_b[:, h, :], c2("keep"), hg_b[:, h, :], 0.0, ALU.mult, ALU.add)\
                       .then_inc(sem("hg_b"), 1)
            for i in range(TICKS):
                second_dve_tick(dve, i)
                split_lo(dve, u + 2 * NT + i + SLOTS)
                c = NT + i // 2
                if i % 2 and GA <= CHUNKS2[c] < GB:
                    gate(dve, c)
            for half in range(2):
                c = len(CHUNKS2) - 2 + half
                mix(dve, c, half)
            for k in range(KD):
                dve.wait_ge(sem("mT_hi"), (k | 1) + 1)
                dve.tensor_tensor(mT_lo[:, k, :], psum[:, 4 + k // 2, (k % 2) * SEQ:(k % 2 + 1) * SEQ],
                                  mT_hi[:, k, :].bitcast(F32), ALU.subtract).then_inc(sem("mT"), 1)
            split_lo(dve, FIRST_UNIT["out2"] + SLOTS)
            for h in range(2):
                cs = slice(512 * h, 512 * (h + 1))
                dve.wait_ge(sem("unit_used"), FIRST_UNIT["out2"] + 2 * h + 2)
                dve.tensor_tensor(scaled[:, :, cs], psum[:, 2 * h:2 * h + 2, :], across_tokens(gate2[:, cs]), ALU.mult)\
                   .then_inc(sem("scaled"), 1)
                dve.wait_ge(sem("scaled"), h + 1)
                for t in range(TT):
                    dve.tensor_tensor(x[:, t, cs], scaled[:, t, cs], x[:, t, cs], ALU.add).then_inc(sem("x_added"), 1)
            dve.wait_ge(sem("final_gain_in"), 16)
            dve.wait_ge(sem("rstd"), 8)
            for t in range(TT):
                dve.scalar_tensor_tensor(xn[:, t, :], x[:, t, :], rstd[:, t:t + 1], gain_row[:, :], ALU.mult, ALU.mult)\
                   .then_inc(sem("final"), 1)

        def second_dve_lo(dve, k):
            dve.wait_ge(sem("hT_hi"), 6 * KD + k + 1)
            dve.tensor_tensor(hT_lo[:, k, :], h_tmp[:, k, :], hT_hi[:, k, :].bitcast(F32), ALU.subtract)\
               .then_inc(sem("hT"), 1)

        def gate(dve, c):
            n = 2 * (CHUNKS2[c] >= GB) + CHUNKS2[c] % D // 512
            to = (gate_b if n >= 2 else gate_a)[:, :, 512 * (n % 2):512 * (n % 2 + 1)]
            dve.wait_ge(sem("in2_out"), c + 1)
            if n >= 2:
                dve.wait_ge(sem("gained"), n + 1)
            dve.tensor_tensor(to, to, sig[:, :, :], ALU.mult).then_inc(sem("gated"), 1)

        def mix(dve, c, half):
            cs = slice(512 * half, 512 * (half + 1))
            gate(dve, c)
            order = in_order(dve, "vector_order")
            dve.wait_ge(sem("gated"), 3 + half)
            b = out_b[:, :, cs]
            order(dve.tensor_tensor(b, b, gate_b[:, :, cs], ALU.mult))
            dve.tensor_tensor(out_a[:, :, cs], out_a[:, :, cs], b, ALU.add).then_inc(sem("m"), 1)

        def normed(dve, a, buf, other):
            dve.wait_ge(sem("head_rstd"), a + 1)
            for h in range(2):
                cs = slice(512 * h, 512 * (h + 1))
                v = buf[:, :, cs].rearrange("p t (h d) -> p t h d", d=HD)
                r_ = head_rstd[:, a, :].rearrange("p (t h) -> p t h", t=TT)[:, :, 4 * h:4 * h + 4]
                dve.tensor_tensor(v, v, r_.unsqueeze(3).broadcast_to([P, TT, 4, HD]), ALU.mult)\
                   .then_inc(sem(f"normed_{a}"), 1)
            dve.wait_ge(sem(f"normed_{a}"), 2)
            if other is not None:
                dve.wait_ge(sem("gained"), 2)
                dve.tensor_tensor(buf[:, :, :], buf[:, :, :], other[:, :, :], ALU.mult).then_inc(sem("a_gated"), 1)
                dve.wait_ge(sem("a_gated"), 1)

        def head_squares(dve, a, squares):
            for t in range(TT):
                dve.wait_ge(sem("square_" + "ab"[a]), t + 1)
                dve.tensor_reduce(head_ss[:, a, t * HEADS:(t + 1) * HEADS],
                                  squares[:, t, :].rearrange("p (h d) -> p h d", d=HD), X_AXIS, ALU.add)\
                   .then_inc(sem("head_ss"), 1)

        def second_dve_tick(dve, i):
            s = i - 1
            if 2 <= s < STEPS:
                level, half = divmod(s, 2)
                size, hs = 2 ** level, slice(4 * half, 4 * half + 4)
                mid = size // 2
                e, k, q, to = (blocks_of(v[:, hs, :], size) for v in (hg_exp, hg_k, hg_q, hg_pair))
                dve.wait_ge(sem("hg_exp"), s - 1)
                if s >= 4:
                    dve.wait_ge(sem("hg_products"), s - 1)
                dve.tensor_tensor(to[:, :, 0:mid], k[:, :, 0:mid], e[:, :, 0:mid], ALU.mult).then_inc(sem("hg_pair"), 1)
                dve.tensor_tensor(to[:, :, mid:size], q[:, :, mid:size], e[:, :, mid:size], ALU.mult)\
                   .then_inc(sem("hg_pair"), 1)
            s = i - 2
            if 0 <= s < STEPS:
                level, half = divmod(s, 2)
                mask = c2("levels")[:, level * P:(level + 1) * P].bitcast(U32).unsqueeze(1).broadcast_to([P, 8, P])
                dve.wait_ge(sem("hg_products"), s + 1)
                if level:
                    dve.wait_ge(sem("hg_att"), s - 1)
                dve.copy_predicated(hg_att[:, 8 * half:8 * half + 8, :], mask,
                                    psum[:, 4 + 2 * half:6 + 2 * half, :].rearrange("p b (n t) -> p (b n) t", t=P))\
                   .then_inc(sem("hg_att"), 1)
            if i == STEPS + 1:
                dve.wait_ge(sem("hg_exp_b"), 1)
                dve.tensor_tensor(hg_q[:, :, :], hg_q[:, :, :], hg_exp[:, :, :], ALU.mult).then_inc(sem("hg_qe"), 1)
            if i == STEPS + 2:
                dve.wait_ge(sem("hg_exp_end"), 1)
                dve.tensor_tensor(hg_k[:, :, :], hg_k[:, :, :], hg_exp[:, :, :], ALU.mult).then_inc(sem("hg_ke"), 1)
            for c, tick in ((1, STATES_12 + 1), (2, STATE_3 + 1)):
                if i == tick:
                    dve.wait_ge(sem("hg_updates"), c + 1)
                    dve.wait_ge(sem("hg_s1"), 1)
                    dve.wait_ge(sem("hg_last"), 1)
                    if c == 2:
                        dve.wait_ge(sem("hg_s"), HEADS)
                    for h in range(HEADS):
                        dve.scalar_tensor_tensor(hg_s[c][:, h, :], hg_s[c - 1][:, h, :], hg_last[:, h, c:c + 1],
                                                 psum[:, 4 + 2 * (c % 2) + h // 4, h % 4 * P:(h % 4 + 1) * P],
                                                 ALU.mult, ALU.add).then_inc(sem("hg_s"), 1)
            if i == OUT_A + 1:
                head_squares(dve, 0, square_a)
            if i == RET_SCORES + 1:
                dve.wait_ge(sem("ret_scores"), 1)
                by_parity = ret_att[:, :, :].rearrange("p (j a t) l -> p a j t l", a=2, t=TT)
                decays = c2("decay").rearrange("p (j a t) -> p a j t", a=2, t=P)
                for b in range(4):
                    js = slice(2 * (b % 2), 2 * (b % 2) + 2)
                    dve.tensor_tensor(by_parity[:, b // 2, js, :, :],
                                      psum[:, 4 + b, :].rearrange("p (j t l) -> p j t l", j=2, t=TT),
                                      decays[:, b // 2, js, :].unsqueeze(2).broadcast_to([P, 2, TT, P]), ALU.mult)\
                       .then_inc(sem("ret_att"), 1)
            if i == RET_STATE + 1:
                normed(dve, 0, out_a, gate_a)
            if i == OUT_B + 1:
                head_squares(dve, 1, square_b)
            if i == OUT_B + 2:
                normed(dve, 1, out_b, None)

        block = ctx.enter_context(nc.Block())
        FFN1 = ("ffn1_w_gate", "ffn1_w_up", "ffn1_w_down")
        FFN2 = ("ffn2_w_gate", "ffn2_w_up", "ffn2_w_down")

        @block.sync
        def _(sp):
            start_sp(sp)
            ffn_sp(sp, "ffn1_0", FFN1, 0)
            load_linear(sp, "qkv", "attn_w_qkv", 0, (0, 4), 6)
            load_linear(sp, "wo", "attn_w_o", 0, (0, 4), 2)
            ffn_sp(sp, "ffn2_0", FFN2, 0)
            ffn_sp(sp, "ffn1_1", FFN1, 1)
            ssm_sp(sp)
            ffn_sp(sp, "ffn2_1", FFN2, 1)
            second_sp(sp)

        @block.gpsimd
        def _(pool):
            start_pool(pool)
            norm_pool(pool, 0)
            ada_pool(pool)
            attn_pool(pool)
            norm_pool(pool, 2)
            norm_pool(pool, 3)
            ssm_pool(pool)
            norm_pool(pool, 5)
            second_pool(pool)

        @block.scalar
        def _(act):
            start_act(act)
            split_hi(act, 1)
            split_hi(act, 2)
            norm_act(act, 0, ("ffn1_norm", 0), True)
            trig_act(act)
            ffn_act(act, "ffn1_0", 0)
            attn_act(act)
            norm_act(act, 2, ("ffn2_norm", 0), True, FIRST_UNIT["ffn2_0"] - 1 + SLOTS)
            ffn_act(act, "ffn2_0", 2)
            norm_act(act, 3, ("ffn1_norm", KD), True, FIRST_UNIT["ffn1_1"] - 1 + SLOTS)
            ffn_act(act, "ffn1_1", 3)
            ssm_act(act)
            norm_act(act, 5, ("ffn2_norm", KD), True, FIRST_UNIT["ffn2_1"] - 1 + SLOTS)
            second_loads(act)
            ffn_act(act, "ffn2_1", 5)
            second_act(act)

        @block.vector
        def _(dve):
            start_dve(dve)
            split_lo(dve, 1)
            split_lo(dve, 2)
            norm_dve(dve, 0, ("ffn1_norm", 0), True)
            trig_dve(dve)
            ffn_dve(dve, "ffn1_0", ada_dve)
            attn_dve(dve)
            norm_dve(dve, 2, ("ffn2_norm", 0), True, FIRST_UNIT["ffn2_0"] - 1 + SLOTS)
            ffn_dve(dve, "ffn2_0")
            norm_dve(dve, 3, ("ffn1_norm", KD), True, FIRST_UNIT["ffn1_1"] - 1 + SLOTS)
            ffn_dve(dve, "ffn1_1")
            ssm_dve(dve)
            norm_dve(dve, 5, ("ffn2_norm", KD), True, FIRST_UNIT["ffn2_1"] - 1 + SLOTS)
            ffn_dve(dve, "ffn2_1")
            second_dve(dve)

        @block.tensor
        def _(pe):
            start_pe(pe)
            norm_pe(pe, 0, True)
            ffn_pe(pe, "ffn1_0", 0, ada_pe)
            attn_pe(pe)
            norm_pe(pe, 2, True)
            ffn_pe(pe, "ffn2_0", 2)
            norm_pe(pe, 3, True)
            ffn_pe(pe, "ffn1_1", 3)
            ssm_pe(pe)
            norm_pe(pe, 5, True)
            ffn_pe(pe, "ffn2_1", 5)
            second_pe(pe)


INPUTS = ["x", "positions", "ffn1_norm", "ffn1_w_gate", "ffn1_w_up", "ffn1_w_down", "mix_norm", "ffn2_norm",
          "ffn2_w_gate", "ffn2_w_up", "ffn2_w_down", "attn_w_qkv", "attn_q_norm", "attn_k_norm", "attn_w_o",
          "ssm_w_in", "ssm_conv_w", "ssm_conv_b", "ssm_dt_bias", "ssm_a_log", "ssm_d", "ssm_norm", "ssm_w_out", "c_2",
          "norm_g_2", "w_ada_2", "b_ada_2", "w_in_2", "hg_lb_logits_2", "hg_norm_g_2", "ret_norm_g_2", "w_out_2",
          "final_g_2"]


def kernel(**inputs):
    from concourse import bacc
    from concourse.bass_utils import run_bass_kernel_spmd

    nc = bacc.Bacc("TRN2", target_bir_lowering=False, num_devices=1)
    arrays = {name: np.ascontiguousarray(inputs[name]) for name in INPUTS}
    arrays["final_g_2"] = arrays["final_g_2"].reshape(1, D)
    arrays["first_constants"] = first_constants()
    arrays["second_constants"] = second_constants()
    w = {n: nc.dram_tensor(f"in_{n}", a.shape, mybir.dt.from_np(a.dtype), kind="ExternalInput").ap()
         for n, a in arrays.items()}
    out = nc.dram_tensor("out", (1, SEQ, D), F32, kind="ExternalOutput").ap()
    build(nc, w, out)
    result = run_bass_kernel_spmd(nc, [{f"in_{n}": a for n, a in arrays.items()}], core_ids=[0])
    return result.results[0]["out"]
```

```python
from contextlib import ExitStack

import numpy as np

import concourse.bass as bass
from concourse import mybir

F32 = mybir.dt.float32
R32 = mybir.dt.float32r
I32 = mybir.dt.int32
U32 = mybir.dt.uint32
ALU = mybir.AluOpType
ACT = mybir.ActivationFunctionType
X_AXIS = mybir.AxisListType.X

P = 128
SEQ = 256
TT = SEQ // P
D = 1024
KD = D // P
FF = 2816
FC = 256
NFC = FF // FC
EPS = 1e-6

HEADS = 8
HD = 128
SCALE = HD ** -0.5
HALF = HD // 2
MASKED = -1e30

DI = 2048
GROUPS = 8
SH = 32
HPG = SH // GROUPS
SP = DI // SH
NB = GROUPS * 128
CONVD = DI + 2 * NB
TAPS = 4
GW = DI // GROUPS
KI = DI // P

HG_C = 64
LEVELS = 6
RH = 8
RDK = 64
RHALF = RDK // 2

SLOTS = 3
UNIT = 4 * 512
PARTS = 2

TWO_PI_HI = 6.28125
TWO_PI_MID = float(np.round((2 * np.pi - TWO_PI_HI) * 2 ** 20) / 2 ** 20)
TWO_PI_LO = float(2 * np.pi - TWO_PI_HI - TWO_PI_MID)
ROUND = 1.5 * 2.0 ** 23


def first_constants():
    i = np.arange(P)
    ident = np.eye(P)
    causal = np.where(i[None, :] <= i[:, None], 0.0, MASKED)
    runsum = (i[:, None] <= i[None, :]) * 1.0
    freq = np.broadcast_to(10000.0 ** (-np.arange(HALF) / HALF), (P, HALF))
    head = i[:, None]
    group_of_head = (head // HPG == np.arange(GROUPS)) * 1.0
    head_in_group = (head % HPG == np.arange(HPG)) * 1.0
    return np.concatenate([ident, causal, causal.T, runsum, np.ones((P, P)), freq, group_of_head, head_in_group],
                          1).astype(np.float32)


FIRST = {"ident": (0, P), "causal": (P, P), "causal_t": (2 * P, P), "runsum": (3 * P, P), "ones": (4 * P, P),
         "freq": (5 * P, HALF), "group_of_head": (5 * P + HALF, GROUPS), "head_in_group": (5 * P + HALF + GROUPS, HPG)}
FIRST_W = 5 * P + HALF + GROUPS + HPG


def second_constants():
    i = np.arange(P)
    s, t = i[:, None], i[None, :]
    masks = [s == t]
    for level in range(1, LEVELS + 1):
        b, h = 2 ** level, 2 ** (level - 1)
        masks.append((s // b == t // b) & (s % b < h) & (t % b >= h))
    masks = np.concatenate([m * 1.0 for m in masks], 1)
    gamma = np.log(1.0 - 2.0 ** (-5.0 - np.arange(RH)))
    rel = t - s
    decay = np.concatenate([np.where(rel >= 0, np.exp(g * np.maximum(rel, 0)), 0.0) * RDK ** -0.5 for g in gamma], 1)
    xi = np.concatenate([np.exp(gamma[2 * j + (i[:, None] >= RDK)] * (t + 1.0)) for j in range(RH // 2)], 1)
    zeta = np.exp(gamma[None, :] * (P - 1.0 - i[:, None])) * RDK ** -0.5
    inv = 1.0 / (10000.0 ** np.linspace(0.0, 1.0, RHALF))
    ang = np.arange(SEQ)[:, None] * inv.astype(np.float32).astype(np.float64)[None, :]
    cos = np.cos(ang).reshape(TT, P, RHALF).transpose(1, 0, 2).reshape(P, TT * RHALF)
    sin = np.sin(ang).reshape(TT, P, RHALF).transpose(1, 0, 2).reshape(P, TT * RHALF)
    keep = np.broadcast_to((np.arange(SEQ) % HG_C != 0) * 1.0, (P, SEQ))
    return np.concatenate([masks, decay, xi, zeta, cos, sin, keep], 1).astype(np.float32)


SECOND, _at = {}, 0
for _name, _w in (("levels", (LEVELS + 1) * P), ("decay", RH * P), ("xi", RH // 2 * P), ("zeta", RH),
                  ("cos", TT * RHALF), ("sin", TT * RHALF), ("keep", SEQ)):
    SECOND[_name] = (_at, _w)
    _at += _w
SECOND_W = _at

ROWS, _at = {}, 0
for _name, _n in (("ffn1_norm", 16), ("mix_norm", 16), ("ffn2_norm", 16), ("norm_g_2", 8), ("ssm_norm", 16),
                  ("ssm_conv_b", 32), ("c_2", 8), ("hg_lb_logits_2", 16)):
    ROWS[_name] = (_at, _n)
    _at += _n
assert _at == P


STAGES = [("ffn1_0", 3 * NFC), ("qkv", 12), ("wo", 4), ("ffn2_0", 3 * NFC), ("ffn1_1", 3 * NFC), ("ssm_xbc", 14),
          ("ssm_dt", 1), ("ssm_xbc_last", 2), ("ssm_z", 8), ("ssm_out", 8), ("ffn2_1", 3 * NFC), ("in2", 36),
          ("out2", 4)]
FFNS = ("ffn1_0", "ffn2_0", "ffn1_1", "ffn2_1")
FIRST_UNIT, UNITS = {}, 0
for _name, _n in STAGES:
    FIRST_UNIT[_name] = UNITS
    UNITS += _n


def place(unit, step=0, per=0):
    return unit + per * step, unit % SLOTS, unit // SLOTS + per // SLOTS * step


def build(nc, w, out):
    with ExitStack() as ctx:
        sems = {}

        def sem(name):
            if name not in sems:
                sems[name] = ctx.enter_context(nc.semaphore(name))
            return sems[name]

        counts = {}

        def in_order(engine, name):
            def order(*instructions):
                for i in instructions:
                    i.then_inc(sem(name), 1)
                counts[name] = counts.get(name, 0) + len(instructions)
                engine.wait_ge(sem(name), counts[name])
            return order

        top = [-(-nc.sbuf_base // 64) * 64]

        def at(offset, name, shape, dt=F32):
            t = nc.alloc_sbuf_tensor_at(name, shape, dt, offset=offset)
            size = int(np.prod(shape[1:])) * 4
            assert offset + size <= nc.sbuf_usable_end, (name, offset + size - nc.sbuf_usable_end)
            return t, offset + -(-size // 64) * 64

        def keep(name, shape, dt=F32):
            t, top[0] = at(top[0], name, shape, dt)
            return t

        def region(start):
            end = [start]

            def take(name, shape, dt=F32):
                t, end[0] = at(end[0], name, shape, dt)
                return t

            return take, end

        x = keep("x", [P, TT, D])
        hT_hi = keep("hT_hi", [P, KD, SEQ], R32)
        hT_lo = keep("hT_lo", [P, KD, SEQ], R32)
        raw = keep("raw", [P, SLOTS, UNIT])
        w_hi = keep("w_hi", [P, SLOTS, UNIT], R32)
        w_lo = keep("w_lo", [P, SLOTS, UNIT], R32)
        ffn_tiles = top[0]
        silu_g = keep("silu_g", [P, TT, FC])
        hid = keep("hid", [P, TT, FC])
        last_hidT_hi, _ = at(ffn_tiles, "last_hidT_hi", [P, 2, SEQ], R32)
        last_hidT_lo, _ = at(ffn_tiles + 4 * TT * FC, "last_hidT_lo", [P, 2, SEQ], R32)
        hidT_hi = keep("hidT_hi", [P, 2, SEQ], R32)
        hidT_lo = keep("hidT_lo", [P, 2, SEQ], R32)
        const1 = keep("const1", [P, FIRST_W])
        cols = keep("cols", [P, P])
        taps = keep("taps", [P, P])
        sumsq = keep("sumsq", [P, 2, TT])
        meansq = keep("meansq", [P, TT])
        rstd = keep("rstd", [P, TT])
        neg_half = keep("neg_half", [P, 2 * SH])
        gate2 = keep("gate2", [P, D])
        mod_cols = keep("mod_cols", [P, 16])
        gain2 = keep("gain2", [P, KD])
        silu_c = keep("silu_c", [P, KD])
        WORK = top[0]

        psum = ctx.enter_context(nc.psum_tensor("psum", [P, 8, 512], F32))

        def c1(name):
            a, n = FIRST[name]
            return const1[:, a:a + n]

        ident, ones = c1("ident"), c1("ones")

        def col(name, n, count=1):
            a = ROWS[name][0] + n
            return cols[:, a:a + count]

        start, start_end = region(WORK + 8192)
        rows_in = start("rows_in", [P, P])
        taps_in = start("taps_in", [P, P])
        pos_i = start("pos_i", [P, TT], I32)
        pos_f = start("pos_f", [P, TT])
        angle = start("angle", [P, 2, TT, HALF])
        turns = start("turns", [P, 2, TT, HALF])
        trig = start("trig", [P, 2, TT, HALF])
        ada_in = start("ada_in", [P, 2, 3 * D])
        ada_term = start("ada_term", [P, 3 * D])
        ada = start("ada", [P, 3 * D])
        b_ada = start("b_ada", [1, 3 * D])

        norm, norm_end = region(WORK)
        xn = norm("xn", [P, TT, D])

        SEEN = (slice(0, P), slice(P, 3 * P))
        r, r_end = region(WORK)
        oT_hi = (r("oT_hi", [P, 4, SEQ], R32), hT_hi[:, 4:8, :])
        oT_lo = (r("oT_lo", [P, 4, SEQ], R32), hT_lo[:, 4:8, :])
        r, r_end = region(WORK + 8192)
        late_start = (nc.sbuf_usable_end - 6 * 1024) // 64 * 64
        rope_c = {}
        late, late_end = region(late_start)
        for name in ("q", "k"):
            for part in ("cos1", "sin2", "cos2", "sin1"):
                rope_c[name, part] = late(f"{name}_{part}", [P, TT, HALF])
        gains = late("qk_gains", [P, 2, HD])
        qk = r("qk", [P, TT, 2 * D])
        v_sb = r("v_sb", [P, TT, D])
        qk_sq = r("qk_sq", [P, TT, 512])
        qk_ss = r("qk_ss", [P, TT, 2 * HEADS])
        qk_ms = r("qk_ms", [P, TT, 2 * HEADS])
        qk_rstd = r("qk_rstd", [P, TT, 2 * HEADS])
        rope_a = r("rope_a", [P, TT, 4, HALF])
        rope_b = r("rope_b", [P, TT, 4, HALF])
        rope_d = r("rope_d", [P, TT, 4, HALF])
        rope_e = r("rope_e", [P, TT, 4, HALF])
        qkT = r("qkT", [P, 2, 2, SEQ])
        prob = r("prob", [P, 2, 3 * P])
        probT = r("probT", [P, 2, 3 * P])
        top_s = r("top_s", [P, HEADS, TT])
        bias_s = r("bias_s", [P, HEADS, TT])
        sum_s = r("sum_s", [P, HEADS, TT])
        inv_s = r("inv_s", [P, HEADS, TT])
        assert max(r_end[0], start_end[0]) <= late_start

        r, r_end = region(WORK)
        conv = r("conv", [P, 2, 4, SEQ])
        r, r_end = region(WORK)
        decay = r("decay", [P, 2, HPG, P])
        within = r("within", [P, 2, HPG, P])
        z = r("z", [P, TT, DI])
        y = r("y", [P, TT, DI])
        r2, r2_end = region(r_end[0])
        xs = r("xs", [P, TT, DI])
        bcT = r("bcT", [P, 2 * GROUPS, SEQ])
        b_rows = r("b_rows", [P, GROUPS, P])
        yT_hi = r2("yT_hi", [P, KI, SEQ], R32)
        yT_lo = r2("yT_lo", [P, KI, SEQ], R32)
        r2, r2_end = region(r_end[0])
        xT = r("xT", [P, 2, 4, SEQ])
        xdt = r2("xdt", [P, 2, HPG, SP])
        x_decayed = r2("x_decayed", [P, HPG, SP])
        x_skip = r2("x_skip", [P, 2, HPG, SP])
        states = r2("states", [P, 2, GW])
        per_head = {n: r(n, [P, SH]) for n in ("dt_bias", "a_rate", "d_skip", "end_decay", "start_decay")}
        per_token = {n: r(n, [P, TT, SH]) for n in ("dt_raw", "dt_exp", "dt_a", "dt_b", "dt_s", "dt_p", "dt", "a_dt",
                                                    "a_sum")}
        group_r = r("group_r", [P, GROUPS], R32)
        sums_hi = r("sums_hi", [P, TT, HPG, P], R32)
        sums_lo = r("sums_lo", [P, TT, HPG, P], R32)
        y_ss = r("y_ss", [P, TT, GROUPS])
        y_ms = r("y_ms", [P, TT, GROUPS])
        y_rstd = r("y_rstd", [P, TT, GROUPS])
        assert r2_end[0] <= r_end[0]

        second = {}
        r, r_end = region(WORK)
        for zone in ("exp", "pair", "query", "key", "sum", "value", "ret_qk", "ret_v", "out_gate"):
            second[zone] = r_end[0]
            r_end[0] += 8192
        second["att"] = ffn_tiles

        def zoned(zone, name, shape, dt=F32, offset=0):
            return at(second[zone] + offset, name, shape, dt)[0]

        h_tmp = zoned("pair", "h_tmp", [P, KD, SEQ])
        hg_exp = zoned("exp", "hg_exp", [P, HEADS, SEQ])
        hg_pair = zoned("pair", "hg_pair", [P, HEADS, SEQ])
        hg_q = zoned("query", "hg_q", [P, HEADS, SEQ])
        hg_k = zoned("key", "hg_k", [P, HEADS, SEQ])
        hg_b = zoned("sum", "hg_b", [P, HEADS, SEQ])
        hg_v = zoned("value", "hg_v", [P, TT, D])
        hg_att = zoned("att", "hg_att", [P, HEADS * TT, P])
        hg_k_rows = zoned("pair", "hg_k_rows", [P, HEADS * TT, P])
        hg_s = [zoned("sum", "hg_s1", [P, HEADS, P]), zoned("sum", "hg_s2", [P, HEADS, P], offset=4096),
                zoned("exp", "hg_s3", [P, HEADS, P])]
        out_a = zoned("key", "out_a", [P, TT, D])
        square_a = zoned("exp", "square_a", [P, TT, D])
        ret_qk = zoned("ret_qk", "ret_qk", [P, TT, 2, D // 2])
        ret_v = zoned("ret_v", "ret_v", [P, TT, D])
        ret_T = zoned("pair", "ret_T", [P, RH // 2, 2, SEQ])
        ret_q_cross = zoned("att", "ret_q_cross", [P, RH // 2, P])
        ret_k_end = zoned("att", "ret_k_end", [P, RH, RDK], offset=2048)
        ret_state = zoned("att", "ret_state", [P, RH // 2, P], offset=4096)
        ret_att = zoned("sum", "ret_att", [P, RH * TT, P])
        out_b = zoned("exp", "out_b", [P, TT, D])
        square_b = zoned("sum", "square_b", [P, TT, D])
        gate_a = zoned("out_gate", "gate_a", [P, TT, D])
        gate_b = zoned("query", "gate_b", [P, TT, D])
        mT_hi = zoned("pair", "mT_hi", [P, KD, SEQ], R32)
        mT_lo = zoned("value", "mT_lo", [P, KD, SEQ], R32)
        scaled = zoned("key", "scaled", [P, TT, D])
        const2_at = r_end[0]
        const2 = r("const2", [P, SECOND_W])
        rot = at(const2_at, "rot", [P, 3, RH, RHALF])[0]
        gain_row = r("gain_row", [P, D])
        sig = r("sig", [P, TT, 512])
        lb = r("lb", [P, HEADS])
        lb_rest = r("lb_rest", [P, HEADS])
        lb_top = r("lb_top", [P, HEADS])
        lb_e = r("lb_e", [P, 2, HEADS])
        hg_last = r("hg_last", [P, HEADS, SEQ // HG_C])
        head_ss = r("head_ss", [P, 2, TT * HEADS])
        head_ms = r("head_ms", [P, 2, TT * HEADS])
        head_rstd = r("head_rstd", [P, 2, TT * HEADS])

        def c2(name):
            a, n = SECOND[name]
            return const2[:, a:a + n]

        def halves_of(name, k0, n0, width=512):
            src = w[name][0].rearrange("(k p) n -> p k n", p=P)
            return [(k, src[:, k0 + k:k0 + k + 2, n0:n0 + width]) for k in (0, 2)]

        def load_unit(sp, unit, halves, step=0, per=0):
            n, slot, turn = place(unit, step, per)
            if unit >= SLOTS:
                sp.wait_ge(sem("lo_ready"), n - (SLOTS - 1))
            for dst, src in halves:
                sp.dma_start(dst, src).then_inc(sem(f"landed_{slot}"), 16)

        def split_hi(act, unit, step=0, per=0):
            if unit >= UNITS:
                return
            n, slot, turn = place(unit, step, per)
            act.wait_ge(sem(f"landed_{slot}"), 16 * PARTS * (turn + 1))
            if unit >= SLOTS:
                act.wait_ge(sem("unit_used"), n - (SLOTS - 1))
            act.activation(w_hi[:, slot, :], raw[:, slot, :], ACT.Copy).then_inc(sem("hi_ready"), 1)

        def split_lo(dve, unit, step=0, per=0):
            if unit >= UNITS:
                return
            n, slot, _ = place(unit, step, per)
            dve.wait_ge(sem("hi_ready"), n + 1)
            dve.tensor_tensor(w_lo[:, slot, :], raw[:, slot, :], w_hi[:, slot, :].bitcast(F32), ALU.subtract)\
               .then_inc(sem("lo_ready"), 1)

        def raw_unit(slot):
            return raw[:, slot, :].rearrange("p (k n) -> p k n", k=4)

        def load_linear(sp, stage, name, n0, k0s, chunks):
            u = FIRST_UNIT[stage]
            for c in range(chunks):
                for k0 in k0s:
                    slot = u % SLOTS
                    load_unit(sp, u, [(raw_unit(slot)[:, k:k + 2, :], src)
                                      for k, src in halves_of(name, k0, n0 + 512 * c)])
                    u += 1

        def use_unit(pe, unit, step=0, per=0):
            n, slot, _ = place(unit, step, per)
            pe.wait_ge(sem("lo_ready"), n + 1)
            return (w_hi[:, slot, :].rearrange("p (k n) -> p k n", k=4),
                    w_lo[:, slot, :].rearrange("p (k n) -> p k n", k=4))

        def pair_banks(c):
            b = 2 * (c % 2)
            return (b, b + 1)

        def linear_unit(pe, unit, k0, tiles, a_hi, a_lo, banks, ready=None):
            hi, lo = use_unit(pe, unit)
            for kk in range(4):
                k = k0 + kk
                if ready:
                    pe.wait_ge(sem(ready[0]), ready[1] + k + 1)
                for t in range(TT):
                    to = psum[:, banks[t], :]
                    a, b = a_hi[:, k, t * P:(t + 1) * P], a_lo[:, k, t * P:(t + 1) * P]
                    pe.matmul(to, a, hi[:, kk, :], start=k == 0, stop=False)
                    pe.matmul(to, a, lo[:, kk, :], start=False, stop=False)
                    m = pe.matmul(to, b, hi[:, kk, :], start=False, stop=k == tiles - 1)
            m.then_inc(sem("unit_used"), 1)

        def linear_chunk(pe, unit, k0s, a_hi, a_lo, banks, ready=None):
            for j, k0 in enumerate(k0s):
                linear_unit(pe, unit + j, k0, k0s[-1] + 4, a_hi, a_lo, banks, ready)

        def turned_chunk(pe, unit, banks, ready=None):
            for j in range(2):
                hi, lo = use_unit(pe, unit + j)
                for kk in range(4):
                    k = 4 * j + kk
                    if ready:
                        pe.wait_ge(sem(ready[0]), ready[1] + k + 1)
                    for c in range(4):
                        to = psum[:, banks[c // 2], (c % 2) * SEQ:(c % 2 + 1) * SEQ]
                        a, b = hi[:, kk, c * P:(c + 1) * P], lo[:, kk, c * P:(c + 1) * P]
                        pe.matmul(to, a, hT_hi[:, k, :], start=k == 0 and c % 2 == 0, stop=False, skip_group_check=True)
                        pe.matmul(to, a, hT_lo[:, k, :], start=False, stop=False, skip_group_check=True)
                        m = pe.matmul(to, b, hT_hi[:, k, :], start=False, stop=k == KD - 1, skip_group_check=True)
                m.then_inc(sem("unit_used"), 1)

        def turned_x_bank(n, k):
            return ((4, 5, 6, 7) if n == 2 else (2, 3, 4, 6))[k // 2]

        def turned_x(n, k):
            return psum[:, turned_x_bank(n, k), (k % 2) * SEQ:(k % 2 + 1) * SEQ]

        def squares(act, n):
            for h in range(2):
                for t in range(TT):
                    if n:
                        act.wait_ge(sem("x_added"), 4 * (n - 1) + 2 * h + t + 1)
                    else:
                        act.wait_ge(sem("x_in"), 16 * TT)
                    cs = slice(512 * h, 512 * (h + 1))
                    act.activation(xn[:, t, cs], x[:, t, cs], ACT.Square, accum_out=sumsq[:, h, t:t + 1])\
                       .then_inc(sem("sumsq"), 1)

        def norm_act(act, n, gain, deferred, late_unit=UNITS):
            if not deferred:
                squares(act, n)
                act.wait_ge(sem("rstd"), n + 1)
                act.activation(xn[:, 1, :], x[:, 1, :], ACT.Copy, scale=rstd[:, 1:2]).then_inc(sem("xn"), 1)
            if gain:
                hT_hi_tiles(act, n, gain, range(KD))
            if deferred:
                squares(act, n)
            split_hi(act, late_unit)

        def hT_hi_tiles(act, n, gain, ks):
            for k in ks:
                act.wait_ge(sem("xT"), KD * n + (k | 1) + 1)
                act.activation(hT_hi[:, k, :], turned_x(n, k), ACT.Copy, scale=col(gain[0], gain[1] + k))\
                   .then_inc(sem("hT_hi"), 1)

        def hT_lo_tiles(dve, n, gain, ks):
            for k in ks:
                dve.wait_ge(sem("hT_hi"), KD * n + (k | 1) + 1)
                dve.scalar_tensor_tensor(hT_lo[:, k, :], turned_x(n, k), col(gain[0], gain[1] + k),
                                         hT_hi[:, k, :].bitcast(F32), ALU.mult, ALU.subtract).then_inc(sem("hT"), 1)

        def norm_pool(pool, n):
            order = in_order(pool, "gpsimd_order")
            pool.wait_ge(sem("sumsq"), 4 * (n + 1))
            order(pool.tensor_tensor(meansq[:, :], sumsq[:, 0, :], sumsq[:, 1, :], ALU.add))
            order(pool.tensor_scalar(meansq[:, :], meansq[:, :], 1.0 / D, EPS, ALU.mult, ALU.add))
            pool.tensor_tensor(rstd[:, :], meansq[:, :], neg_half[:, 0:TT], ALU.pow).then_inc(sem("rstd"), 1)

        def norm_dve(dve, n, gain, deferred, units=()):
            early, late = units[:-1], units[-1:]
            if not deferred:
                for unit in early:
                    split_lo(dve, unit)
                dve.wait_ge(sem("rstd"), n + 1)
                dve.tensor_scalar(xn[:, 0, :], x[:, 0, :], rstd[:, 0:1], None, ALU.mult).then_inc(sem("xn"), 1)
            if gain:
                hT_lo_tiles(dve, n, gain, range(4))
                if deferred:
                    for unit in early:
                        split_lo(dve, unit)
                hT_lo_tiles(dve, n, gain, range(4, KD))
            for unit in late:
                split_lo(dve, unit)

        def second_and_third(stage):
            return FIRST_UNIT[stage] + 1, FIRST_UNIT[stage] + 2

        def norm_pe(pe, n, deferred, xn_before=0):
            for k in range(KD):
                for t in range(TT):
                    if k % 4 == 0:
                        if not deferred:
                            pe.wait_ge(sem("xn"), xn_before + TT)
                        elif n:
                            pe.wait_ge(sem("x_added"), 4 * (n - 1) + 2 * (k // 4) + t + 1)
                        else:
                            pe.wait_ge(sem("x_in"), 16 * TT)
                    m = pe.transpose(psum[:, turned_x_bank(n, k), (k % 2) * SEQ + t * P:(k % 2) * SEQ + (t + 1) * P],
                                     (x if deferred else xn)[:, t, k * P:(k + 1) * P], ident)
                m.then_inc(sem("xT"), 1)

        GU_BANKS, SECOND_GU_BANKS = (0, 1), (7, 3)

        def ffn_sp(sp, f, names, layer):
            u0 = FIRST_UNIT[f]
            gate, up, down = (w[n][layer] for n in names)
            gate = gate.rearrange("(k p) n -> p k n", p=P)
            up = up.rearrange("(k p) n -> p k n", p=P)
            down = down.rearrange("(c k p) n -> p c k n", k=2, p=P)

            def gate_up(u, c, step=0, per=0):
                for h in range(2):
                    dst = raw[:, (u + h) % SLOTS, :].rearrange("p (k g n) -> p k g n", k=4, g=2)
                    cs = bass.ds(c * FC, FC)
                    load_unit(sp, u + h, [(dst[:, :, 0, :], gate[:, 4 * h:4 * h + 4, cs]),
                                          (dst[:, :, 1, :], up[:, 4 * h:4 * h + 4, cs])], step, per)

            def down_rows(u, c, step=0, per=0):
                dst = raw[:, u % SLOTS, :].rearrange("p (k n) -> p k n", k=2)
                rows = down[:, bass.ds(c, 1), :, :].rearrange("p c k n -> p (c k) n")
                load_unit(sp, u, [(dst[:, k:k + 1, :], rows[:, k:k + 1, :]) for k in range(2)], step, per)

            gate_up(u0, 0)
            gate_up(u0 + 2, 1)
            down_rows(u0 + 4, 0)
            with sp.Fori(2, NFC) as c:
                gate_up(u0 + 5, c, c - 2, 3)
                down_rows(u0 + 7, c - 1, c - 2, 3)
            down_rows(u0 + 3 * NFC - 1, NFC - 1)

        def ffn_pe(pe, f, n, before_last=None):
            u0 = FIRST_UNIT[f]

            def gate_up(u, c, step=0, per=0, first=False, banks=GU_BANKS):
                for h in range(2):
                    hi, lo = use_unit(pe, u + h, step, per)
                    if h == 0 and not first and banks == GU_BANKS:
                        pe.wait_ge(sem("ffn_hid"), TT * (NFC * FFNS.index(f) + c))
                    for kk in range(4):
                        k = 4 * h + kk
                        if first:
                            pe.wait_ge(sem("hT"), KD * n + k + 1)
                        for t in range(TT):
                            to = psum[:, banks[t], :]
                            a, b = hT_hi[:, k, t * P:(t + 1) * P], hT_lo[:, k, t * P:(t + 1) * P]
                            pe.matmul(to, a, hi[:, kk, :], start=k == 0, stop=False)
                            pe.matmul(to, a, lo[:, kk, :], start=False, stop=False)
                            m = pe.matmul(to, b, hi[:, kk, :], start=False, stop=k == KD - 1)
                    m.then_inc(sem("unit_used"), 1)
                    if h == 0 and banks == SECOND_GU_BANKS:
                        turn(0)

            def down(u, c, step=0, per=0, first=False, last=False, ks=(0, 1)):
                n_, slot, _ = place(u, step, per)
                pe.wait_ge(sem("lo_ready"), n_ + 1)
                pe.wait_ge(sem("ffn_hidT"), NFC * FFNS.index(f) + c + 1)
                hi = w_hi[:, slot, :].rearrange("p (k n) -> p k n", k=2)
                lo = w_lo[:, slot, :].rearrange("p (k n) -> p k n", k=2)
                if last:
                    for h in range(2):
                        cs = slice(512 * h, 512 * h + 512)
                        for t in range(TT):
                            for k in range(2):
                                to = psum[:, 4 + 2 * t + h, :]
                                a, b = last_hidT_hi[:, k, t * P:(t + 1) * P], last_hidT_lo[:, k, t * P:(t + 1) * P]
                                pe.matmul(to, a, hi[:, k, cs], start=False, stop=False)
                                pe.matmul(to, a, lo[:, k, cs], start=False, stop=False)
                                m = pe.matmul(to, b, hi[:, k, cs], start=False, stop=k == 1)
                        m.then_inc(sem("unit_used" if h else "down_half"), 1)
                    return
                for k in ks:
                    for t in range(TT):
                        a, b = hidT_hi[:, k, t * P:(t + 1) * P], hidT_lo[:, k, t * P:(t + 1) * P]
                        begin = first and k == 0
                        for h in range(2):
                            to, cs = psum[:, 4 + 2 * t + h, :], slice(512 * h, 512 * h + 512)
                            if begin and 4 + 2 * t + h == SECOND_GU_BANKS[0]:
                                pe.wait_ge(sem("ffn_hid"), TT * (NFC * FFNS.index(f) + 1) + 1)
                            pe.matmul(to, a, hi[:, k, cs], start=begin, stop=False)
                            pe.matmul(to, a, lo[:, k, cs], start=False, stop=False)
                            m = pe.matmul(to, b, hi[:, k, cs], start=False, stop=False)
                if k == 1:
                    m.then_inc(sem("unit_used"), 1)

            def turn(c):
                for t in range(TT):
                    pe.wait_ge(sem("ffn_hid"), TT * (NFC * FFNS.index(f) + c) + t + 1)
                    for k in range(2):
                        m = pe.transpose(psum[:, 2, k * SEQ + t * P:k * SEQ + (t + 1) * P],
                                         hid[:, t, k * P:(k + 1) * P], ident)
                m.then_inc(sem("ffn_turned"), 1)

            gate_up(u0, 0, first=True)
            gate_up(u0 + 2, 1, banks=SECOND_GU_BANKS)
            down(u0 + 4, 0, first=True)
            turn(1)
            with pe.Fori(2, NFC - 1) as c:
                gate_up(u0 + 5, c, c - 2, 3)
                down(u0 + 7, c - 1, c - 2, 3)
                turn(c)
            gate_up(u0 + 3 * NFC - 4, NFC - 1)
            down(u0 + 3 * NFC - 2, NFC - 2, ks=(0,))
            turn(NFC - 1)
            down(u0 + 3 * NFC - 2, NFC - 2, ks=(1,))
            if before_last:
                before_last(pe)
            down(u0 + 3 * NFC - 1, NFC - 1, last=True)

        def ffn_act(act, f, n, after_second=None):
            u0 = FIRST_UNIT[f]

            def gate(u, c, step=0, per=0, first=False, banks=GU_BANKS):
                act.wait_ge(sem("unit_used"), place(u, step, per)[0] + 1)
                if first:
                    act.wait_ge(sem("rstd"), n + 1)
                else:
                    act.wait_ge(sem("ffn_hid"), TT * (NFC * FFNS.index(f) + c))
                for t in range(TT):
                    act.activation(silu_g[:, t, :], psum[:, banks[t], 0:FC], ACT.Silu, scale=rstd[:, t:t + 1])\
                       .then_inc(sem("ffn_silu"), 1)

            def turned(c, to=hidT_hi):
                act.wait_ge(sem("ffn_turned"), NFC * FFNS.index(f) + c + 1)
                act.activation(to[:, :, :], psum[:, 2, :].rearrange("p (k n) -> p k n", k=2), ACT.Copy)\
                   .then_inc(sem("ffn_hidT_hi"), 1)

            split_hi(act, u0 + SLOTS)
            gate(u0 + 1, 0, first=True)
            split_hi(act, u0 + 1 + SLOTS)
            turned(0)
            split_hi(act, u0 + 2 + SLOTS)
            gate(u0 + 3, 1, banks=SECOND_GU_BANKS)
            split_hi(act, u0 + 3 + SLOTS)
            split_hi(act, u0 + 4 + SLOTS)
            turned(1)
            if after_second:
                after_second(act)
            with act.Fori(2, NFC - 1) as c:
                split_hi(act, u0 + 5 + SLOTS, c - 2, 3)
                gate(u0 + 6, c, c - 2, 3)
                split_hi(act, u0 + 6 + SLOTS, c - 2, 3)
                split_hi(act, u0 + 7 + SLOTS, c - 2, 3)
                turned(c)
            split_hi(act, u0 + 3 * NFC - 4 + SLOTS)
            gate(u0 + 3 * NFC - 3, NFC - 1)
            split_hi(act, u0 + 3 * NFC - 3 + SLOTS)
            turned(NFC - 1, last_hidT_hi)
            split_hi(act, u0 + 3 * NFC - 2 + SLOTS)

        def ffn_dve(dve, f, after_first=None, after_second=None, before_last=None):
            u0 = FIRST_UNIT[f]

            def times_up(c, first=False, banks=GU_BANKS):
                if not first:
                    dve.wait_ge(sem("ffn_turned"), NFC * FFNS.index(f) + c)
                for t in range(TT):
                    dve.wait_ge(sem("ffn_silu"), TT * (NFC * FFNS.index(f) + c) + t + 1)
                    dve.scalar_tensor_tensor(hid[:, t, :], psum[:, banks[t], FC:2 * FC], rstd[:, t:t + 1], silu_g[:, t, :],
                                             ALU.mult, ALU.mult).then_inc(sem("ffn_hid"), 1)

            def turned(c, hi=hidT_hi, lo=hidT_lo):
                dve.wait_ge(sem("ffn_hidT_hi"), NFC * FFNS.index(f) + c + 1)
                dve.tensor_tensor(lo[:, :, :], psum[:, 2, :].rearrange("p (k n) -> p k n", k=2),
                                  hi[:, :, :].bitcast(F32), ALU.subtract).then_inc(sem("ffn_hidT"), 1)

            split_lo(dve, u0 + SLOTS)
            times_up(0, first=True)
            split_lo(dve, u0 + 1 + SLOTS)
            turned(0)
            if after_first:
                after_first(dve)
            split_lo(dve, u0 + 2 + SLOTS)
            times_up(1, banks=SECOND_GU_BANKS)
            split_lo(dve, u0 + 3 + SLOTS)
            split_lo(dve, u0 + 4 + SLOTS)
            turned(1)
            if after_second:
                after_second(dve)
            with dve.Fori(2, NFC - 1) as c:
                split_lo(dve, u0 + 5 + SLOTS, c - 2, 3)
                times_up(c)
                split_lo(dve, u0 + 6 + SLOTS, c - 2, 3)
                split_lo(dve, u0 + 7 + SLOTS, c - 2, 3)
                turned(c)
            split_lo(dve, u0 + 3 * NFC - 4 + SLOTS)
            times_up(NFC - 1)
            split_lo(dve, u0 + 3 * NFC - 3 + SLOTS)
            turned(NFC - 1, last_hidT_hi, last_hidT_lo)
            if before_last:
                before_last(dve)
            for h in range(2):
                if h:
                    dve.wait_ge(sem("unit_used"), u0 + 3 * NFC)
                else:
                    dve.wait_ge(sem("down_half"), FFNS.index(f) + 1)
                cs = slice(512 * h, 512 * h + 512)
                for t in range(TT):
                    dve.scalar_tensor_tensor(x[:, t, cs], psum[:, 4 + 2 * t + h, :], 0.5, x[:, t, cs],
                                             ALU.mult, ALU.add).then_inc(sem("x_added"), 1)

        def start_sp(sp):
            for t in range(TT):
                sp.dma_start(x[:, t, :], w["x"][0, t * P:(t + 1) * P, :]).then_inc(sem("x_in"), 16)

        def load_rows(engine, names, landed):
            for name in names:
                a, n = ROWS[name]
                engine.dma_start(rows_in[a:a + n, :], w[name].rearrange("l (r c) -> (l r) c", c=P))\
                      .then_inc(sem(landed), 16)

        def start_act_loads(act):
            act.dma_start(const1[:, :], w["first_constants"]).then_inc(sem("const1_in"), 16)
            load_rows(act, list(ROWS)[4:], "last_rows_in")
            act.dma_start(taps_in[:, :], w["ssm_conv_w"][0].rearrange("t (r c) -> (t r) c", c=P))\
               .then_inc(sem("taps_in"), 16)

        def start_pool(pool):
            load_rows(pool, list(ROWS)[:4], "first_rows_in")
            pool.memset(neg_half[:, :], -0.5).then_inc(sem("neg_half"), 1)
            pool.dma_start(pos_i[:, :], w["positions"][0].rearrange("(t p) -> p t", p=P),
                           allow_slow_non_contiguous=True).then_inc(sem("pos_in"), 16)
            pool.dma_start(gains[:, 0, :], w["attn_q_norm"][0].partition_broadcast(P)).then_inc(sem("pos_in"), 16)
            pool.dma_start(gains[:, 1, :], w["attn_k_norm"][0].partition_broadcast(P)).then_inc(sem("pos_in"), 16)
            pool.dma_start(b_ada[:, :], w["b_ada_2"]).then_inc(sem("b_ada_in"), 16)
            pool.wait_ge(sem("neg_half"), 1)

        def ada_pool(pool):
            src = w["w_ada_2"][0].rearrange("(k p) n -> p k n", p=P)
            order = in_order(pool, "gpsimd_order")

            def load(k):
                pool.dma_start(ada_in[:, k % 2, :], src[:, k, :]).then_inc(sem(f"ada_in_{k % 2}"), 16)

            load(0)
            load(1)
            pool.wait_ge(sem("silu_c"), 1)
            for k in range(KD):
                pool.wait_ge(sem(f"ada_in_{k % 2}"), 16 * (k // 2 + 1))
                to = ada if k == 0 else ada_term
                order(pool.tensor_scalar(to[:, :], ada_in[:, k % 2, :], silu_c[:, k:k + 1], None, ALU.mult))
                if k + 2 < KD:
                    load(k + 2)
                if k:
                    order(pool.tensor_tensor(ada[:, :], ada[:, :], ada_term[:, :], ALU.add))
            pool.wait_ge(sem("b_ada_in"), 16)
            pool.tensor_tensor(ada[0:1, :], ada[0:1, :], b_ada[:, :], ALU.add).then_inc(sem("ada"), 1)

        def start_pe(pe):
            pe.wait_ge(sem("const1_in"), 16)
            norm_pe(pe, 0, True)
            pe.wait_ge(sem("first_rows_in"), 16 * 4)
            pe.wait_ge(sem("last_rows_in"), 16 * (len(ROWS) - 4))
            pe.transpose(psum[:, 0, 0:P], rows_in[:, :], ident).then_inc(sem("rows_turned"), 1)
            pe.wait_ge(sem("taps_in"), 16)
            pe.transpose(psum[:, 5, 0:P], taps_in[:, :], ident).then_inc(sem("rows_turned"), 1)
            pe.wait_ge(sem("cols"), 1)

        def start_act(act):
            start_act_loads(act)
            split_hi(act, 0)
            act.wait_ge(sem("cols"), 1)
            hT_hi_tiles(act, 0, ("ffn1_norm", 0), range(KD))
            split_hi(act, 1)
            squares(act, 0)
            split_hi(act, 2)
            act.activation(silu_c[:, :], col("c_2", 0, KD), ACT.Silu).then_inc(sem("silu_c"), 1)

        def trig_act(act):
            act.wait_ge(sem("angles"), 1)
            act.activation(trig[:, :, :, :], angle[:, :, :, :], ACT.Sin).then_inc(sem("trig"), 1)

        def start_dve(dve):
            dve.wait_ge(sem("rows_turned"), 1)
            dve.tensor_copy(cols[:, :], psum[:, 0, 0:P]).then_inc(sem("cols"), 1)
            dve.wait_ge(sem("cols"), 1)
            split_lo(dve, 0)
            hT_lo_tiles(dve, 0, ("ffn1_norm", 0), range(KD))
            split_lo(dve, 1)
            dve.wait_ge(sem("rows_turned"), 2)
            dve.tensor_copy(taps[:, :], psum[:, 5, 0:P]).then_inc(sem("cols"), 1)
            split_lo(dve, 2)

        def angles_dve(dve):
            order = in_order(dve, "vector_order")
            dve.wait_ge(sem("pos_in"), 48)
            order(dve.tensor_copy(pos_f[:, :], pos_i[:, :]))
            for t in range(TT):
                order(dve.tensor_scalar(angle[:, 0, t, :], c1("freq"), pos_f[:, t:t + 1], None, ALU.mult))
            order(dve.tensor_copy(angle[:, 1, :, :], angle[:, 0, :, :]))
            order(dve.tensor_scalar(turns[:, 0, :, :], angle[:, 0, :, :], 1 / (2 * np.pi), None, ALU.mult),
                  dve.tensor_scalar(turns[:, 1, :, :], angle[:, 1, :, :], 1 / (2 * np.pi), 0.25, ALU.mult, ALU.add))
            order(dve.tensor_scalar(turns[:, :, :, :], turns[:, :, :, :], ROUND, None, ALU.add))
            order(dve.tensor_scalar(turns[:, :, :, :], turns[:, :, :, :], ROUND, None, ALU.subtract))
            for part in (TWO_PI_HI, TWO_PI_MID, TWO_PI_LO):
                order(dve.scalar_tensor_tensor(angle[:, :, :, :], turns[:, :, :, :], -part, angle[:, :, :, :],
                                               ALU.mult, ALU.add))
            order(dve.tensor_scalar(angle[:, 1, :, :], angle[:, 1, :, :], np.pi / 2, None, ALU.add))
            limit = 3.1415925
            dve.tensor_scalar(angle[:, :, :, :], angle[:, :, :, :], -limit, limit, ALU.max, ALU.min)\
               .then_inc(sem("angles"), 1)

        def rope_tables_dve(dve):
            dve.wait_ge(sem("trig"), 1)
            sin, cos = trig[:, 0, :, :], trig[:, 1, :, :]
            for g, name in enumerate(("q", "k")):
                for part, table, h in (("cos1", cos, 0), ("sin2", sin, 1), ("cos2", cos, 1), ("sin1", sin, 0)):
                    gain = gains[:, g:g + 1, h * HALF:(h + 1) * HALF].broadcast_to([P, TT, HALF])
                    dve.tensor_tensor(rope_c[name, part][:, :, :], table, gain, ALU.mult).then_inc(sem("rope_tables"), 1)

        def ada_pe(pe):
            pe.wait_ge(sem("ada"), 1)
            for h in range(2):
                pe.matmul(psum[:, h, :], ones, ada[:, 2 * D + 512 * h:2 * D + 512 * (h + 1)], start=True, stop=True)
            for j in range(2 * KD):
                m = pe.matmul(psum[:, 3, j:j + 1], ada[:, j * P:(j + 1) * P], ones[:, 0:1], start=True, stop=True)
            m.then_inc(sem("mod_ready"), 1)

        def ada_dve(dve):
            dve.wait_ge(sem("mod_ready"), 1)
            dve.tensor_copy(gate2[:, :].rearrange("p (a n) -> p a n", a=2), psum[:, 0:2, :]).then_inc(sem("mod_read"), 1)
            dve.tensor_copy(mod_cols[:, :], psum[:, 3, 0:2 * KD]).then_inc(sem("mod_read"), 1)
            dve.wait_ge(sem("mod_read"), 2)
            dve.scalar_tensor_tensor(gain2[:, :], mod_cols[:, KD:2 * KD], 1.0, col("norm_g_2", 0, KD),
                                     ALU.add, ALU.mult).then_inc(sem("gain2"), 1)

        def heads(ap):
            return ap.rearrange("p t (h d) -> p t h d", d=HD)

        QKV_COLUMNS = (0, D, 2 * D, 512, D + 512, 2 * D + 512)
        ROPED = (0, 1, 3, 4)
        BY_ROWS = ((0, 0), (0, 1), (4, 0), (4, 1))
        FIRST_SLOT = 6
        HEAD_SLOTS = HEADS + 5

        def head_in(slot, step):
            for h in range(HEADS):
                if h + 2 * (h // 4) + step == slot:
                    return h
            return None

        def attn_sp(sp):
            u = FIRST_UNIT["qkv"]
            for c, n0 in enumerate(QKV_COLUMNS):
                for j in range(2):
                    load_unit(sp, u + 2 * c + j, [(raw_unit((u + 2 * c + j) % SLOTS)[:, k:k + 2, :], src)
                                                  for k, src in halves_of("attn_w_qkv", 4 * j, n0)])
            load_by_rows(sp, "wo", "attn_w_o")

        def load_by_rows(sp, stage, name):
            u = FIRST_UNIT[stage]
            for j, (k0, n) in enumerate(BY_ROWS):
                load_unit(sp, u + j, [(raw_unit((u + j) % SLOTS)[:, k:k + 2, :], src)
                                      for k, src in halves_of(name, k0, 512 * n)])

        def attn_pe(pe):
            pe.wait_ge(sem("mod_read"), 2)
            norm_pe(pe, 1, True)
            u = FIRST_UNIT["qkv"]
            for c in range(6):
                if c >= 2:
                    pe.wait_ge(sem("qkv_copied"), TT * (c - 1))
                for j in range(2):
                    linear_unit(pe, u + 2 * c + j, 4 * j, KD, hT_hi, hT_lo, pair_banks(c),
                                ("hT", KD * 1) if c == 0 else None)
                    head_slot_pe(pe, 2 * c + j - FIRST_SLOT)
            pe.wait_ge(sem("qkv_copied"), TT * 6)
            u = FIRST_UNIT["wo"]

            def wo_tiles(j, ks):
                n = BY_ROWS[j][1]
                hi, lo = use_unit(pe, u + j)
                for k in ks:
                    pe.wait_ge(sem("oT"), k + 1)
                    for t in range(TT):
                        to = psum[:, pair_banks(n)[t], :]
                        a, b = (o[:, k % 4, t * P:(t + 1) * P] for o in (oT_hi[k // 4], oT_lo[k // 4]))
                        pe.matmul(to, a, hi[:, k % 4, :], start=k == 0, stop=False)
                        pe.matmul(to, a, lo[:, k % 4, :], start=False, stop=False)
                        m = pe.matmul(to, b, hi[:, k % 4, :], start=False, stop=k == HEADS - 1)
                if ks[-1] % 4 == 3:
                    m.then_inc(sem("unit_used"), 1)

            wo_tiles(0, (0, 1))
            for slot, j, ks in ((6, 0, (2, 3)), (7, 1, (0,)), (8, 1, (1,)), (9, 1, (2,)), (10, 1, (3,)),
                                (11, 2, (4, 5)), (12, 2, (6, 7))):
                head_slot_pe(pe, slot)
                wo_tiles(j, ks)
            wo_tiles(3, (4, 5, 6, 7))

        def head_slot_pe(pe, slot):
            h = head_in(slot, 1)
            if h is not None:
                pe.wait_ge(sem("qkT"), h + 1)
                if h:
                    pe.wait_ge(sem("exps"), 2 * h)
                pe.matmul(psum[:, 5, 0:P], qkT[:, h % 2, 0, 0:P], qkT[:, h % 2, 1, 0:P], start=True, stop=True)
                pe.matmul(psum[:, 5, P:3 * P], qkT[:, h % 2, 0, P:SEQ], qkT[:, h % 2, 1, :], start=True, stop=True)\
                  .then_inc(sem("scores"), 1)
            h = head_in(slot, 0)
            if h is not None:
                pe.wait_ge(sem("roped_1"), 2 + 2 * (h // 4))
                pe.wait_ge(sem("roped_2"), 2 + 2 * (h // 4))
                if h:
                    pe.wait_ge(sem("qkT"), h)
                for j in range(2):
                    for t in range(TT):
                        cs = slice(j * D + h * HD, j * D + (h + 1) * HD)
                        m = pe.transpose(psum[:, 4, j * SEQ + t * P:j * SEQ + (t + 1) * P], qk[:, t, cs], ident)
                m.then_inc(sem("qk_turned"), 1)
            h = head_in(slot, 2)
            if h is not None:
                pe.wait_ge(sem("prob"), TT * (h + 1))
                if h:
                    pe.wait_ge(sem("probT"), h)
                for b in range(3):
                    m = pe.transpose(psum[:, 6, b * P:(b + 1) * P], prob[:, h % 2, b * P:(b + 1) * P], ident)
                m.then_inc(sem("prob_turned"), 1)
            h = head_in(slot, 3)
            if h is not None:
                pe.wait_ge(sem("probT"), h + 1)
                pe.wait_ge(sem("qkv_copied"), TT * (3 + 3 * (h // 4)))
                if h:
                    pe.wait_ge(sem("oT"), h)
                hs = slice(h * HD, (h + 1) * HD)
                pe.matmul(psum[:, 7, 0:SEQ], v_sb[:, 0, hs], probT[:, h % 2, 0:SEQ], start=True, stop=False)
                pe.matmul(psum[:, 7, P:SEQ], v_sb[:, 1, hs], probT[:, h % 2, SEQ:SEQ + P], start=False, stop=True)\
                  .then_inc(sem("o_ready"), 1)

        def attn_act(act):
            u = FIRST_UNIT["qkv"]
            norm_act(act, 1, ("mix_norm", 0), True, u - 1 + SLOTS)
            act.wait_ge(sem("rstd"), 2)
            for i in range(12):
                split_hi(act, u + i + SLOTS)
                c = i // 2
                if i % 2:
                    act.wait_ge(sem("unit_used"), u + i + 1)
                    n0 = QKV_COLUMNS[c]
                    to = qk[:, :, n0:n0 + 512] if n0 < 2 * D else v_sb[:, :, n0 - 2 * D:n0 - 2 * D + 512]
                    for t in range(TT):
                        act.activation(to[:, t, :], psum[:, pair_banks(c)[t], :], ACT.Copy, scale=rstd[:, t:t + 1])\
                           .then_inc(sem("qkv_copied"), 1)
                    if c in ROPED:
                        if c:
                            act.wait_ge(sem("qk_ss"), ROPED.index(c))
                        act.wait_ge(sem("qkv_copied"), TT * (c + 1))
                        act.activation(qk_sq[:, :, :], to, ACT.Square).then_inc(sem("qk_sq"), 1)
                head_slot_act(act, i - FIRST_SLOT)
            u = FIRST_UNIT["wo"]
            for slot in range(6, HEAD_SLOTS):
                head_slot_act(act, slot)
                if slot == 10:
                    split_hi(act, u + SLOTS)
            split_hi(act, u + 1 + SLOTS)
            split_hi(act, u + 2 + SLOTS)

        def head_slot_act(act, slot):
            h = head_in(slot, 0)
            if h is not None:
                act.wait_ge(sem("qk_turned"), h + 1)
                if h >= 2:
                    act.wait_ge(sem("scores"), h - 1)
                act.activation(qkT[:, h % 2, :, :], psum[:, 4, :].rearrange("p (j n) -> p j n", j=2), ACT.Copy)\
                   .then_inc(sem("qkT"), 1)
            h = head_in(slot, 2)
            if h is not None:
                act.wait_ge(sem("prob_turned"), h + 1)
                if h >= 2:
                    act.wait_ge(sem("o_ready"), h - 1)
                act.activation(probT[:, h % 2, :], psum[:, 6, 0:3 * P], ACT.Copy).then_inc(sem("probT"), 1)
            h = head_in(slot, 1)
            if h is not None:
                act.wait_ge(sem("bias"), h + 1)
                if h >= 2:
                    act.wait_ge(sem("prob_turned"), h - 1)
                for t in range(TT):
                    act.activation(prob[:, h % 2, SEEN[t]], psum[:, 5, SEEN[t]], ACT.Exp,
                                   bias=bias_s[:, h, t:t + 1], scale=SCALE, accum_out=sum_s[:, h, t:t + 1])\
                       .then_inc(sem("exps"), 1)
            h = head_in(slot, 3)
            if h is not None:
                act.wait_ge(sem("o_ready"), h + 1)
                act.activation(oT_hi[h // 4][:, h % 4, :], psum[:, 7, 0:SEQ], ACT.Copy).then_inc(sem("oT_hi"), 1)

        def attn_pool(pool):
            norm_pool(pool, 1)
            order = in_order(pool, "gpsimd_order")
            pool.wait_ge(sem("rope_tables"), 8)
            for n, c in enumerate(ROPED):
                cs = slice(4 * n, 4 * n + 4)
                pool.wait_ge(sem("qk_ss"), n + 1)
                order(pool.tensor_scalar(qk_ms[:, :, cs], qk_ss[:, :, cs], 1.0 / HD, EPS, ALU.mult, ALU.add))
                pool.tensor_tensor(qk_rstd[:, :, cs], qk_ms[:, :, cs],
                                   neg_half[:, 0:8].rearrange("p (t h) -> p t h", t=TT), ALU.pow)\
                    .then_inc(sem("qk_rstd"), 1)
                pool.wait_ge(sem("qk_scaled"), n + 1)
                if n:
                    pool.wait_ge(sem("roped_2"), n)
                name, _, one, two = roped_chunk(c)
                pool.tensor_tensor(rope_d[:, :, :, :], two, by_head(rope_c[name, "cos2"]), ALU.mult)\
                    .then_inc(sem("rope_de"), 1)
                pool.tensor_tensor(rope_e[:, :, :, :], one, by_head(rope_c[name, "sin1"]), ALU.mult)\
                    .then_inc(sem("rope_de"), 1)
                pool.wait_ge(sem("rope_de"), 2 * n + 2)
                pool.wait_ge(sem("rope_ab"), 2 * n + 2)
                pool.tensor_tensor(two, rope_d[:, :, :, :], rope_e[:, :, :, :], ALU.add).then_inc(sem("roped_2"), 1)

        def roped_chunk(c):
            n0 = QKV_COLUMNS[c]
            both = heads(qk[:, :, n0:n0 + 512])
            return "q" if n0 < D else "k", both, both[:, :, :, 0:HALF], both[:, :, :, HALF:HD]

        def by_head(table):
            return table[:, :, :].unsqueeze(2).broadcast_to([P, TT, 4, HALF])

        def attn_dve(dve):
            u = FIRST_UNIT["qkv"]
            norm_dve(dve, 1, ("mix_norm", 0), True, second_and_third("qkv"))
            for i in range(12):
                bias_dve(dve, i - FIRST_SLOT)
                split_lo(dve, u + i + SLOTS)
                c = i // 2
                if i % 2 and c - 1 in ROPED:
                    rope_end_dve(dve, ROPED.index(c - 1), c - 1)
                if i % 2 and c in ROPED:
                    n = ROPED.index(c)
                    dve.wait_ge(sem("qk_sq"), n + 1)
                    dve.tensor_reduce(qk_ss[:, :, 4 * n:4 * n + 4], heads(qk_sq[:, :, :]), X_AXIS, ALU.add)\
                       .then_inc(sem("qk_ss"), 1)
                if i % 2 == 0 and c - 1 in ROPED:
                    rope_dve(dve, ROPED.index(c - 1), c - 1)
                prob_dve(dve, i - FIRST_SLOT)
            u = FIRST_UNIT["wo"]
            for slot in range(6, HEAD_SLOTS):
                bias_dve(dve, slot)
                prob_dve(dve, slot)
                if slot == 10:
                    split_lo(dve, u + SLOTS)
            split_lo(dve, u + 1 + SLOTS)
            for h in range(2):
                if h:
                    split_lo(dve, u + 2 + SLOTS)
                dve.wait_ge(sem("unit_used"), u + 3 + h)
                add_half(dve, h, pair_banks(h))

        def rope_dve(dve, n, c):
            name, both, one, two = roped_chunk(c)
            dve.wait_ge(sem("qk_rstd"), n + 1)
            r_ = qk_rstd[:, :, 4 * n:4 * n + 4].unsqueeze(3).broadcast_to([P, TT, 4, HD])
            dve.tensor_tensor(both, both, r_, ALU.mult).then_inc(sem("qk_scaled"), 1)
            dve.wait_ge(sem("qk_scaled"), n + 1)
            if n:
                dve.wait_ge(sem("roped_1"), n)
            dve.wait_ge(sem("rope_tables"), 8)
            dve.tensor_tensor(rope_a[:, :, :, :], one, by_head(rope_c[name, "cos1"]), ALU.mult)\
               .then_inc(sem("rope_ab"), 1)
            dve.tensor_tensor(rope_b[:, :, :, :], two, by_head(rope_c[name, "sin2"]), ALU.mult)\
               .then_inc(sem("rope_ab"), 1)

        def rope_end_dve(dve, n, c):
            one = roped_chunk(c)[2]
            dve.wait_ge(sem("rope_ab"), 2 * n + 2)
            dve.wait_ge(sem("rope_de"), 2 * n + 2)
            dve.tensor_tensor(one, rope_a[:, :, :, :], rope_b[:, :, :, :], ALU.subtract)\
               .then_inc(sem("roped_1"), 1)

        def bias_dve(dve, slot):
            order = in_order(dve, "vector_order")
            h = head_in(slot, 1)
            if h is not None:
                dve.wait_ge(sem("scores"), h + 1)
                diagonal = psum[:, 5, 0:3 * P].rearrange("p (b k) -> p b k", k=P)[:, 0:3:2, :]
                order(dve.tensor_tensor(diagonal, diagonal, c1("causal").unsqueeze(1).broadcast_to([P, 2, P]), ALU.add))
                order(*(dve.tensor_reduce(top_s[:, h, t:t + 1], psum[:, 5, SEEN[t]], X_AXIS, ALU.max)
                        for t in range(TT)))
                dve.tensor_scalar(bias_s[:, h, :], top_s[:, h, :], -SCALE, None, ALU.mult).then_inc(sem("bias"), 1)

        def prob_dve(dve, slot):
            order = in_order(dve, "vector_order")
            h = head_in(slot, 3)
            if h is not None:
                dve.wait_ge(sem("oT_hi"), h + 1)
                to, hi = (o[h // 4][:, h % 4, :] for o in (oT_lo, oT_hi))
                dve.tensor_tensor(to, psum[:, 7, 0:SEQ], hi.bitcast(F32), ALU.subtract).then_inc(sem("oT"), 1)
            h = head_in(slot, 1)
            if h is not None:
                dve.wait_ge(sem("exps"), 2 * h + 2)
                order(dve.reciprocal(inv_s[:, h, :], sum_s[:, h, :]))
                for t in range(TT):
                    dve.tensor_scalar(prob[:, h % 2, SEEN[t]], prob[:, h % 2, SEEN[t]], inv_s[:, h, t:t + 1], None,
                                      ALU.mult).then_inc(sem("prob"), 1)

        def add_to_x(dve, stage, units, banks):
            u = FIRST_UNIT[stage]
            for h in range(2):
                for j in range(units - 1):
                    split_lo(dve, u + units * h + j + SLOTS)
                dve.wait_ge(sem("unit_used"), u + units * (h + 1))
                add_half(dve, h, banks[h])
                if h == 0:
                    split_lo(dve, u + units - 1 + SLOTS)

        def add_half(dve, h, banks):
            cs = slice(512 * h, 512 * h + 512)
            for t in range(TT):
                dve.tensor_tensor(x[:, t, cs], psum[:, banks[t], :], x[:, t, cs], ALU.add).then_inc(sem("x_added"), 1)

        CHUNKS = CONVD // 512
        X_CHUNKS = DI // 512
        B_CHUNKS = NB // 512
        ITEMS = GROUPS * TT

        def xbc_unit(c):
            return FIRST_UNIT["ssm_xbc_last"] if c == CHUNKS - 1 else FIRST_UNIT["ssm_xbc"] + 2 * c

        def ssm_sp(sp):
            load_linear(sp, "ssm_xbc", "ssm_w_in", DI, (0, 4), CHUNKS - 1)
            u = FIRST_UNIT["ssm_dt"]
            src = w["ssm_w_in"][0].rearrange("(k p) n -> p k n", p=P)[:, :, DI + CONVD:DI + CONVD + SH]
            dst = raw[:, u % SLOTS, 0:KD * SH].rearrange("p (k n) -> p k n", k=KD)
            load_unit(sp, u, [(dst[:, k:k + 4, :], src[:, k:k + 4, :]) for k in (0, 4)])
            load_linear(sp, "ssm_xbc_last", "ssm_w_in", DI + 512 * (CHUNKS - 1), (0, 4), 1)
            load_linear(sp, "ssm_z", "ssm_w_in", 0, (0, 4), DI // 512)
            load_linear(sp, "ssm_out", "ssm_w_out", 0, (0, 4, 8, 12), 2)

        def ssm_pe(pe):
            norm_pe(pe, 4, False)

            def step_sizes():
                use_unit(pe, FIRST_UNIT["ssm_dt"])
                slot = FIRST_UNIT["ssm_dt"] % SLOTS
                hi = w_hi[:, slot, 0:KD * SH].rearrange("p (k n) -> p k n", k=KD)
                lo = w_lo[:, slot, 0:KD * SH].rearrange("p (k n) -> p k n", k=KD)
                for t in range(TT):
                    to = psum[:, 6, t * SH:(t + 1) * SH]
                    for k in range(KD):
                        a, b = hT_hi[:, k, t * P:(t + 1) * P], hT_lo[:, k, t * P:(t + 1) * P]
                        pe.matmul(to, a, hi[:, k, :], start=k == 0, stop=False)
                        pe.matmul(to, a, lo[:, k, :], start=False, stop=False)
                        m = pe.matmul(to, b, hi[:, k, :], start=False, stop=k == KD - 1)
                m.then_inc(sem("unit_used"), 1)

            for c in range(CHUNKS):
                if c == CHUNKS - 1:
                    step_sizes()
                if c >= 2:
                    pe.wait_ge(sem("conv_out"), 4 * (c - 1))
                b = 2 * (c % 2)
                turned_chunk(pe, xbc_unit(c), (b, b + 1), ("hT", KD * 4) if c == 0 else None)
                if 1 <= c <= X_CHUNKS + B_CHUNKS:
                    ssm_turn(pe, c - 1)
                if c == CHUNKS - 1:
                    pe.wait_ge(sem("a_dt"), 1)
                    for t in range(TT):
                        pe.matmul(psum[:, 7, t * SH:(t + 1) * SH], c1("runsum"), per_token["a_dt"][:, t, :],
                                  start=True, stop=True)
                    pe.matmul(psum[:, 7, 2 * SH:3 * SH], ones, per_token["a_dt"][:, 0, :], start=True, stop=True)
                    for t in range(TT):
                        m = pe.matmul(psum[0:SH, 6, t * P:(t + 1) * P], per_token["a_dt"][:, t, :], c1("runsum"),
                                      start=True, stop=True)
                    m.then_inc(sem("a_sums"), 1)

            def z_unit(j):
                q, k0 = j // 2, 4 * (j % 2)
                if j % 2 == 0:
                    pe.wait_ge(sem("conv_out"), 4 * (CHUNKS - 1))
                    if q:
                        pe.wait_ge(sem("z"), q)
                hi, lo = use_unit(pe, FIRST_UNIT["ssm_z"] + j)
                for kk in range(4):
                    k = k0 + kk
                    for t in range(TT):
                        a, b = hT_hi[:, k, t * P:(t + 1) * P], hT_lo[:, k, t * P:(t + 1) * P]
                        pe.matmul(psum[:, t, :], a, hi[:, kk, :], start=k == 0, stop=False)
                        pe.matmul(psum[:, t, :], a, lo[:, kk, :], start=False, stop=False)
                        m = pe.matmul(psum[:, t, :], b, hi[:, kk, :], start=False, stop=k == KD - 1)
                m.then_inc(sem("unit_used"), 1)

            def scores(i):
                g, t = divmod(i, TT)
                if i >= 2:
                    pe.wait_ge(sem("ssm_diff"), HPG * (i - 1))
                for n, part in enumerate((sums_hi, sums_lo)):
                    pe.matmul(psum[:, 2 + i % 2, :], group_r[0:SH, g:g + 1].broadcast_to([SH, P]),
                              part[0:SH, t, :, :], start=n == 0, stop=n == 1)
                if i >= 2:
                    pe.wait_ge(sem("within"), i - 1)
                ts = slice(t * P, (t + 1) * P)
                pe.matmul(psum[:, 4 + i % 2, 0:P], bcT[:, g, ts], bcT[:, GROUPS + g, ts], start=True, stop=True)\
                  .then_inc(sem("ssm_scores"), 1)

            def state_sums(g):
                pe.wait_ge(sem("x_decayed"), g + 1)
                if g:
                    pe.wait_ge(sem("y"), TT * g - 1)
                pe.matmul(psum[:, 6, GW:2 * GW], b_rows[:, g, :], x_decayed[:, :, :], start=True, stop=True)\
                  .then_inc(sem("state_sums"), 1)

            def outputs(i):
                g, t = divmod(i, TT)
                pe.wait_ge(sem("within"), i + 1)
                pe.wait_ge(sem("xdt"), i + 1)
                pe.wait_ge(sem("states"), g + 1)
                if i >= 2:
                    pe.wait_ge(sem("y"), i - 1)
                bank = psum[:, 6 + i % 2, :]
                for hh in range(HPG):
                    m = pe.matmul(bank[:, hh * SP:(hh + 1) * SP], within[:, i % 2, hh, :], xdt[:, i % 2, hh, :],
                                  start=True, stop=True)
                if t:
                    m = pe.matmul(bank[:, GW:2 * GW], bcT[:, GROUPS + g, P:SEQ], states[:, g % 2, :],
                                  start=True, stop=True)
                m.then_inc(sem("ssm_out"), 1)

            def turn_y(q):
                pe.wait_ge(sem("y_scaled"), 4 * (q + 1))
                if q == 0:
                    pe.wait_ge(sem("ssm_diff"), HPG * ITEMS)
                elif q == 1:
                    pe.wait_ge(sem("within"), ITEMS)
                else:
                    pe.wait_ge(sem("yT"), 4 * (q - 1))
                for kk in range(4):
                    k, b = 4 * q + kk, 2 + 2 * (q % 2) + kk // 2
                    for t in range(TT):
                        at_ = (kk % 2) * SEQ + t * P
                        m = pe.transpose(psum[:, b, at_:at_ + P], y[:, t, k * P:(k + 1) * P], ident)
                    m.then_inc(sem("y_turned"), 1)

            for j in range(ITEMS // 2 + 1):
                if j < ITEMS // 2:
                    z_unit(j)
                    if j == 0:
                        pe.wait_ge(sem("conv_out"), 4 * CHUNKS)
                        pe.wait_ge(sem("a_sum"), 2)
                        pe.wait_ge(sem("sums_lo"), HPG)
                if j:
                    state_sums(j - 1)
                if j < ITEMS // 2:
                    scores(2 * j)
                    scores(2 * j + 1)
                else:
                    turn_y(0)
                    turn_y(1)
                if j:
                    outputs(2 * j - 2)
                    outputs(2 * j - 1)
            pe.wait_ge(sem("z"), 4)
            u = FIRST_UNIT["ssm_out"]
            for q in range(4):
                linear_unit(pe, u + q, 4 * q, KI, yT_hi, yT_lo, (0, 1), ("yT", 0))
                if q < 2:
                    turn_y(q + 2)
            linear_chunk(pe, u + 4, (0, 4, 8, 12), yT_hi, yT_lo, (5, 7))

        def ssm_turn(pe, c):
            pe.wait_ge(sem("xbc"), 4 * (c + 1))
            if c:
                pe.wait_ge(sem("rows"), c)
            for i in range(4):
                if c < X_CHUNKS:
                    for t in range(TT):
                        m = pe.transpose(psum[:, 4 + t, i * P:(i + 1) * P], xT[:, c % 2, i, t * P:(t + 1) * P], ident)
                else:
                    m = pe.transpose(psum[:, 4, i * P:(i + 1) * P], bcT[:, 4 * (c - X_CHUNKS) + i, 0:P], ident)
            m.then_inc(sem("rows_ready"), 1)

        def ssm_act(act):
            norm_act(act, 4, ("mix_norm", KD), False, FIRST_UNIT["ssm_xbc"] - 1 + SLOTS)

            def copy_rows(c):
                act.wait_ge(sem("rows_ready"), c + 1)
                if c < X_CHUNKS:
                    act.activation(xs[:, :, 512 * c:512 * (c + 1)], psum[:, 4:6, :], ACT.Copy).then_inc(sem("rows"), 1)
                else:
                    g = 4 * (c - X_CHUNKS)
                    act.activation(b_rows[:, g:g + 4, :], psum[:, 4, :].rearrange("p (g n) -> p g n", g=4), ACT.Copy)\
                       .then_inc(sem("rows"), 1)

            for c in range(CHUNKS):
                if c == CHUNKS - 1:
                    split_hi(act, FIRST_UNIT["ssm_dt"] + SLOTS)
                    act.activation(group_r[:, :], c1("group_of_head"), ACT.Copy).then_inc(sem("sums_hi"), 1)
                    act.wait_ge(sem("per_head_in"), 48)
                    act.activation(per_head["a_rate"][:, :], per_head["a_rate"][:, :], ACT.Exp).then_inc(sem("a_rate"), 1)
                    act.wait_ge(sem("dt_abs"), 1)
                    act.activation(per_token["dt_exp"][:, :, :], per_token["dt_a"][:, :, :], ACT.Exp, scale=-1.0)\
                       .then_inc(sem("dt_exp"), 1)
                u = xbc_unit(c)
                split_hi(act, u + SLOTS)
                act.wait_ge(sem("unit_used"), u + 2)
                if c >= 2:
                    act.wait_ge(sem("xbc"), 4 * (c - 1))
                for i in range(4):
                    tile = 4 * c + i
                    act.activation(conv[:, c % 2, i, :], psum[:, 2 * (c % 2) + i // 2, (i % 2) * SEQ:(i % 2 + 1) * SEQ],
                                   ACT.Copy, scale=taps[:, (TAPS - 1) * 32 + tile:(TAPS - 1) * 32 + tile + 1])\
                       .then_inc(sem("conv_first"), 1)
                split_hi(act, u + 1 + SLOTS)
                if c == CHUNKS - 1:
                    act.wait_ge(sem("a_sums"), 1)
                    for hh in range(HPG):
                        act.activation(sums_hi[0:SH, :, hh, :], psum[0:SH, 6, 0:SEQ].rearrange("p (t n) -> p t n", t=TT),
                                       ACT.Copy, scale=c1("head_in_group")[0:SH, hh:hh + 1])\
                           .then_inc(sem("sums_hi"), 1)
                if 1 <= c <= X_CHUNKS + B_CHUNKS:
                    copy_rows(c - 1)
                for i in range(4):
                    tile = 4 * c + i
                    act.wait_ge(sem("conv_out"), tile + 1)
                    if i == 0 and 2 <= c < X_CHUNKS:
                        act.wait_ge(sem("rows_ready"), c - 1)
                    to = xT[:, c % 2, i, :] if c < X_CHUNKS else bcT[:, tile - 4 * X_CHUNKS, :]
                    act.activation(to, conv[:, c % 2, i, :], ACT.Silu, bias=col("ssm_conv_b", tile))\
                       .then_inc(sem("xbc"), 1)
            act.wait_ge(sem("a_sum"), 2)
            act.activation(per_head["end_decay"][:, :], per_head["end_decay"][:, :], ACT.Exp).then_inc(sem("decays"), 1)
            act.activation(per_head["start_decay"][:, :], per_token["a_sum"][:, 1, :], ACT.Exp)\
               .then_inc(sem("decays"), 1)

            def exps(i):
                act.wait_ge(sem("ssm_diff"), HPG * (i + 1))
                act.activation(decay[:, i % 2, :, :], decay[:, i % 2, :, :], ACT.Exp).then_inc(sem("decay"), 1)

            def copy_states(g):
                act.wait_ge(sem("state_sums"), g + 1)
                act.activation(states[:, g % 2, :], psum[:, 6, GW:2 * GW], ACT.Copy).then_inc(sem("states"), 1)

            def group_squares(q):
                act.wait_ge(sem("y_gated"), q + 1)
                for t in range(TT):
                    for g in (2 * q, 2 * q + 1):
                        cs = slice(GW * g, GW * (g + 1))
                        act.activation(z[:, t, cs], y[:, t, cs], ACT.Square, accum_out=y_ss[:, t, g:g + 1])\
                           .then_inc(sem("y_ss"), 1)

            def group_scale(q):
                act.wait_ge(sem("y_rstd"), q + 1)
                for t in range(TT):
                    for g in (2 * q, 2 * q + 1):
                        cs = slice(GW * g, GW * (g + 1))
                        act.activation(y[:, t, cs], y[:, t, cs], ACT.Copy, scale=y_rstd[:, t, g:g + 1])\
                           .then_inc(sem("y_scaled"), 1)

            def silu_z(q):
                act.wait_ge(sem("z"), q + 1)
                zq = z[:, :, 512 * q:512 * (q + 1)]
                act.activation(zq, zq, ACT.Silu).then_inc(sem("z_silu"), 1)

            def turned_y(q):
                for k in range(4 * q, 4 * q + 4):
                    act.wait_ge(sem("y_turned"), (k | 1) + 1)
                    act.activation(yT_hi[:, k, :], y_bank(k), ACT.Copy, scale=col("ssm_norm", k))\
                       .then_inc(sem("yT_hi"), 1)

            for j in range(ITEMS // 2 + 1):
                q = j // 2
                if j:
                    copy_states(j - 1)
                if j < ITEMS // 2 and j % 2:
                    act.wait_ge(sem("unit_used"), FIRST_UNIT["ssm_z"] + j + 1)
                    act.activation(z[:, :, 512 * q:512 * (q + 1)], psum[:, 0:TT, :], ACT.Copy).then_inc(sem("z"), 1)
                if j < ITEMS // 2:
                    split_hi(act, FIRST_UNIT["ssm_z"] + j + SLOTS)
                if j % 2 == 0 and q >= 2:
                    group_scale(q - 2)
                if j < ITEMS // 2:
                    exps(2 * j)
                    exps(2 * j + 1)
                if j % 2:
                    if q:
                        group_squares(q - 1)
                    if q < 3:
                        silu_z(q)
            act.wait_ge(sem("x_skip"), ITEMS)
            turned_y(0)
            silu_z(3)
            turned_y(1)
            group_squares(3)
            turned_y(2)
            group_scale(3)
            turned_y(3)
            for j in range(7):
                split_hi(act, FIRST_UNIT["ssm_out"] + j + SLOTS)

        def y_bank(k):
            b = 2 + 2 * (k // 4 % 2) + k % 4 // 2
            return psum[:, b, (k % 2) * SEQ:(k % 2 + 1) * SEQ]

        def ssm_pool(pool):
            for name, src in (("dt_bias", "ssm_dt_bias"), ("a_rate", "ssm_a_log"), ("d_skip", "ssm_d")):
                pool.dma_start(per_head[name][:, :], w[src][0].partition_broadcast(P)).then_inc(sem("per_head_in"), 16)
            norm_pool(pool, 4)
            pool.wait_ge(sem("rows"), X_CHUNKS)
            pool.wait_ge(sem("dt"), 1)
            pool.wait_ge(sem("decays"), 2)
            order = in_order(pool, "gpsimd_order")

            def group_rstd(q):
                gs = slice(2 * q, 2 * q + 2)
                pool.wait_ge(sem("y_ss"), 4 * (q + 1))
                order(pool.tensor_scalar(y_ms[:, :, gs], y_ss[:, :, gs], 1.0 / GW, EPS, ALU.mult, ALU.add))
                pool.tensor_tensor(y_rstd[:, :, gs], y_ms[:, :, gs],
                                   neg_half[:, 0:4].rearrange("p (t g) -> p t g", t=TT), ALU.pow)\
                    .then_inc(sem("y_rstd"), 1)

            for i in range(ITEMS):
                g, t = divmod(i, TT)
                src = xs[:, t, g * GW:(g + 1) * GW].rearrange("p (h d) -> p h d", d=SP)
                hs = slice(HPG * g, HPG * (g + 1))
                if i >= 2:
                    pool.wait_ge(sem("ssm_out"), i - 1)
                pool.tensor_tensor(xdt[:, i % 2, :, :], src, by_channel(per_token["dt"][:, t, hs]), ALU.mult)\
                    .then_inc(sem("xdt"), 1)
                if t == 0:
                    pool.wait_ge(sem("xdt"), i + 1)
                    pool.tensor_tensor(x_decayed[:, :, :], xdt[:, i % 2, :, :],
                                       by_channel(per_head["end_decay"][:, hs]), ALU.mult).then_inc(sem("x_decayed"), 1)
                if i >= 2:
                    pool.wait_ge(sem("y"), i - 1)
                pool.tensor_tensor(x_skip[:, i % 2, :, :], src, by_channel(per_head["d_skip"][:, hs]), ALU.mult)\
                    .then_inc(sem("x_skip"), 1)
                if t and i >= 7 and i % 4 == 3:
                    group_rstd((i - 7) // 4)
            group_rstd(3)

        def by_channel(ap):
            return ap.unsqueeze(2).broadcast_to([P, HPG, SP])

        def ssm_dve(dve):
            norm_dve(dve, 4, ("mix_norm", KD), False, second_and_third("ssm_xbc"))
            order = in_order(dve, "vector_order")
            raw_, a, b, s, p, e = (per_token[n][:, :, :] for n in ("dt_raw", "dt_a", "dt_b", "dt_s", "dt_p", "dt_exp"))
            across = lambda ap: ap.unsqueeze(1).broadcast_to([P, TT, SH])
            for c in range(CHUNKS):
                u = xbc_unit(c)
                if c == CHUNKS - 1:
                    split_lo(dve, FIRST_UNIT["ssm_dt"] + SLOTS)
                    dve.wait_ge(sem("per_head_in"), 48)
                    dve.wait_ge(sem("unit_used"), FIRST_UNIT["ssm_dt"] + 1)
                    order(dve.tensor_tensor(raw_, psum[:, 6, 0:TT * SH].rearrange("p (t h) -> p t h", t=TT),
                                            across(per_head["dt_bias"][:, :]), ALU.add))
                    dve.scalar_tensor_tensor(a, raw_, -1.0, raw_, ALU.mult, ALU.max).then_inc(sem("dt_abs"), 1)
                    dve.wait_ge(sem("dt_exp"), 1)
                    order(dve.tensor_scalar(b, e, 2.0, None, ALU.add))
                    order(dve.reciprocal(p, b))
                    order(dve.tensor_tensor(s, e, p, ALU.mult))
                    order(dve.tensor_tensor(b, s, s, ALU.mult))
                    n_terms = 9
                    order(dve.tensor_scalar(p, b, 1.0 / (2 * n_terms + 1), None, ALU.mult))
                    for n in range(n_terms - 1, 0, -1):
                        order(dve.scalar_tensor_tensor(p, p, 1.0 / (2 * n + 1), b, ALU.add, ALU.mult))
                    order(dve.scalar_tensor_tensor(p, p, 1.0, s, ALU.add, ALU.mult))
                    order(dve.tensor_scalar(p, p, 2.0, None, ALU.mult))
                    dve.scalar_tensor_tensor(per_token["dt"][:, :, :], raw_, 0.0, p, ALU.max, ALU.add).then_inc(sem("dt"), 1)
                    dve.wait_ge(sem("dt"), 1)
                    dve.wait_ge(sem("a_rate"), 1)
                    dve.scalar_tensor_tensor(per_token["a_dt"][:, :, :], per_token["dt"][:, :, :], -1.0,
                                             across(per_head["a_rate"][:, :]), ALU.mult, ALU.mult)\
                       .then_inc(sem("a_dt"), 1)
                split_lo(dve, u + SLOTS)
                if c == CHUNKS - 1:
                    dve.wait_ge(sem("a_sums"), 1)
                    dve.tensor_copy(per_token["a_sum"][:, :, :], psum[:, 7, 0:TT * SH].rearrange("p (t h) -> p t h", t=TT))\
                       .then_inc(sem("a_sum"), 1)
                    dve.wait_ge(sem("a_sum"), 1)
                    dve.tensor_tensor(per_head["end_decay"][:, :], psum[:, 7, 2 * SH:3 * SH], per_token["a_sum"][:, 0, :],
                                      ALU.subtract).then_inc(sem("a_sum"), 1)
                for j in range(2):
                    dve.wait_ge(sem("conv_first"), 4 * c + 2 * j + 2)
                    for back in range(1, TAPS):
                        steps = []
                        for i in (2 * j, 2 * j + 1):
                            tap = (TAPS - 1 - back) * 32 + 4 * c + i
                            to = conv[:, c % 2, i, back:SEQ]
                            src = psum[:, 2 * (c % 2) + j, (i % 2) * SEQ:(i % 2 + 1) * SEQ - back]
                            steps.append(dve.scalar_tensor_tensor(to, src, taps[:, tap:tap + 1], to, ALU.mult, ALU.add))
                        if back < TAPS - 1:
                            order(*steps)
                        else:
                            for step in steps:
                                step.then_inc(sem("conv_out"), 1)
                if c == CHUNKS - 1:
                    for hh in range(HPG):
                        dve.wait_ge(sem("sums_hi"), HPG + 1)
                        dve.scalar_tensor_tensor(sums_lo[0:SH, :, hh, :],
                                                 psum[0:SH, 6, 0:SEQ].rearrange("p (t n) -> p t n", t=TT),
                                                 c1("head_in_group")[0:SH, hh:hh + 1],
                                                 sums_hi[0:SH, :, hh, :].bitcast(F32), ALU.mult, ALU.subtract)\
                           .then_inc(sem("sums_lo"), 1)
                split_lo(dve, u + 1 + SLOTS)

            def differences(i):
                g, t = divmod(i, TT)
                dve.wait_ge(sem("ssm_scores"), i + 1)
                for hh in range(HPG):
                    h = HPG * g + hh
                    dve.scalar_tensor_tensor(decay[:, i % 2, hh, :], psum[:, 2 + i % 2, hh * P:(hh + 1) * P],
                                             per_token["a_sum"][:, t, h:h + 1], c1("causal_t"),
                                             ALU.subtract, ALU.add).then_inc(sem("ssm_diff"), 1)

            def weigh(i):
                dve.wait_ge(sem("decay"), i + 1)
                if i >= 2:
                    dve.wait_ge(sem("ssm_out"), i - 1)
                dve.tensor_tensor(within[:, i % 2, :, :], decay[:, i % 2, :, :],
                                  psum[:, 4 + i % 2, 0:P].unsqueeze(1).broadcast_to([P, HPG, P]), ALU.mult)\
                   .then_inc(sem("within"), 1)

            y_order = in_order(dve, "vector_order")

            def lo_of_y(q):
                for k in range(4 * q, 4 * q + 4):
                    dve.wait_ge(sem("yT_hi"), (k | 1) + 1)
                    dve.scalar_tensor_tensor(yT_lo[:, k, :], y_bank(k), col("ssm_norm", k),
                                             yT_hi[:, k, :].bitcast(F32), ALU.mult, ALU.subtract)\
                       .then_inc(sem("yT"), 1)

            def finish(i):
                g, t = divmod(i, TT)
                dve.wait_ge(sem("ssm_out"), i + 1)
                dve.wait_ge(sem("x_skip"), i + 1)
                dve.wait_ge(sem("states"), g + 1)
                to = y[:, t, g * GW:(g + 1) * GW].rearrange("p (h d) -> p h d", d=SP)
                bank = psum[:, 6 + i % 2, :]
                inside = bank[:, 0:GW].rearrange("p (h d) -> p h d", d=SP)
                skip = x_skip[:, i % 2, :, :]
                if t == 0:
                    dve.tensor_tensor(to, inside, skip, ALU.add).then_inc(sem("y"), 1)
                else:
                    y_order(dve.tensor_tensor(to, bank[:, GW:2 * GW].rearrange("p (h d) -> p h d", d=SP),
                                              by_channel(per_head["start_decay"][:, HPG * g:HPG * (g + 1)]), ALU.mult))
                    y_order(dve.tensor_tensor(to, inside, to, ALU.add))
                    dve.tensor_tensor(to, to, skip, ALU.add).then_inc(sem("y"), 1)

            for j in range(ITEMS // 2 + 1):
                if j < ITEMS // 2:
                    differences(2 * j)
                    differences(2 * j + 1)
                    if j < ITEMS // 2 - 1:
                        split_lo(dve, FIRST_UNIT["ssm_z"] + j + SLOTS)
                if j:
                    finish(2 * j - 2)
                    finish(2 * j - 1)
                if j < ITEMS // 2:
                    weigh(2 * j)
                    weigh(2 * j + 1)
                    if j == ITEMS // 2 - 1:
                        split_lo(dve, FIRST_UNIT["ssm_z"] + j + SLOTS)
                else:
                    lo_of_y(0)
                if j and j % 2 == 0:
                    q = j // 2 - 1
                    cs = slice(512 * q, 512 * (q + 1))
                    dve.wait_ge(sem("y"), 4 * (q + 1))
                    dve.wait_ge(sem("z_silu"), q + 1)
                    dve.tensor_tensor(y[:, :, cs], y[:, :, cs], z[:, :, cs], ALU.mult).then_inc(sem("y_gated"), 1)
            for q in range(1, 4):
                lo_of_y(q)
            add_to_x(dve, "ssm_out", 4, ((0, 1), (5, 7)))

        TURNED = [0, 512, 1024, 1536]
        HG_I, HG_Z, RQ, RV, RZ, GA, GB = 2048, 3072, 4096, 5120, 6144, 7168, 8192
        CHUNKS2 = TURNED + [HG_I, HG_I + 512, RQ, RQ + 512, RV, RV + 512, HG_Z, HG_Z + 512, GA, GA + 512,
                            RZ, RZ + 512, GB, GB + 512]
        NT = len(TURNED)
        TICKS = 2 * (len(CHUNKS2) - NT)
        STEPS = 2 * (LEVELS + 1)
        K_ROWS, STATES_12, STATE_3, OUT_A, RET_TURN, RET_SCORES, RET_STATE, OUT_B = range(STEPS + 3, STEPS + 11)

        def second_sp(sp):
            u = FIRST_UNIT["in2"]
            for c, n0 in enumerate(CHUNKS2):
                for j in range(2):
                    n = u + 2 * c + j
                    load_unit(sp, n, [(raw_unit(n % SLOTS)[:, k:k + 2, :], src)
                                      for k, src in halves_of("w_in_2", 4 * j, n0)])
            load_by_rows(sp, "out2", "w_out_2")
            for t in range(TT):
                sp.wait_ge(sem(f"final_{t}"), 2)
                sp.dma_start(out[0, t * P:(t + 1) * P, :], xn[:, t, :]).then_inc(sem("stored"), 16)
            sp.wait_ge(sem("stored"), 16 * TT)

        def second_pe(pe):
            norm_pe(pe, 6, False, TT)
            u = FIRST_UNIT["in2"]
            for c in range(NT):
                if c >= 2:
                    pe.wait_ge(sem("in2_out"), c - 1)
                turned_chunk(pe, u + 2 * c, pair_banks(c), ("hT", KD * 6) if c == 0 else None)
            for i in range(TICKS):
                c, j = NT + i // 2, i % 2
                if j == 0:
                    pe.wait_ge(sem("in2_out"), c - 1)
                hi, lo = use_unit(pe, u + 2 * NT + i)
                for kk in range(4):
                    k = 4 * j + kk
                    for t in range(TT):
                        to = psum[:, pair_banks(c)[t], :]
                        a, b = hT_hi[:, k, t * P:(t + 1) * P], hT_lo[:, k, t * P:(t + 1) * P]
                        pe.matmul(to, a, hi[:, kk, :], start=k == 0, stop=False)
                        pe.matmul(to, a, lo[:, kk, :], start=False, stop=False)
                        m = pe.matmul(to, b, hi[:, kk, :], start=False, stop=k == KD - 1)
                m.then_inc(sem("unit_used"), 1)
                second_pe_tick(pe, i)
            for half in range(2):
                pe.wait_ge(sem("m"), half + 1)
                for k in range(4 * half, 4 * half + 4):
                    for t in range(TT):
                        a = (k % 2) * SEQ + t * P
                        m = pe.transpose(psum[:, 4 + k // 2, a:a + P], out_a[:, t, k * P:(k + 1) * P], ident)
                    m.then_inc(sem("m_turned"), 1)
                for n in range(2):
                    pe.wait_ge(sem("in2_out"), len(CHUNKS2) - 1 + n)
                    linear_unit(pe, FIRST_UNIT["out2"] + 2 * half + n, 4 * half, KD, mT_hi, mT_lo, pair_banks(n),
                                ("mT", 0))

        def second_pe_tick(pe, i):
            s = i - 1
            if 0 <= s < STEPS:
                level, half = divmod(s, 2)
                if level:
                    pe.wait_ge(sem("hg_pair"), 2 * (s - 1))
                else:
                    pe.wait_ge(sem("hg_k"), half + 1)
                if s >= 2:
                    pe.wait_ge(sem("hg_att"), s - 1)
                for hh in range(4):
                    h = 4 * half + hh
                    for t in range(TT):
                        ts = slice(t * P, (t + 1) * P)
                        a, b = (hg_pair, hg_pair) if level else (hg_k, hg_q)
                        at_ = (hh % 2) * SEQ + t * P
                        m = pe.matmul(psum[:, 4 + 2 * half + hh // 2, at_:at_ + P], a[:, h, ts], b[:, h, ts],
                                      start=True, stop=True)
                m.then_inc(sem("hg_products"), 1)
            if i == K_ROWS:
                pe.wait_ge(sem("hg_ke"), 1)
                pe.wait_ge(sem("hg_att"), STEPS)
                for n in range(HEADS * TT):
                    h, t = divmod(n, TT)
                    m = pe.transpose(psum[:, 4 + n // 4, n % 4 * P:(n % 4 + 1) * P], hg_k[:, h, t * P:(t + 1) * P], ident)
                    if n % 8 == 7:
                        m.then_inc(sem("hg_k_turned"), 1)
            if i in (STATES_12, STATE_3):
                for c in ((0, 1) if i == STATES_12 else (2,)):
                    t, rows = c // 2, slice(c % 2 * HG_C, (c % 2 + 1) * HG_C)
                    pe.wait_ge(sem("hg_k_rows"), 2)
                    if c == 2:
                        pe.wait_ge(sem("hg_s1"), 1)
                    for h in range(HEADS):
                        m = pe.matmul(psum[:, 4 + 2 * (c % 2) + h // 4, h % 4 * P:(h % 4 + 1) * P],
                                      hg_k_rows[rows, h * TT + t, :], hg_v[rows, t, h * P:(h + 1) * P],
                                      start=True, stop=True)
                    m.then_inc(sem("hg_updates"), 1)
            if i == OUT_A:
                pe.wait_ge(sem("hg_qe"), 1)
                pe.wait_ge(sem("hg_s"), 2 * HEADS)
                for t in range(TT):
                    for h in range(HEADS):
                        bank = psum[:, 4 + 2 * t + h // 4, h % 4 * P:(h % 4 + 1) * P]
                        pe.matmul(bank, hg_att[:, h * TT + t, :], hg_v[:, t, h * P:(h + 1) * P], start=True, stop=False,
                                  skip_group_check=True)
                        for c in ((1,) if t == 0 else (2, 3)):
                            rows = slice(c % 2 * HG_C, (c % 2 + 1) * HG_C)
                            m = pe.matmul(bank[rows, :], hg_q[:, h, c * HG_C:(c + 1) * HG_C], hg_s[c - 1][:, h, :],
                                          start=False, stop=True, skip_group_check=True)
                    m.then_inc(sem("out_a_ready"), 1)
            if i == RET_TURN:
                pe.wait_ge(sem("out_a"), TT)
                pe.wait_ge(sem("ret_rotated"), 4)
                for j in range(RH // 2):
                    for a in range(2):
                        for t in range(TT):
                            at_ = a * SEQ + t * P
                            m = pe.transpose(psum[:, 4 + j, at_:at_ + P], ret_qk[:, t, a, j * P:(j + 1) * P], ident)
                    m.then_inc(sem("ret_turned"), 1)
            if i == RET_SCORES:
                pe.wait_ge(sem("ret_T"), 4)
                for n in range(RH * TT):
                    j, odd, t = n // 4, n // 2 % 2, n % 2
                    rows, ts = slice(odd * RDK, (odd + 1) * RDK), slice(t * P, (t + 1) * P)
                    at_ = j % 2 * SEQ + t * P
                    m = pe.matmul(psum[:, 4 + 2 * odd + j // 2, at_:at_ + P], ret_T[rows, j, 1, ts],
                                  ret_T[rows, j, 0, ts], start=True, stop=True)
                m.then_inc(sem("ret_scores"), 1)
            if i == RET_STATE:
                pe.wait_ge(sem("ret_att"), 4)
                pe.wait_ge(sem("ret_k_end"), 1)
                for h in range(RH):
                    rows = slice(h % 2 * RDK, (h % 2 + 1) * RDK)
                    m = pe.matmul(psum[rows, 4, h // 2 * P:(h // 2 + 1) * P], ret_k_end[:, h, :],
                                  ret_v[:, 0, h * P:(h + 1) * P], start=True, stop=True)
                m.then_inc(sem("ret_state_ready"), 1)
            if i == OUT_B:
                pe.wait_ge(sem("ret_state"), 1)
                pe.wait_ge(sem("ret_q_cross"), 1)
                for t in range(TT):
                    for h in range(RH):
                        rows = slice(h % 2 * RDK, (h % 2 + 1) * RDK)
                        bank = psum[:, 4 + 2 * t + h % 2, h // 2 * P:(h // 2 + 1) * P]
                        m = pe.matmul(bank, ret_att[:, h * TT + t, :], ret_v[:, t, h * P:(h + 1) * P],
                                      start=True, stop=t == 0)
                        if t:
                            m = pe.matmul(bank, ret_q_cross[rows, h // 2, :], ret_state[rows, h // 2, :],
                                          start=False, stop=True)
                    m.then_inc(sem("out_b_ready"), 1)

        def second_loads(act):
            act.dma_start(const2[:, :], w["second_constants"]).then_inc(sem("const2_in"), 16)
            act.dma_start(gain_row[:, :], w["hg_norm_g_2"][0].partition_broadcast(P)).then_inc(sem("gain_a_in"), 16)

        def blocks_of(ap, size):
            return ap.rearrange("p h (n b) -> p (h n) b", b=size)

        def second_act(act):
            norm_act(act, 6, None, False, FIRST_UNIT["in2"] - 1 + SLOTS)
            for k in range(KD):
                act.wait_ge(sem("h_tmp"), k + 1)
                act.activation(hT_hi[:, k, :], h_tmp[:, k, :], ACT.Copy).then_inc(sem("hT_hi"), 1)
            act.wait_ge(sem("lb_diff"), 2)
            act.activation(lb_e[:, :, :], lb_e[:, :, :], ACT.Exp).then_inc(sem("lb_e"), 1)
            u = FIRST_UNIT["in2"]

            def leave(c):
                act.wait_ge(sem("unit_used"), u + 2 * c + 2)
                n0, b = CHUNKS2[c], pair_banks(c)[0]
                src = psum[:, b:b + 2, :]
                cs = slice(n0 % D, n0 % D + 512)
                if c < NT:
                    hs = slice(4 * (c % 2), 4 * (c % 2) + 4)
                    to = hg_q if c < 2 else hg_k
                    act.activation(to[:, hs, :], src.rearrange("p b (h n) -> p (b h) n", h=2),
                                   ACT.Silu if c < 2 else ACT.Sigmoid).then_inc(sem("in2_out"), 1)
                elif n0 < HG_Z:
                    act.activation(hg_v[:, :, cs], src, ACT.Copy).then_inc(sem("in2_out"), 1)
                elif n0 < RQ:
                    act.activation(gate_a[:, :, cs], src, ACT.Silu).then_inc(sem("in2_out"), 1)
                elif n0 < RV:
                    act.activation(ret_qk[:, :, (n0 - RQ) // 512, :], src, ACT.Copy).then_inc(sem("in2_out"), 1)
                elif n0 < RZ:
                    act.activation(ret_v[:, :, cs], src, ACT.Copy).then_inc(sem("in2_out"), 1)
                elif n0 < GA:
                    act.wait_ge(sem("out_a_ready"), TT)
                    act.activation(gate_b[:, :, cs], src, ACT.Silu).then_inc(sem("in2_out"), 1)
                else:
                    n = 2 * (n0 >= GB) + (n0 % D) // 512
                    if n:
                        act.wait_ge(sem("gated"), n)
                    act.activation(sig[:, :, :], src, ACT.Sigmoid).then_inc(sem("in2_out"), 1)

            for c in range(NT):
                split_hi(act, u + 2 * c + SLOTS)
                leave(c)
                split_hi(act, u + 2 * c + 1 + SLOTS)
            for half in range(2):
                act.wait_ge(sem("hg_f"), 4 * half + 4)
                act.wait_ge(sem("hg_k"), half + 1)
                hs = slice(4 * half, 4 * half + 4)
                act.activation(hg_b[:, hs, :], hg_b[:, hs, :], ACT.Ln).then_inc(sem("hg_log"), 1)
            def hi_of_m(half):
                for k in range(4 * half, 4 * half + 4):
                    act.wait_ge(sem("m_turned"), (k | 1) + 1)
                    act.activation(mT_hi[:, k, :], psum[:, 4 + k // 2, (k % 2) * SEQ:(k % 2 + 1) * SEQ], ACT.Copy)\
                       .then_inc(sem("mT_hi"), 1)

            for i in range(TICKS):
                second_act_tick(act, i)
                if i == TICKS - 1:
                    leave(NT + i // 2)
                    hi_of_m(0)
                split_hi(act, u + 2 * NT + i + SLOTS)
                if i % 2 and i < TICKS - 1:
                    leave(NT + i // 2)
            hi_of_m(1)
            split_hi(act, FIRST_UNIT["out2"] + SLOTS)
            squares(act, 7)
            act.wait_ge(sem("gained_x"), TT)
            for t in range(TT):
                act.wait_ge(sem("rstd"), 8 + t)
                act.activation(xn[:, t, 0:512], scaled[:, t, 0:512], ACT.Copy, scale=rstd[:, t:t + 1])\
                   .then_inc(sem(f"final_{t}"), 1)

        def second_act_tick(act, i):
            s = i - 1
            if 2 <= s < STEPS:
                hs = slice(4 * (s % 2), 4 * (s % 2) + 4)
                act.wait_ge(sem("hg_diff"), 2 * (s - 1))
                act.activation(hg_exp[:, hs, :], hg_exp[:, hs, :], ACT.Exp).then_inc(sem("hg_exp"), 1)
            if i == STEPS + 1:
                act.wait_ge(sem("hg_pair"), 2 * (STEPS - 2))
                act.activation(hg_exp[:, :, :], hg_b[:, :, :], ACT.Exp).then_inc(sem("hg_exp_b"), 1)
                act.activation(hg_last[:, :, :], blocks_of(hg_b[:, :, :], HG_C)[:, :, HG_C - 1].rearrange(
                    "p (h c) -> p h c", h=HEADS), ACT.Exp).then_inc(sem("hg_last"), 1)
            if i == STEPS + 2:
                act.wait_ge(sem("hg_end_diff"), 1)
                act.activation(hg_exp[:, :, :], hg_exp[:, :, :], ACT.Exp).then_inc(sem("hg_exp_end"), 1)
            if i == K_ROWS + 1:
                for b in range(2):
                    act.wait_ge(sem("hg_k_turned"), b + 1)
                    act.activation(hg_k_rows[:, 8 * b:8 * b + 8, :],
                                   psum[:, 4 + 2 * b:6 + 2 * b, :].rearrange("p b (n c) -> p (b n) c", c=P), ACT.Copy)\
                       .then_inc(sem("hg_k_rows"), 1)
            if i == STATES_12 + 1:
                act.wait_ge(sem("hg_updates"), 1)
                act.activation(hg_s[0][:, :, :], psum[:, 4:6, :].rearrange("p b (h e) -> p (b h) e", e=P), ACT.Copy)\
                   .then_inc(sem("hg_s1"), 1)
            if i == OUT_A + 1:
                for t in range(TT):
                    act.wait_ge(sem("out_a_ready"), t + 1)
                    act.activation(out_a[:, t, :].rearrange("p (b n) -> p b n", b=2), psum[:, 4 + 2 * t:6 + 2 * t, :],
                                   ACT.Copy).then_inc(sem("out_a"), 1)
                for t in range(TT):
                    act.wait_ge(sem("out_a"), TT)
                    act.activation(square_a[:, t, :], out_a[:, t, :], ACT.Square).then_inc(sem("square_a"), 1)
            if i == RET_TURN + 1:
                for j in range(4):
                    act.wait_ge(sem("ret_turned"), j + 1)
                    act.activation(ret_T[:, j, :, :], psum[:, 4 + j, :].rearrange("p (a n) -> p a n", a=2), ACT.Copy)\
                       .then_inc(sem("ret_T"), 1)
            if i == RET_STATE + 1:
                act.wait_ge(sem("ret_state_ready"), 1)
                act.activation(ret_state[:, :, :], psum[:, 4, :].rearrange("p (j e) -> p j e", e=P), ACT.Copy)\
                   .then_inc(sem("ret_state"), 1)
            if i == OUT_B + 1:
                act.wait_ge(sem("head_ss"), TT)
                for t in range(TT):
                    act.wait_ge(sem("out_b_ready"), t + 1)
                    act.activation(out_b[:, t, :].rearrange("p (j a e) -> p a j e", a=2, e=P),
                                   psum[:, 4 + 2 * t:6 + 2 * t, :].rearrange("p a (j e) -> p a j e", e=P), ACT.Copy).then_inc(sem("out_b"), 1)
                for t in range(TT):
                    act.wait_ge(sem("out_b"), TT)
                    act.activation(square_b[:, t, :], out_b[:, t, :], ACT.Square).then_inc(sem("square_b"), 1)

        def second_pool(pool):
            norm_pool(pool, 6)
            pool.memset(hg_att[:, :, :], 0.0).then_inc(sem("att_clear"), 1)
            for s in range(2, STEPS):
                level, half = divmod(s, 2)
                size, hs = 2 ** level, slice(4 * half, 4 * half + 4)
                mid = size // 2
                b, e = blocks_of(hg_b[:, hs, :], size), blocks_of(hg_exp[:, hs, :], size)
                ref = b[:, :, mid - 1:mid].broadcast_to([P, 4 * SEQ // size, mid])
                pool.wait_ge(sem("hg_b"), 4 * half + 4)
                if s >= 4:
                    pool.wait_ge(sem("hg_pair"), 2 * (s - 3))
                pool.tensor_tensor(e[:, :, 0:mid], ref, b[:, :, 0:mid], ALU.subtract).then_inc(sem("hg_diff"), 1)
                pool.tensor_tensor(e[:, :, mid:size], b[:, :, mid:size], ref, ALU.subtract).then_inc(sem("hg_diff"), 1)
            pool.wait_ge(sem("hg_qe"), 1)
            b, e = blocks_of(hg_b[:, :, :], HG_C), blocks_of(hg_exp[:, :, :], HG_C)
            pool.tensor_tensor(e, b[:, :, HG_C - 1:HG_C].broadcast_to([P, HEADS * SEQ // HG_C, HG_C]), b, ALU.subtract)\
                .then_inc(sem("hg_end_diff"), 1)
            pool.wait_ge(sem("hg_att"), STEPS)
            pool.wait_ge(sem("in2_out"), NT + 4)
            order = in_order(pool, "gpsimd_order")
            for a in range(2):
                for t in range(TT):
                    v = ret_qk[:, t, a, :].rearrange("p (h d) -> p h d", d=RDK)
                    one, two = v[:, :, 0:RHALF], v[:, :, RHALF:RDK]
                    cos, sin = (c2(n)[:, t * RHALF:(t + 1) * RHALF].unsqueeze(1).broadcast_to([P, RH, RHALF])
                                for n in ("cos", "sin"))
                    order(pool.tensor_tensor(rot[:, 0, :, :], one, cos, ALU.mult),
                          pool.tensor_tensor(rot[:, 1, :, :], two, sin, ALU.mult),
                          pool.tensor_tensor(rot[:, 2, :, :], one, sin, ALU.mult))
                    order(pool.tensor_tensor(one, rot[:, 0, :, :], rot[:, 1, :, :], ALU.subtract))
                    order(pool.tensor_tensor(rot[:, 0, :, :], two, cos, ALU.mult))
                    pool.tensor_tensor(two, rot[:, 0, :, :], rot[:, 2, :, :], ALU.add).then_inc(sem("ret_rotated"), 1)
                    pool.wait_ge(sem("ret_rotated"), 2 * a + t + 1)
            pool.wait_ge(sem("gain_a_in"), 16)
            for h in range(2):
                cs = slice(512 * h, 512 * (h + 1))
                pool.wait_ge(sem("gated"), h + 1)
                pool.tensor_tensor(gate_a[:, :, cs], gate_a[:, :, cs], across_tokens(gain_row[:, cs]), ALU.mult)\
                    .then_inc(sem("gained"), 1)
            pool.wait_ge(sem("out_a_ready"), TT)
            pool.tensor_tensor(ret_k_end[:, :, :], ret_qk[:, 0, 1, :].rearrange("p (h d) -> p h d", d=RDK),
                               c2("zeta").unsqueeze(2).broadcast_to([P, RH, RDK]), ALU.mult)\
                .then_inc(sem("ret_k_end"), 1)
            pool.wait_ge(sem("ret_T"), 4)
            pool.tensor_tensor(ret_q_cross[:, :, :], ret_T[:, :, 0, P:SEQ], c2("xi").rearrange("p (j t) -> p j t", t=P),
                               ALU.mult).then_inc(sem("ret_q_cross"), 1)
            head_rstd_pool(pool, 0)
            pool.wait_ge(sem("gained"), 2)
            pool.dma_start(gain_row[:, :], w["ret_norm_g_2"][0].partition_broadcast(P)).then_inc(sem("gain_b_in"), 16)
            pool.wait_ge(sem("gain_b_in"), 16)
            pool.wait_ge(sem("in2_out"), NT + 12)
            for h in range(2):
                cs = slice(512 * h, 512 * (h + 1))
                pool.tensor_tensor(gate_b[:, :, cs], gate_b[:, :, cs], across_tokens(gain_row[:, cs]), ALU.mult)\
                    .then_inc(sem("gained"), 1)
            head_rstd_pool(pool, 1)
            pool.wait_ge(sem("gained"), 4)
            pool.dma_start(gain_row[:, :], w["final_g_2"][0].partition_broadcast(P)).then_inc(sem("final_gain_in"), 16)
            order = in_order(pool, "gpsimd_order")
            for t in range(TT):
                ts = slice(t, t + 1)
                pool.wait_ge(sem("sumsq"), 4 * 7 + 2 + t + 1)
                order(pool.tensor_tensor(meansq[:, ts], sumsq[:, 0, ts], sumsq[:, 1, ts], ALU.add))
                order(pool.tensor_scalar(meansq[:, ts], meansq[:, ts], 1.0 / D, EPS, ALU.mult, ALU.add))
                pool.tensor_tensor(rstd[:, ts], meansq[:, ts], neg_half[:, ts], ALU.pow).then_inc(sem("rstd"), 1)

        def across_tokens(row):
            return row.unsqueeze(1).broadcast_to([P, TT, row.shape[1]])

        def head_rstd_pool(pool, a):
            pool.wait_ge(sem("head_ss"), TT * (a + 1))
            order = in_order(pool, "gpsimd_order")
            order(pool.tensor_scalar(head_ms[:, a, :], head_ss[:, a, :], 1.0 / HD, EPS, ALU.mult, ALU.add))
            pool.tensor_tensor(head_rstd[:, a, :], head_ms[:, a, :], neg_half[:, 0:TT * HEADS], ALU.pow)\
                .then_inc(sem("head_rstd"), 1)

        def second_dve(dve):
            l0, l1 = col("hg_lb_logits_2", 0, HEADS), col("hg_lb_logits_2", HEADS, HEADS)
            order = in_order(dve, "vector_order")
            order(dve.tensor_tensor(lb_top[:, :], l0, l1, ALU.max))
            for n, l in enumerate((l0, l1)):
                dve.tensor_tensor(lb_e[:, n, :], l, lb_top[:, :], ALU.subtract).then_inc(sem("lb_diff"), 1)
            early, late = second_and_third("in2")
            split_lo(dve, early)
            norm_dve(dve, 6, None, False)
            for k in range(KD):
                dve.wait_ge(sem("xT"), 6 * KD + (k | 1) + 1)
                if k == 0:
                    dve.wait_ge(sem("gain2"), 1)
                dve.tensor_scalar(h_tmp[:, k, :], turned_x(6, k),
                                  gain2[:, k:k + 1], mod_cols[:, k:k + 1], ALU.mult, ALU.add).then_inc(sem("h_tmp"), 1)
                if k:
                    second_dve_lo(dve, k - 1)
            second_dve_lo(dve, KD - 1)
            split_lo(dve, late)
            dve.wait_ge(sem("lb_e"), 1)
            order(dve.tensor_tensor(lb_top[:, :], lb_e[:, 0, :], lb_e[:, 1, :], ALU.add))
            order(dve.reciprocal(lb_rest[:, :], lb_top[:, :]))
            order(dve.tensor_tensor(lb[:, :], lb_e[:, 0, :], lb_rest[:, :], ALU.mult))
            order(dve.tensor_scalar(lb_rest[:, :], lb[:, :], -1.0, 1.0, ALU.mult, ALU.add))
            u = FIRST_UNIT["in2"]
            for c in range(NT):
                split_lo(dve, u + 2 * c + SLOTS)
                split_lo(dve, u + 2 * c + 1 + SLOTS)
                if c >= 2:
                    half = c - 2
                    dve.wait_ge(sem("in2_out"), c + 1)
                    for h in range(4 * half, 4 * half + 4):
                        dve.tensor_scalar(hg_b[:, h, :], hg_k[:, h, :], lb_rest[:, h:h + 1], lb[:, h:h + 1],
                                          ALU.mult, ALU.add).then_inc(sem("hg_f"), 1)
                    dve.wait_ge(sem("hg_f"), 4 * half + 4)
                    hs = slice(4 * half, 4 * half + 4)
                    dve.tensor_scalar(hg_k[:, hs, :], hg_b[:, hs, :], -1.0, 1.0, ALU.mult, ALU.add)\
                       .then_inc(sem("hg_k"), 1)
            dve.wait_ge(sem("const2_in"), 16)
            dve.wait_ge(sem("att_clear"), 1)
            for half in range(2):
                dve.wait_ge(sem("hg_log"), half + 1)
                for h in range(4 * half, 4 * half + 4):
                    dve.tensor_tensor_scan(hg_b[:, h, :], c2("keep"), hg_b[:, h, :], 0.0, ALU.mult, ALU.add)\
                       .then_inc(sem("hg_b"), 1)
            for i in range(TICKS):
                if i < TICKS - 2:
                    second_dve_tick(dve, i)
                if i == TICKS - 1:
                    lo_of_m(dve, 0)
                split_lo(dve, u + 2 * NT + i + SLOTS)
                c = NT + i // 2
                if i % 2 and GA <= CHUNKS2[c] < GB:
                    gate(dve, c)
                if i == TICKS - 3:
                    mix(dve, c, 0)
            mix(dve, len(CHUNKS2) - 1, 1)
            lo_of_m(dve, 1)
            split_lo(dve, FIRST_UNIT["out2"] + SLOTS)
            for h in range(2):
                cs = slice(512 * h, 512 * (h + 1))
                dve.wait_ge(sem("unit_used"), FIRST_UNIT["out2"] + h + 3)
                for t in range(TT):
                    order(dve.tensor_tensor(scaled[:, t, cs], psum[:, 2 * h + t, :], gate2[:, cs], ALU.mult))
                    dve.tensor_tensor(x[:, t, cs], scaled[:, t, cs], x[:, t, cs], ALU.add).then_inc(sem("x_added"), 1)
                if h == 0:
                    dve.wait_ge(sem("final_gain_in"), 16)
                    dve.wait_ge(sem("x_added"), 4 * 6 + 2)
                    for t in range(TT):
                        dve.tensor_tensor(scaled[:, t, cs], x[:, t, cs], gain_row[:, cs], ALU.mult)\
                           .then_inc(sem("gained_x"), 1)
            for t in range(TT):
                dve.wait_ge(sem("rstd"), 8 + t)
                dve.scalar_tensor_tensor(xn[:, t, cs], x[:, t, cs], rstd[:, t:t + 1], gain_row[:, cs],
                                         ALU.mult, ALU.mult).then_inc(sem(f"final_{t}"), 1)

        def second_dve_lo(dve, k):
            dve.wait_ge(sem("hT_hi"), 6 * KD + k + 1)
            dve.tensor_tensor(hT_lo[:, k, :], h_tmp[:, k, :], hT_hi[:, k, :].bitcast(F32), ALU.subtract)\
               .then_inc(sem("hT"), 1)

        def gate(dve, c):
            n = 2 * (CHUNKS2[c] >= GB) + CHUNKS2[c] % D // 512
            to = (gate_b if n >= 2 else gate_a)[:, :, 512 * (n % 2):512 * (n % 2 + 1)]
            dve.wait_ge(sem("in2_out"), c + 1)
            if n >= 2:
                dve.wait_ge(sem("gained"), n + 1)
            dve.tensor_tensor(to, to, sig[:, :, :], ALU.mult).then_inc(sem("gated"), 1)

        def lo_of_m(dve, half):
            for k in range(4 * half, 4 * half + 4):
                dve.wait_ge(sem("mT_hi"), (k | 1) + 1)
                dve.tensor_tensor(mT_lo[:, k, :], psum[:, 4 + k // 2, (k % 2) * SEQ:(k % 2 + 1) * SEQ],
                                  mT_hi[:, k, :].bitcast(F32), ALU.subtract).then_inc(sem("mT"), 1)

        def mix(dve, c, half):
            cs = slice(512 * half, 512 * (half + 1))
            normed(dve, 1, out_b, None, (half,))
            gate(dve, c)
            order = in_order(dve, "vector_order")
            dve.wait_ge(sem("gated"), 3 + half)
            b = out_b[:, :, cs]
            order(dve.tensor_tensor(b, b, gate_b[:, :, cs], ALU.mult))
            dve.tensor_tensor(out_a[:, :, cs], out_a[:, :, cs], b, ALU.add).then_inc(sem("m"), 1)

        def normed(dve, a, buf, other, halves=(0, 1)):
            order = in_order(dve, "vector_order")
            dve.wait_ge(sem("head_rstd"), a + 1)
            for h in halves:
                cs = slice(512 * h, 512 * (h + 1))
                v = buf[:, :, cs].rearrange("p t (h d) -> p t h d", d=HD)
                r_ = head_rstd[:, a, :].rearrange("p (t h) -> p t h", t=TT)[:, :, 4 * h:4 * h + 4]
                order(dve.tensor_tensor(v, v, r_.unsqueeze(3).broadcast_to([P, TT, 4, HD]), ALU.mult))
            if other is not None:
                dve.wait_ge(sem("gained"), 2)
                order(dve.tensor_tensor(buf[:, :, :], buf[:, :, :], other[:, :, :], ALU.mult))

        def head_squares(dve, a, squares):
            for t in range(TT):
                dve.wait_ge(sem("square_" + "ab"[a]), t + 1)
                dve.tensor_reduce(head_ss[:, a, t * HEADS:(t + 1) * HEADS],
                                  squares[:, t, :].rearrange("p (h d) -> p h d", d=HD), X_AXIS, ALU.add)\
                   .then_inc(sem("head_ss"), 1)

        def second_dve_tick(dve, i):
            s = i - 1
            if 2 <= s < STEPS:
                level, half = divmod(s, 2)
                size, hs = 2 ** level, slice(4 * half, 4 * half + 4)
                mid = size // 2
                e, k, q, to = (blocks_of(v[:, hs, :], size) for v in (hg_exp, hg_k, hg_q, hg_pair))
                dve.wait_ge(sem("hg_exp"), s - 1)
                if s >= 4:
                    dve.wait_ge(sem("hg_products"), s - 1)
                dve.tensor_tensor(to[:, :, 0:mid], k[:, :, 0:mid], e[:, :, 0:mid], ALU.mult).then_inc(sem("hg_pair"), 1)
                dve.tensor_tensor(to[:, :, mid:size], q[:, :, mid:size], e[:, :, mid:size], ALU.mult)\
                   .then_inc(sem("hg_pair"), 1)
            s = i - 2
            if 0 <= s < STEPS:
                level, half = divmod(s, 2)
                mask = c2("levels")[:, level * P:(level + 1) * P].bitcast(U32).unsqueeze(1).broadcast_to([P, 8, P])
                dve.wait_ge(sem("hg_products"), s + 1)
                if level:
                    dve.wait_ge(sem("hg_att"), s - 1)
                dve.copy_predicated(hg_att[:, 8 * half:8 * half + 8, :], mask,
                                    psum[:, 4 + 2 * half:6 + 2 * half, :].rearrange("p b (n t) -> p (b n) t", t=P))\
                   .then_inc(sem("hg_att"), 1)
            if i == STEPS + 1:
                dve.wait_ge(sem("hg_exp_b"), 1)
                dve.tensor_tensor(hg_q[:, :, :], hg_q[:, :, :], hg_exp[:, :, :], ALU.mult).then_inc(sem("hg_qe"), 1)
            if i == STEPS + 2:
                dve.wait_ge(sem("hg_exp_end"), 1)
                dve.tensor_tensor(hg_k[:, :, :], hg_k[:, :, :], hg_exp[:, :, :], ALU.mult).then_inc(sem("hg_ke"), 1)
            for c, tick in ((1, STATES_12 + 1), (2, STATE_3 + 1)):
                if i == tick:
                    dve.wait_ge(sem("hg_updates"), c + 1)
                    dve.wait_ge(sem("hg_s1"), 1)
                    dve.wait_ge(sem("hg_last"), 1)
                    if c == 2:
                        dve.wait_ge(sem("hg_s"), HEADS)
                    for h in range(HEADS):
                        dve.scalar_tensor_tensor(hg_s[c][:, h, :], hg_s[c - 1][:, h, :], hg_last[:, h, c:c + 1],
                                                 psum[:, 4 + 2 * (c % 2) + h // 4, h % 4 * P:(h % 4 + 1) * P],
                                                 ALU.mult, ALU.add).then_inc(sem("hg_s"), 1)
            if i == OUT_A + 1:
                head_squares(dve, 0, square_a)
            if i == RET_SCORES + 1:
                dve.wait_ge(sem("ret_scores"), 1)
                by_parity = ret_att[:, :, :].rearrange("p (j a t) l -> p a j t l", a=2, t=TT)
                decays = c2("decay").rearrange("p (j a t) -> p a j t", a=2, t=P)
                for b in range(4):
                    js = slice(2 * (b % 2), 2 * (b % 2) + 2)
                    dve.tensor_tensor(by_parity[:, b // 2, js, :, :],
                                      psum[:, 4 + b, :].rearrange("p (j t l) -> p j t l", j=2, t=TT),
                                      decays[:, b // 2, js, :].unsqueeze(2).broadcast_to([P, 2, TT, P]), ALU.mult)\
                       .then_inc(sem("ret_att"), 1)
            if i == RET_STATE + 1:
                normed(dve, 0, out_a, gate_a)
            if i == OUT_B + 1:
                head_squares(dve, 1, square_b)

        block = ctx.enter_context(nc.Block())
        FFN1 = ("ffn1_w_gate", "ffn1_w_up", "ffn1_w_down")
        FFN2 = ("ffn2_w_gate", "ffn2_w_up", "ffn2_w_down")

        @block.sync
        def _(sp):
            start_sp(sp)
            ffn_sp(sp, "ffn1_0", FFN1, 0)
            attn_sp(sp)
            ffn_sp(sp, "ffn2_0", FFN2, 0)
            ffn_sp(sp, "ffn1_1", FFN1, 1)
            ssm_sp(sp)
            ffn_sp(sp, "ffn2_1", FFN2, 1)
            second_sp(sp)

        @block.gpsimd
        def _(pool):
            start_pool(pool)
            norm_pool(pool, 0)
            ada_pool(pool)
            attn_pool(pool)
            norm_pool(pool, 2)
            norm_pool(pool, 3)
            ssm_pool(pool)
            norm_pool(pool, 5)
            second_pool(pool)

        @block.scalar
        def _(act):
            start_act(act)
            ffn_act(act, "ffn1_0", 0, trig_act)
            attn_act(act)
            norm_act(act, 2, ("ffn2_norm", 0), True, FIRST_UNIT["ffn2_0"] - 1 + SLOTS)
            ffn_act(act, "ffn2_0", 2)
            norm_act(act, 3, ("ffn1_norm", KD), True, FIRST_UNIT["ffn1_1"] - 1 + SLOTS)
            ffn_act(act, "ffn1_1", 3)
            ssm_act(act)
            norm_act(act, 5, ("ffn2_norm", KD), True, FIRST_UNIT["ffn2_1"] - 1 + SLOTS)
            second_loads(act)
            ffn_act(act, "ffn2_1", 5)
            second_act(act)

        @block.vector
        def _(dve):
            start_dve(dve)
            ffn_dve(dve, "ffn1_0", angles_dve, rope_tables_dve, ada_dve)
            attn_dve(dve)
            norm_dve(dve, 2, ("ffn2_norm", 0), True, second_and_third("ffn2_0")[1:])
            ffn_dve(dve, "ffn2_0")
            norm_dve(dve, 3, ("ffn1_norm", KD), True, second_and_third("ffn1_1"))
            ffn_dve(dve, "ffn1_1")
            ssm_dve(dve)
            norm_dve(dve, 5, ("ffn2_norm", KD), True, second_and_third("ffn2_1")[1:])
            ffn_dve(dve, "ffn2_1")
            second_dve(dve)

        @block.tensor
        def _(pe):
            start_pe(pe)
            ffn_pe(pe, "ffn1_0", 0, ada_pe)
            attn_pe(pe)
            norm_pe(pe, 2, True)
            ffn_pe(pe, "ffn2_0", 2)
            norm_pe(pe, 3, True)
            ffn_pe(pe, "ffn1_1", 3)
            ssm_pe(pe)
            norm_pe(pe, 5, True)
            ffn_pe(pe, "ffn2_1", 5)
            second_pe(pe)


INPUTS = ["x", "positions", "ffn1_norm", "ffn1_w_gate", "ffn1_w_up", "ffn1_w_down", "mix_norm", "ffn2_norm",
          "ffn2_w_gate", "ffn2_w_up", "ffn2_w_down", "attn_w_qkv", "attn_q_norm", "attn_k_norm", "attn_w_o",
          "ssm_w_in", "ssm_conv_w", "ssm_conv_b", "ssm_dt_bias", "ssm_a_log", "ssm_d", "ssm_norm", "ssm_w_out", "c_2",
          "norm_g_2", "w_ada_2", "b_ada_2", "w_in_2", "hg_lb_logits_2", "hg_norm_g_2", "ret_norm_g_2", "w_out_2",
          "final_g_2"]


def kernel(**inputs):
    from concourse import bacc
    from concourse.bass_utils import run_bass_kernel_spmd

    nc = bacc.Bacc("TRN2", target_bir_lowering=False, num_devices=1)
    arrays = {name: np.ascontiguousarray(inputs[name]) for name in INPUTS}
    arrays["final_g_2"] = arrays["final_g_2"].reshape(1, D)
    arrays["first_constants"] = first_constants()
    arrays["second_constants"] = second_constants()
    w = {n: nc.dram_tensor(f"in_{n}", a.shape, mybir.dt.from_np(a.dtype), kind="ExternalInput").ap()
         for n, a in arrays.items()}
    out = nc.dram_tensor("out", (1, SEQ, D), F32, kind="ExternalOutput").ap()
    build(nc, w, out)
    result = run_bass_kernel_spmd(nc, [{f"in_{n}": a for n, a in arrays.items()}], core_ids=[0])
    return result.results[0]["out"]
```
